# Optimizing a Trainium2 kernel written in Bass

```python
import math
import jax, jax.numpy as jnp
from jax import lax
import numpy as np

D_MODEL = 1024
BATCH = 1
SEQ = 256
DEPTH = 1
DEC_BATCH = 1
DEC_SEQ = 512
PAST_LEN = 128

GLA_HEADS = 4
GLA_DK = 64
GLA_DV = 128
GLA_GATE_RANK = 16
GLA_TAU = 16.0
GLA_CHUNK = 64
DIFF_HEADS = 4
DIFF_DH = 64
DIFF_DV = 2 * DIFF_DH
Q_BLOCK = 128
ROPE_THETA = 10000.0
N_EXPERTS = 16
EC_FACTOR = 2
D_EXPERT = 2 * D_MODEL
RMS_EPS = 1e-6

GLA_QK = GLA_HEADS * GLA_DK
GLA_V = GLA_HEADS * GLA_DV
DIFF_QK = DIFF_HEADS * 2 * DIFF_DH
DIFF_V = DIFF_HEADS * DIFF_DV
MIX_WIDTH = GLA_V + DIFF_V
IN_SIZES = (GLA_QK, GLA_QK, GLA_V, GLA_V, GLA_GATE_RANK, GLA_GATE_RANK, DIFF_QK, DIFF_QK, DIFF_V)
IN_WIDTH = sum(IN_SIZES)

kernel_name = "hymba_gla_diffattn_ec_moe_encoder"

def rms_norm(x, gain):
    xf = x.astype(jnp.float32)
    y = xf * lax.rsqrt(jnp.mean(xf * xf, axis=-1, keepdims=True) + RMS_EPS)
    return y * gain.astype(jnp.float32)

def lambda_init(layer):
    return 0.8 - 0.6 * math.exp(-0.3 * layer)

def apply_rope(x):
    T, dh = x.shape[1], x.shape[-1]
    inv_freq = jnp.power(ROPE_THETA, -jnp.arange(0, dh, 2, dtype=jnp.float32) / dh)
    ang = jnp.arange(T, dtype=jnp.float32)[:, None] * inv_freq[None, :]
    cos = jnp.cos(ang)[None, :, None, None, :]
    sin = jnp.sin(ang)[None, :, None, None, :]
    x1, x2 = x[..., : dh // 2], x[..., dh // 2:]
    return jnp.concatenate([x1 * cos - x2 * sin, x2 * cos + x1 * sin], axis=-1)

def gla_chunked(q, k, v, log_a, strict):
    B, T, H, DK = q.shape
    DV = v.shape[-1]
    C = GLA_CHUNK
    N = T // C

    def blk(t):
        return t.reshape(B, N, C, H, t.shape[-1]).transpose(0, 3, 1, 2, 4).astype(jnp.float32)

    q, k, v, log_a = blk(q), blk(k), blk(v), blk(log_a)
    b = jnp.cumsum(log_a, axis=3)
    b_mid = b[:, :, :, C // 2 - 1: C // 2, :]
    b_last = b[:, :, :, C - 1: C, :]
    scores = jnp.einsum('bhncd,bhnsd->bhncs', q * jnp.exp(b - b_mid), k * jnp.exp(b_mid - b))
    idx = jnp.arange(C)
    mask = (idx[:, None] > idx[None, :]) if strict else (idx[:, None] >= idx[None, :])
    scores = jnp.where(mask, scores, 0.0)
    o_intra = jnp.einsum('bhncs,bhnse->bhnce', scores, v)
    u = jnp.einsum('bhncd,bhnce->nbhde', k * jnp.exp(b_last - b), v)
    decay = jnp.exp(b_last[:, :, :, 0, :]).transpose(2, 0, 1, 3)

    def step(s, inp):
        d, du = inp
        return d[..., None] * s + du, s

    s0 = jnp.zeros((B, H, DK, DV), jnp.float32)
    _, s_prev = lax.scan(step, s0, (decay, u))
    o_inter = jnp.einsum('bhncd,nbhde->bhnce', q * jnp.exp(b), s_prev)
    o = o_intra + o_inter
    return o.transpose(0, 2, 3, 1, 4).reshape(B, T, H, DV)

def gla_mixer(q, k, v, og, lr_f, lr_b, wg_f, bg_f, wg_b, bg_b, norm_g):
    B, T, _ = q.shape
    q = q.reshape(B, T, GLA_HEADS, GLA_DK).astype(jnp.float32) * (GLA_DK ** -0.5)
    k = k.reshape(B, T, GLA_HEADS, GLA_DK)
    v = v.reshape(B, T, GLA_HEADS, GLA_DV)
    z_f = (lr_f @ wg_f).astype(jnp.float32) + bg_f.astype(jnp.float32)
    z_b = (lr_b @ wg_b).astype(jnp.float32) + bg_b.astype(jnp.float32)
    la_f = (jax.nn.log_sigmoid(z_f) / GLA_TAU).reshape(B, T, GLA_HEADS, GLA_DK)
    la_b = (jax.nn.log_sigmoid(z_b) / GLA_TAU).reshape(B, T, GLA_HEADS, GLA_DK)
    o_f = gla_chunked(q, k, v, la_f, False)
    fl = lambda t: jnp.flip(t, axis=1)
    o_b = fl(gla_chunked(fl(q), fl(k), fl(v), fl(la_b), True))
    o = rms_norm(o_f + o_b, norm_g).reshape(B, T, GLA_V)
    return o * jax.nn.silu(og.astype(jnp.float32))

def diff_attention(q, k, v, qn_g, kn_g, lq1, lk1, lq2, lk2, norm_g, lam_init):
    B, T, _ = q.shape
    q = q.reshape(B, T, DIFF_HEADS, 2, DIFF_DH)
    k = k.reshape(B, T, DIFF_HEADS, 2, DIFF_DH)
    v = v.reshape(B, T, DIFF_HEADS, DIFF_DV).astype(jnp.float32)
    q = apply_rope(rms_norm(q, qn_g)) * (DIFF_DH ** -0.5)
    k = apply_rope(rms_norm(k, kn_g))
    f32 = jnp.float32
    lam = (jnp.exp(jnp.sum(lq1.astype(f32) * lk1.astype(f32)))
           - jnp.exp(jnp.sum(lq2.astype(f32) * lk2.astype(f32))) + lam_init)
    nb = T // Q_BLOCK
    qb = q.reshape(B, nb, Q_BLOCK, DIFF_HEADS, 2, DIFF_DH).transpose(1, 0, 2, 3, 4, 5)

    def block(qblk):
        s = jnp.einsum('bqhmd,bkhmd->bhmqk', qblk, k)
        p = jax.nn.softmax(s, axis=-1)
        w = p[:, :, 0] - lam * p[:, :, 1]
        return jnp.einsum('bhqk,bkhe->bqhe', w, v)

    o = lax.map(block, qb)
    o = o.transpose(1, 0, 2, 3, 4).reshape(B, T, DIFF_HEADS, DIFF_DV)
    o = rms_norm(o, norm_g) * (1.0 - lam_init)
    return o.reshape(B, T, DIFF_V)

def expert_choice_ffn(h, w_router, w_gate, w_up, w_down):
    B, T, D = h.shape
    n = B * T
    cap = max(1, EC_FACTOR * n // N_EXPERTS)
    xt = h.reshape(n, D)
    aff = jax.nn.softmax((xt @ w_router).astype(jnp.float32), axis=-1)
    gates, idx = lax.top_k(aff.T, cap)
    xe = xt[idx]
    a = jnp.einsum('ecd,edf->ecf', xe, w_gate)
    u = jnp.einsum('ecd,edf->ecf', xe, w_up)
    ye = jnp.einsum('ecf,efd->ecd', jax.nn.silu(a) * u, w_down).astype(jnp.float32)
    ye = ye * gates[..., None]
    out = jnp.zeros((n, D), jnp.float32).at[idx.reshape(-1)].add(ye.reshape(-1, D))
    return out.reshape(B, T, D)

def encoder_layer(x, layer, norm1_g, w_in, gla_wg_f, gla_bg_f, gla_wg_b, gla_bg_b, gla_norm_g,
                  qk_norm_q, qk_norm_k, lambda_q1, lambda_k1, lambda_q2, lambda_k2, diff_norm_g,
                  w_out, norm2_g, w_router, w_gate, w_up, w_down):
    dt = x.dtype
    h = rms_norm(x, norm1_g).astype(dt)
    proj = h @ w_in
    offs = [int(o) for o in np.cumsum(IN_SIZES)[:-1]]
    gq, gk, gv, gog, glr_f, glr_b, dq, dk, dv = jnp.split(proj, offs, axis=-1)
    a = gla_mixer(gq, gk, gv, gog, glr_f, glr_b, gla_wg_f, gla_bg_f, gla_wg_b, gla_bg_b, gla_norm_g)
    d = diff_attention(dq, dk, dv, qk_norm_q, qk_norm_k, lambda_q1, lambda_k1, lambda_q2,
                       lambda_k2, diff_norm_g, lambda_init(layer))
    mix = jnp.concatenate([a, d], axis=-1).astype(dt)
    x = x + (mix @ w_out).astype(dt)
    h2 = rms_norm(x, norm2_g).astype(dt)
    x = x + expert_choice_ffn(h2, w_router, w_gate, w_up, w_down).astype(dt)
    return x

def setup_inputs(seed: int = 0) -> dict:
    key = jax.random.key(seed)
    ks = jax.random.split(key, 24)
    f32 = jnp.float32
    nrm = lambda k, shape, scale: jax.random.normal(k, shape, f32) * scale
    gain = lambda k, n: 1.0 + 0.01 * jax.random.normal(k, (DEPTH, n), f32)
    return {
        "x_prompt": jax.random.normal(ks[0], (BATCH, SEQ, D_MODEL), f32),
        "x_sample": jax.random.normal(ks[1], (DEC_BATCH, DEC_SEQ, D_MODEL), f32),
        "norm1_g": gain(ks[2], D_MODEL),
        "w_in": nrm(ks[3], (DEPTH, D_MODEL, IN_WIDTH), D_MODEL ** -0.5),
        "gla_wg_f": nrm(ks[4], (DEPTH, GLA_GATE_RANK, GLA_QK), GLA_GATE_RANK ** -0.5),
        "gla_bg_f": nrm(ks[5], (DEPTH, GLA_QK), 0.1),
        "gla_wg_b": nrm(ks[6], (DEPTH, GLA_GATE_RANK, GLA_QK), GLA_GATE_RANK ** -0.5),
        "gla_bg_b": nrm(ks[7], (DEPTH, GLA_QK), 0.1),
        "gla_norm_g": gain(ks[8], GLA_DV),
        "qk_norm_q": gain(ks[9], DIFF_DH),
        "qk_norm_k": gain(ks[10], DIFF_DH),
        "lambda_q1": nrm(ks[11], (DEPTH, DIFF_DH), 0.1),
        "lambda_k1": nrm(ks[12], (DEPTH, DIFF_DH), 0.1),
        "lambda_q2": nrm(ks[13], (DEPTH, DIFF_DH), 0.1),
        "lambda_k2": nrm(ks[14], (DEPTH, DIFF_DH), 0.1),
        "diff_norm_g": gain(ks[15], DIFF_DV),
        "w_out": nrm(ks[16], (DEPTH, MIX_WIDTH, D_MODEL), MIX_WIDTH ** -0.5),
        "norm2_g": gain(ks[17], D_MODEL),
        "w_router": nrm(ks[18], (DEPTH, D_MODEL, N_EXPERTS), D_MODEL ** -0.5),
        "w_gate": nrm(ks[19], (DEPTH, N_EXPERTS, D_MODEL, D_EXPERT), D_MODEL ** -0.5),
        "w_up": nrm(ks[20], (DEPTH, N_EXPERTS, D_MODEL, D_EXPERT), D_MODEL ** -0.5),
        "w_down": nrm(ks[21], (DEPTH, N_EXPERTS, D_EXPERT, D_MODEL), D_EXPERT ** -0.5),
    }

def reference(x_prompt, x_sample, norm1_g, w_in, gla_wg_f, gla_bg_f, gla_wg_b, gla_bg_b,
              gla_norm_g, qk_norm_q, qk_norm_k, lambda_q1, lambda_k1, lambda_q2, lambda_k2,
              diff_norm_g, w_out, norm2_g, w_router, w_gate, w_up, w_down):
    y_prompt = x_prompt
    y_sample = x_sample
    for l in range(DEPTH):
        lw = (norm1_g[l], w_in[l], gla_wg_f[l], gla_bg_f[l], gla_wg_b[l], gla_bg_b[l],
              gla_norm_g[l], qk_norm_q[l], qk_norm_k[l], lambda_q1[l], lambda_k1[l],
              lambda_q2[l], lambda_k2[l], diff_norm_g[l], w_out[l], norm2_g[l],
              w_router[l], w_gate[l], w_up[l], w_down[l])
        y_prompt = encoder_layer(y_prompt, l, *lw)
        y_sample = encoder_layer(y_sample, l, *lw)
    return (y_prompt, y_sample)


_drawn_inputs = setup_inputs


def setup_inputs(seed=0):
    import zlib

    import numpy as np

    out = dict(_drawn_inputs(seed))
    spreads = {}
    factors = {'norm1_g': 3.751,
     'gla_bg_f': 3.957,
     'gla_bg_b': 3.818,
     'gla_norm_g': 28.106,
     'qk_norm_q': 5.307,
     'qk_norm_k': 6.133,
     'lambda_k2': 2.758,
     'diff_norm_g': 97.638,
     'norm2_g': 17.052}
    for name, (base, spread) in spreads.items():
        noise = np.random.default_rng([zlib.crc32(name.encode()), seed]).standard_normal(out[name].shape)
        drawn = base * np.exp(spread * noise) if base else spread * noise
        out[name] = __import__('jax').numpy.asarray(drawn.astype(out[name].dtype))
    for name, factor in factors.items():
        out[name] = (out[name] * factor).astype(out[name].dtype)
    return out
```

```python
from contextlib import ExitStack

import numpy as np

import concourse.bass as bass
from concourse import mybir
from concourse.alu_op_type import AluOpType as ALU

ACT = mybir.ActivationFunctionType
F32 = mybir.dt.float32
F32R = mybir.dt.float32r
U32 = mybir.dt.uint32
AX_X = mybir.AxisListType.X

P = 128
D = 1024
KD = D // P
T_PROMPT, T_SAMPLE = 256, 512
TOK = T_PROMPT + T_SAMPLE
NT = TOK // P
GROUPS = ((0, 2), (2, 4))
HEADS = 4
DK, DV = 64, 128
RANK = 16
CHUNK = 64
NCH = TOK // CHUNK
SL = 512
C_QK, C_V, C_OG, C_LR = 0, 512, 1024, 1536
C_DQ, C_DK, C_DV = 1568, 2080, 2592
SLICES = (C_QK, C_DQ, C_DK, C_V, C_DV, C_OG)
EPS = 1e-6
TAU = 16.0
LAM_INIT = 0.2
NE = 16
FE = 2 * D
CAP_P, CAP_S = 2 * T_PROMPT // NE, 2 * T_SAMPLE // NE
CAP = CAP_P + CAP_S
NPAIR = NE // 2
FS = 512
NS = FE // FS
FC = FS // P
RAW = 8
CONV = 4
AHEAD = 3
TW = 2048


def tile_plan():
    plan = []
    for c in range(4):
        plan += [("qk", c, 0), ("qk", c, 1)]
    plan += [("lr", 0, 0), ("lr", 0, 1)]
    body = [("dqk", s, t) for s in range(2) for t in range(NT)]
    body += [("tok", s, t) for s in range(3, 6) for t in range(NT)]
    lag = 3
    for n, u in enumerate(body):
        plan.append(u)
        if n >= lag and n - lag < 2 * NT:
            v = n - lag
            plan.append(("rope", v // NT, v % NT))
    return plan


def evacuated_by(kind):
    return "dve" if kind == "dqk" else "act"


def weight_plan():
    order = []
    for q in range(2 * NS):
        order += [("g", q, 0), ("g", q, 1), ("u", q, 0), ("u", q, 1)]
        if q >= 1:
            order += [("d", q - 1, 0), ("d", q - 1, 1)]
    return order + [("d", 2 * NS - 1, 0), ("d", 2 * NS - 1, 1)]


class Chain:

    def __init__(self, eng, sem):
        self.eng, self.sem, self.n, self.base = eng, sem, 0, 0

    def mark(self, ins):
        self.n += 1
        return ins.then_inc(self.sem, 1)

    def own(self):
        self.eng.wait_ge(self.sem, self.base + self.n)

    def link(self, ins):
        self.mark(ins)
        self.own()


def build(nc, a, y_prompt, y_sample, h2_dram):
    ctx = ExitStack()
    with ctx:
        def sb(name, shape, dt=F32):
            return ctx.enter_context(nc.sbuf_tensor(name, shape, dt))

        def sem(name):
            return ctx.enter_context(nc.semaphore(name))

        ps = ctx.enter_context(nc.psum_tensor("ps", [P, 8, 512], F32))

        span = 210304
        sb("whole", [P, span // 4])
        origin = nc.sbuf_base - span

        def at(name, off, shape, dt=F32):
            return nc.alloc_sbuf_tensor_at(name, shape, dt, offset=origin + off)

        ring = at("ring", 0, [P, 8, 4096])
        wh = at("wh", 0, [P, CONV, TW], F32R)
        wl = at("wl", 32768, [P, CONV, TW], F32R)
        raw = at("raw", 65536, [P, RAW, TW])
        X = at("X", 131072, [P, NT, D])
        HT = at("HT", 155648, [P, KD, TOK])
        Yh = [at(f"Yh{j}", 155648 + 8192 * j, [P, D], F32R) for j in range(2)]
        Yl = [at(f"Yl{j}", 159744 + 8192 * j, [P, D], F32R) for j in range(2)]
        gTh = at("gTh", 172032, [P, FC, CAP], F32R)
        gTl = at("gTl", 173568, [P, FC, CAP], F32R)
        hid = at("hid", 175104, [P, FS])
        XTh = [at("XTh0", 177152, [P, KD, CAP], F32R), at("XTh1", 199680, [P, KD, CAP], F32R)]
        hn = at("hn", 180224, [P, 2, D])
        XE = at("XE", 180224, [P, D])
        sel = [at("sel0", 184320, [P, TOK], F32R), at("sel1", 196608, [P, TOK], F32R)]
        gnorm = at("gnorm", 188416, [P, D])
        XTl = [at("XTl0", 188416, [P, KD, CAP], F32R), at("XTl1", 205824, [P, KD, CAP], F32R)]
        tabs = at("tabs", 192512, [P, 4, 4, DK])
        wlr = at("wlr", 196608, [P, KD, 2 * RANK])
        wg = at("wg", 197632, [2 * RANK, HEADS, P])
        lrT = at("lrT", 199680, [2 * RANK, TOK])
        scanm = at("scanm", 202752, [P, TOK])
        pmask = at("pmask", 205824, [P, 2, P], U32)
        og_gain = at("og_gain", 206848, [P, 2, DV])
        wr = at("wr", 207872, [P, KD, NE])
        ident = at("ident", 208896, [P, P])
        st = at("st", 209408, [P, 192])
        bg = at("bg", 210176, [P, HEADS])
        nlam = at("nlam", 210208, [P, 4])
        idx_col = at("idx_col", 210240, [P, 2], U32)
        cur = at("cur", 210272, [P, 2])

        flat = ring[:].rearrange("p r n -> p (r n)")

        def part(off, n, base=flat):
            return base[:, off:off + n]

        W = [ring[:, s, :].rearrange("p (k n) -> p k n", k=KD) for s in range(2)]
        o = 2 * 4096
        Q = part(o, 3072).rearrange("p (h t) -> p h t", h=HEADS); o += 3072
        K = part(o, 3072).rearrange("p (h t) -> p h t", h=HEADS); o += 3072
        V = part(o, 3072).rearrange("p (t n) -> p t n", t=NT); o += 3072
        VD = part(o, 3072).rearrange("p (t n) -> p t n", t=NT); o += 3072
        OG = part(o, 3072).rearrange("p (t n) -> p t n", t=NT); o += 3072
        QT = part(o, 3072).rearrange("p (h t) -> p h t", h=HEADS); o += 3072
        KT = part(o, 3072).rearrange("p (h t) -> p h t", h=HEADS); o += 3072
        OA = part(o, 3072).rearrange("p (t n) -> p t n", t=NT); o += 3072
        assert o == 8 * 4096
        OD = K.rearrange("p h t -> p (h t)").rearrange("p (t n) -> p t n", t=NT)
        oaf = OA.rearrange("p t n -> p (t n)")
        hnf = hn[:].rearrange("p b n -> p (b n)")
        sq = [part(0, SL, oaf), part(SL, SL, oaf)]
        yr = [part(2 * SL, SL, oaf), part(3 * SL, SL, oaf)]
        t1 = [part(4 * SL, SL, oaf), part(5 * SL, SL, oaf)]
        t2 = [part(0, SL, hnf), part(SL, SL, hnf)]
        gains = OG[:, 0, 0:256].rearrange("p (m d) -> p m d", m=4)
        lamv = OG[:, 0, 256:512].rearrange("p (m d) -> p m d", m=4)
        o = 0
        gl = []
        for _ in range(7):
            gl.append(part(o, TOK)); o += TOK
        zT1, zT2, cum, qtil, ktil, qhat, khat = gl
        khT = part(o, TOK).rearrange("p (t c) -> p t c", t=NT); o += TOK
        states = part(o, NCH * DV).rearrange("p (n e) -> p n e", n=NCH); o += NCH * DV
        assert o <= 2 * 4096
        Ssb = part(0, TOK, hnf).rearrange("p (t c) -> p t c", t=NT)
        bmid = part(TOK, NCH, hnf)
        blast = part(TOK + NCH, NCH, hnf)
        decay = part(TOK + 2 * NCH, NCH, hnf)
        qf = Q.rearrange("p h t -> p (h t)")
        prob = [part(0, 1024, qf).rearrange("p (m n) -> p m n", m=2),
                part(1024, 1024, qf).rearrange("p (m n) -> p m n", m=2)]
        wmix = [part(2048, 512, qf), part(2560, 512, qf)]
        wT = [part(1024, 512, hnf).rearrange("p (t c) -> p t c", t=4),
              part(1536, 512, hnf).rearrange("p (t c) -> p t c", t=4)]
        tmpE = part(0, 3072, qf).rearrange("p (t n) -> p t n", t=NT)
        h2T = [part(30720, 1024).rearrange("p (k c) -> p k c", k=KD),
               part(31744, 1024).rearrange("p (k c) -> p k c", k=KD)]
        junk = hn[:, 1, :]
        junk1 = ring[:, 6, 0:1024]
        iota = scanm[:]
        tabf = tabs[:].rearrange("p a b c -> p (a b c)")
        aff = lrT[0:NE, :]
        topv = part(0, CAP, tabf)[0:NE]
        topf = part(CAP, CAP, tabf)[0:NE]
        topi = part(2 * CAP, CAP, tabf)[0:NE].bitcast(U32)
        gidx = part(3 * CAP, NE + 1, tabf).bitcast(U32)
        grow = part(3 * CAP + 24, NE, tabf)
        gate = part(3 * CAP + 48, NE, tabf)

        s_x = [sem(f"x_loaded{t}") for t in range(NT)]
        s_const = sem("constants_loaded")
        s_wlr, s_wg = sem("lowrank_weights_loaded"), sem("gate_weights_loaded")
        s_win = [sem(f"projection_slice_loaded{i}") for i in range(2)]
        s_wout = sem("w_out_loaded")
        s_late = sem("late_constants_loaded")
        s_dve, s_act, s_pool = sem("dve_step"), sem("act_step"), sem("pool_step")
        s_ss1, s_var1, s_rt1, s_hn1, s_tr1 = (sem(n) for n in
            ("squares1", "variance1", "root1", "normed1", "transposed1"))
        s_ht_a, s_ht_d = sem("ht_from_act"), sem("ht_from_dve")
        s_unit, s_free_a, s_free_d = sem("unit_in_psum"), sem("unit_copied_by_act"), sem("unit_copied_by_dve")
        s_sq, s_sumq, s_varq, s_rtq, s_swap, s_rope = (sem(n) for n in
            ("squares_qk", "sums_qk", "variance_qk", "root_qk", "swapped_half", "roped"))
        s_tab = sem("rotary_tables_ready")
        s_z, s_zb, s_absz, s_sp, s_cum, s_mid, s_dmid, s_dlast = (sem(n) for n in
            ("gate_logits", "gate_bias_added", "abs_logits", "softplus", "cumsum_done", "mid_last_copied",
             "minus_mid", "last_minus"))
        s_e1, s_e3, s_e4, s_dec = sem("exp_mid"), sem("exp_cum"), sem("exp_last"), sem("decay_ready")
        s_qt, s_qh, s_kh = sem("scores_factors"), sem("inter_queries"), sem("state_keys")
        s_kt, s_ktc, s_sc, s_pred, s_u, s_st, s_o, s_oc = (sem(n) for n in
            ("keys_turned", "keys_copied", "gla_scores", "gla_masked", "state_updates", "states_done",
             "gla_out", "gla_out_copied"))
        s_s, s_mx, s_p, s_w, s_wt, s_wtc, s_pv, s_pvc = (sem(n) for n in
            ("scores", "row_max", "exps", "weights_mixed", "weights_turned", "weights_copied", "attn_out",
             "attn_out_copied"))
        s_ego, s_vare, s_rte, s_mix = sem("exp_gate"), sem("variance_heads"), sem("root_heads"), sem("mixed")
        s_mt, s_mta, s_mtd, s_op, s_x1 = (sem(n) for n in
            ("mix_turned", "mixT_from_act", "mixT_from_dve", "out_projected", "residual_added"))
        s_ss2, s_var2, s_rt2, s_hn2, s_tr2, s_h2a, s_h2d = (sem(n) for n in
            ("squares2", "variance2", "root2", "normed2", "h2_turned", "h2T_from_act",
             "h2T_from_dve"))
        s_h2w = [sem(f"h2_stored{b}") for b in range(2)]
        s_lg, s_lmx, s_lex, s_aff, s_afT, s_afc = (sem(n) for n in
            ("router_logits", "router_max", "router_exp", "affinity", "affinity_turned", "affinity_copied"))
        s_top, s_topT, s_route = sem("top_ready"), sem("top_turned"), sem("routes_ready")
        s_lamd, s_lame = sem("lambda_dots"), sem("lambda_exps")
        s_land = [sem(f"weight_tile_landed{i}") for i in range(RAW)]
        s_wh, s_wl, s_used = sem("tile_high_part"), sem("tile_low_part"), sem("tile_used")
        s_icol, s_gat, s_xtp, s_xth, s_xtl = (sem(n) for n in
            ("index_column", "rows_gathered", "rows_turned", "xT_high", "xT_low"))
        s_silu, s_hid, s_hT, s_gth, s_gtl = (sem(n) for n in
            ("silu_of_gate", "hidden_ready", "hidden_turned", "hiddenT_high", "hiddenT_low"))
        s_yh, s_yl, s_sel, s_scat, s_acc = (sem(n) for n in
            ("y_high", "y_low", "selection_ready", "scattered", "accumulated"))
        s_out = sem("output_stored")

        UNITS = tile_plan()
        NCONST = 20

        def slice_end(n):
            mine = [u for u, (kind, s, t) in enumerate(UNITS)
                    if (0 if kind == "qk" else s + 1 if kind == "dqk" else s if kind == "tok" else -1) == n]
            return mine[-1] + 1

        def freed_count(u):
            who = evacuated_by(UNITS[u][0])
            n = sum(evacuated_by(k[0]) == who for k in UNITS[:u + 1])
            return (s_free_d if who == "dve" else s_free_a), n

        n_free_a = sum(evacuated_by(k[0]) == "act" for k in UNITS)
        n_free_d = len(UNITS) - n_free_a

        TILES = weight_plan()
        NTI = len(TILES)
        assert NTI % RAW == 0 and NTI % CONV == 0
        place = {t: n for n, t in enumerate(TILES)}

        def tile_used(i, kind, q):
            return s_used, NTI * i + (place[kind, q, 1] + 1)

        ATT = [(g, h, t) for g in range(2) for h in range(HEADS) for t in range(GROUPS[g][1])]

        block = ctx.enter_context(nc.Block())

        @block.sync
        def _(sp):
            for t in range(NT):
                src = a["x_prompt"][0] if t < 2 else a["x_sample"][0]
                r = t if t < 2 else t - 2
                sp.dma_start(X[:, t, :], src[r * P:(r + 1) * P, :]).then_inc(s_x[t], 16)

            def load_slice(n):
                if n >= 2:
                    sp.wait_ge(s_unit, slice_end(n - 2))
                sp.dma_start(W[n % 2], a["w_in"][0][:, SLICES[n]:SLICES[n] + SL]
                             .rearrange("(k p) n -> p k n", p=P)).then_inc(s_win[n % 2], 16)

            load_slice(0)
            sp.dma_start(wlr[:], a["w_in"][0][:, C_LR:C_LR + 2 * RANK]
                         .rearrange("(k p) n -> p k n", p=P)).then_inc(s_wlr, 16)
            for n in range(1, len(SLICES)):
                load_slice(n)
            sp.wait_ge(s_o, 2 * HEADS)
            for f in range(2):
                sp.dma_start(W[f], a["w_out"][0][:, f * SL:(f + 1) * SL]
                             .rearrange("(k p) n -> p k n", p=P)).then_inc(s_wout, 16)
            sp.wait_ge(s_hn1, NT)
            sp.dma_start(gnorm[:], a["norm2_g"][0:1, :].broadcast_to([P, D])).then_inc(s_late, 16)
            sp.wait_ge(s_cum, HEADS)
            sp.dma_start(iota, a["iota"]).then_inc(s_late, 16)

            def load_tile(i, n):
                kind, q, part_ = TILES[n]
                e, s = 2 * i + q // NS, q % NS
                rows, cols = (slice(s * FS + part_ * 256, s * FS + part_ * 256 + 256), slice(0, D)) \
                    if kind == "d" else (slice(part_ * 512, part_ * 512 + 512), slice(s * FS, (s + 1) * FS))
                w = a[{"g": "w_gate", "u": "w_up", "d": "w_down"}[kind]][0]
                src = w[e, rows, cols] if isinstance(e, int) else \
                    w[bass.ds(e, 1), rows, cols].rearrange("a r c -> (a r) c")
                sp.dma_start(raw[:, n % RAW, :].rearrange("p (k c) -> p k c", k=2 if kind == "d" else 4),
                             src.rearrange("(k p) c -> p k c", p=P)).then_inc(s_land[n % RAW], 16)

            sp.wait_ge(s_mt, 2 * NT)
            for n in range(RAW - 1):
                load_tile(0, n)
            for t in range(NT):
                sp.wait_ge(s_hn2, t + 1)
                sp.dma_start(h2_dram[t * P:(t + 1) * P, :], hn[:, t % 2, :]).then_inc(s_h2w[t % 2], 16)
            sp.wait_ge(s_lg, NT)
            load_tile(0, RAW - 1)
            with sp.Fori(0, NPAIR - 1) as i:
                for n in range(RAW, NTI + RAW):
                    sp.wait_ge(s_wl, i * NTI + (n - RAW + 1))
                    load_tile(i if n < NTI else i + 1, n % NTI)
            for n in range(RAW, NTI):
                sp.wait_ge(s_wl, (NPAIR - 1) * NTI + n - RAW + 1)
                load_tile(NPAIR - 1, n)
            for t in range(NT):
                sp.wait_ge(s_acc, NPAIR * 2 * NT - (2 * NT) + 2 * (t + 1))
                dst = y_prompt[0] if t < 2 else y_sample[0]
                r = t if t < 2 else t - 2
                sp.dma_start(dst[r * P:(r + 1) * P, :], X[:, t, :]).then_inc(s_out, 16)
            sp.wait_ge(s_out, 16 * NT)
            for b in range(2):
                sp.wait_ge(s_h2w[b], 16 * (NT // 2))

        @block.gpsimd
        def _(pool):
            ch = Chain(pool, s_pool)
            n = 0
            for dst, src in (
                (gnorm[:], a["norm1_g"][0:1, :].broadcast_to([P, D])),
                (ident[:], a["ident"]),
                (tabs[:].rearrange("p a b c -> p (a b c)"), a["rot"]),
                (scanm[:], a["scan_mask"]),
                (pmask[:].rearrange("p a b -> p (a b)"), a["pair_mask"]),
                (wr[:], a["w_router"][0].rearrange("(k p) e -> p k e", p=P)),
                (og_gain[:, 0, :], a["gla_norm_g"][0:1, :].broadcast_to([P, DV])),
                (og_gain[:, 1, :], a["diff_norm_g"][0:1, :].broadcast_to([P, DV])),
                (bg[0:DK, :], a["gla_bg_f"][0].rearrange("(h d) -> d h", d=DK)),
                (bg[DK:P, :], a["gla_bg_b"][0].rearrange("(h d) -> d h", d=DK)),
            ):
                with nc.allow_non_contiguous_dma(reason="256 gate biases, one a partition and head"):
                    pool.dma_start(dst, src).then_inc(s_const, 16)
                n += 1
            for m, name in enumerate(("lambda_q1", "lambda_k1", "lambda_q2", "lambda_k2")):
                pool.dma_start(lamv[:, m, :], a[name][0:1, :].broadcast_to([P, DK])).then_inc(s_const, 16)
                n += 1
            for m, name in ((0, "qk_norm_q"), (2, "qk_norm_k")):
                pool.dma_start(gains[:, m, :], a[name][0:1, :].broadcast_to([P, DK])).then_inc(s_const, 16)
                for lo, hi in ((0, 32), (32, 0)):
                    pool.dma_start(gains[:, m + 1, lo:lo + 32], a[name][0:1, hi:hi + 32].broadcast_to([P, 32]))\
                        .then_inc(s_const, 16)
                n += 3
            assert n == NCONST
            ch.link(pool.memset(wg[:], 0.0))
            pool.dma_start(wg[0:RANK, :, 0:DK], a["gla_wg_f"][0].rearrange("r (h d) -> r h d", h=HEADS))\
                .then_inc(s_wg, 16)
            pool.dma_start(wg[RANK:2 * RANK, :, DK:P], a["gla_wg_b"][0].rearrange("r (h d) -> r h d", h=HEADS))\
                .then_inc(s_wg, 16)

            pool.wait_ge(s_tab, 4)
            for v in range(2 * NT):
                s, t = v // NT, v % NT
                pos = t if t < 2 else t - 2
                y3 = yr[v % 2].rearrange("p (m c) -> p m c", m=8)
                o3 = t2[v % 2].rearrange("p (m c) -> p m c", m=8)
                B = tabs[:, 2 * s + 1, pos, :]
                pool.wait_ge(s_free_d, v + 1)
                if v >= 2:
                    pool.wait_ge(s_rope, v - 1)
                for lo, hi in ((0, 32), (32, 0)):
                    pool.tensor_tensor(o3[:, :, lo:lo + 32], y3[:, :, hi:hi + 32],
                                       B[:, lo:lo + 32].unsqueeze(1).broadcast_to([P, 8, 32]),
                                       ALU.mult).then_inc(s_swap, 1)

            for h in range(HEADS):
                pool.wait_ge(s_mid, h + 1)
                if h >= 1:
                    pool.wait_ge(s_e4, h)
                pool.tensor_tensor(zT2.rearrange("p (n c) -> p n c", n=NCH),
                                   blast.unsqueeze(2).broadcast_to([P, NCH, CHUNK]),
                                   cum.rearrange("p (n c) -> p n c", n=NCH), ALU.subtract).then_inc(s_dlast, 1)
                pool.wait_ge(s_e3, h + 1)
                pool.tensor_tensor(qhat, qhat, Q[:, h, :], ALU.mult).then_inc(s_qh, 1)
                pool.wait_ge(s_e4, h + 1)
                pool.tensor_tensor(khat, khat, K[:, h, :], ALU.mult).then_inc(s_kh, 1)

            def gather(n):
                pool.wait_ge(s_icol, n)
                pool.nop(nofuse=True)
                pool.indirect_dma_start(out=XE[0:CAP, :], out_offset=None, in_=h2_dram,
                                        in_offset=bass.IndirectOffsetOnAxis(ap=idx_col[0:CAP, 0:1], axis=0))\
                    .then_inc(s_gat, 16)
            for b in range(2):
                pool.wait_ge(s_h2w[b], 16 * (NT // 2))
            gather(1)
            with pool.Fori(0, NPAIR - 1) as i:
                for j in range(2):
                    gather(2 * i + (j + 2))
            gather(NE)

        @block.tensor
        def _(pe):
            def bank(b):
                return ps[:, b, :]

            pe.wait_ge(s_const, 16 * NCONST)
            for t in range(NT):
                pe.wait_ge(s_hn1, t + 1)
                if t >= 2:
                    pe.wait_ge(s_ht_a, t - 1)
                    pe.wait_ge(s_ht_d, t - 1)
                for k in range(KD):
                    mm = pe.transpose(ps[:, 2 * (t % 2) + k // 4, (k % 4) * P:(k % 4 + 1) * P],
                                      hn[:, t % 2, k * P:(k + 1) * P], ident[:])
                    if k % 4 == 3:
                        mm.then_inc(s_tr1, 1)
            pe.wait_ge(s_ht_a, NT)
            pe.wait_ge(s_ht_d, NT)

            for u, (kind, s, t) in enumerate(UNITS):
                b = u % 8
                if u >= 8:
                    pe.wait_ge(*freed_count(u - 8))
                if kind == "qk":
                    if s == 0 and t == 0:
                        pe.wait_ge(s_win[0], 16)
                    t0, n = (0, T_PROMPT) if t == 0 else (T_PROMPT, T_SAMPLE)
                    for k in range(KD):
                        mm = pe.matmul(ps[:, b, 0:n], W[0][:, k, s * P:(s + 1) * P], HT[:, k, t0:t0 + n],
                                       start=(k == 0), stop=(k == KD - 1))
                    mm.then_inc(s_unit, 1)
                elif kind == "lr":
                    if t == 0:
                        pe.wait_ge(s_wlr, 16)
                    t0, n = (0, T_PROMPT) if t == 0 else (T_PROMPT, T_SAMPLE)
                    for k in range(KD):
                        mm = pe.matmul(ps[0:2 * RANK, b, 0:n], wlr[:, k, :], HT[:, k, t0:t0 + n],
                                       start=(k == 0), stop=(k == KD - 1))
                    mm.then_inc(s_unit, 1)
                elif kind == "rope":
                    v = s * NT + t
                    pe.wait_ge(s_rope, v + 1)
                    for h in range(HEADS):
                        mm = pe.transpose(ps[:, b, h * P:(h + 1) * P], t1[v % 2][:, h * P:(h + 1) * P], ident[:])
                    mm.then_inc(s_unit, 1)
                else:
                    n = s + 1 if kind == "dqk" else s
                    if t == 0:
                        pe.wait_ge(s_win[n % 2], 16 * (n // 2 + 1))
                    for k in range(KD):
                        mm = pe.matmul(bank(b), HT[:, k, t * P:(t + 1) * P], W[n % 2][:, k, :],
                                       start=(k == 0), stop=(k == KD - 1))
                    mm.then_inc(s_unit, 1)

            pe.wait_ge(s_free_a, n_free_a)
            pe.wait_ge(s_free_d, n_free_d)
            pe.wait_ge(s_wg, 32)
            for h in range(HEADS):
                if h >= 1:
                    pe.wait_ge(s_zb, 2 * h)
                for g, (t0, n) in enumerate(GROUPS):
                    pe.matmul(ps[:, g, 0:n * P], wg[:, h, :], lrT[:, t0 * P:(t0 + n) * P],
                              start=True, stop=True).then_inc(s_z, 1)

                def scores(g):
                    t0, n = GROUPS[g]
                    if 2 * h + g >= 1:
                        pe.wait_ge(s_pred, 2 * h + g)
                    for d in range(2):
                        for t in range(n):
                            c = slice((t0 + t) * P, (t0 + t + 1) * P)
                            mm = pe.matmul(ps[:, 2 + d, t * P:(t + 1) * P], ktil[d * DK:(d + 1) * DK, c],
                                           qtil[d * DK:(d + 1) * DK, c], start=True, stop=True)
                    mm.then_inc(s_sc, 1)

                def updates(g):
                    t0, n = GROUPS[g]
                    pe.wait_ge(s_ktc, 2 * h + g + 1)
                    if 2 * h + g >= 1:
                        pe.wait_ge(s_st, 2 * h + g)
                    for odd in range(2):
                        r = slice(odd * CHUNK, (odd + 1) * CHUNK)
                        for t in range(n):
                            mm = pe.matmul(ps[:, 6 + odd, t * P:(t + 1) * P], khT[r, t0 + t, :],
                                           V[r, t0 + t, h * DV:(h + 1) * DV], start=True, stop=True)
                    mm.then_inc(s_u, 1)

                def outputs(g):
                    t0, n = GROUPS[g]
                    pe.wait_ge(s_pred, 2 * h + g + 1)
                    pe.wait_ge(s_st, 2 * h + g + 1)
                    pe.wait_ge(s_qh, h + 1)
                    for t in range(n):
                        o = ps[:, 4 + g, t * P:(t + 1) * P]
                        pe.matmul(o, Ssb[:, t0 + t, :], V[:, t0 + t, h * DV:(h + 1) * DV],
                                  start=(t == 0), stop=False, skip_group_check=True)
                        for odd in range(2):
                            c = 2 * (t0 + t) + odd
                            mm = pe.matmul(ps[odd * CHUNK:(odd + 1) * CHUNK, 4 + g, t * P:(t + 1) * P],
                                           qhat[:, c * CHUNK:(c + 1) * CHUNK], states[:, c, :],
                                           start=False, stop=True, skip_group_check=True)
                    mm.then_inc(s_o, 1)

                pe.wait_ge(s_qt, 2 * (h + 1))
                scores(0)
                pe.wait_ge(s_kh, h + 1)
                for g, (t0, n) in enumerate(GROUPS):
                    if h >= 1:
                        pe.wait_ge(s_oc, 2 * (h - 1) + g + 1)
                    for t in range(n):
                        mm = pe.transpose(ps[:, 4 + g, t * P:(t + 1) * P],
                                          khat[:, (t0 + t) * P:(t0 + t + 1) * P], ident[:])
                    mm.then_inc(s_kt, 1)
                updates(0)
                scores(1)
                updates(1)
                outputs(0)
                outputs(1)

            pe.wait_ge(s_oc, 2 * HEADS)
            for i in range(len(ATT) + 2):
                if i < len(ATT):
                    g, h, t = ATT[i]
                    t0, n = GROUPS[g]
                    if i >= 2:
                        pe.wait_ge(s_p, 2 * (i - 1))
                    for m in range(2):
                        r = slice(m * DK, (m + 1) * DK)
                        mm = pe.matmul(ps[:, 2 * (i % 2) + m, 0:n * P],
                                       QT[r, h, (t0 + t) * P:(t0 + t + 1) * P],
                                       KT[r, h, t0 * P:(t0 + n) * P], start=True, stop=True)
                    mm.then_inc(s_s, 1)
                if 1 <= i <= len(ATT):
                    v = i - 1
                    n = GROUPS[ATT[v][0]][1]
                    pe.wait_ge(s_w, v + 1)
                    if v >= 2:
                        pe.wait_ge(s_wtc, v - 1)
                    for k in range(n):
                        mm = pe.transpose(ps[:, 4 + v % 2, k * P:(k + 1) * P],
                                          wmix[v % 2][:, k * P:(k + 1) * P], ident[:])
                    mm.then_inc(s_wt, 1)
                if i >= 2:
                    v = i - 2
                    g, h, t = ATT[v]
                    t0, n = GROUPS[g]
                    pe.wait_ge(s_wtc, v + 1)
                    if v >= 2:
                        pe.wait_ge(s_pvc, v - 1)
                    for k in range(n):
                        mm = pe.matmul(ps[:, 6 + v % 2, 0:DV], wT[v % 2][:, k, :],
                                       VD[:, t0 + k, h * DV:(h + 1) * DV], start=(k == 0), stop=(k == n - 1))
                    mm.then_inc(s_pv, 1)

            def turn(src, t, done, a_copied, d_copied, base):
                if t >= 2:
                    pe.wait_ge(a_copied, t - 1)
                    pe.wait_ge(d_copied, t - 1)
                for k in range(KD):
                    mm = pe.transpose(ps[:, 2 * (t % 2) + k // 4, (k % 4) * P:(k % 4 + 1) * P], src(k), ident[:])
                    if k % 4 == 3:
                        mm.then_inc(done, 1)

            pe.wait_ge(s_mix, 2)
            for t in range(NT + 1):
                if t < NT:
                    turn(lambda k: (OA if k < 4 else OD)[:, t, (k % 4) * P:(k % 4 + 1) * P], t,
                         s_mt, s_mta, s_mtd, 0)
                if t >= 1:
                    v = t - 1
                    if v == 0:
                        pe.wait_ge(s_wout, 32)
                        pe.wait_ge(s_pvc, len(ATT))
                        pe.wait_ge(s_wtc, len(ATT))
                    pe.wait_ge(s_mta, v + 1)
                    pe.wait_ge(s_mtd, v + 1)
                    for f in range(2):
                        u = 2 * v + f
                        if u >= 4:
                            pe.wait_ge(s_x1, u - 3)
                        for k in range(KD):
                            mm = pe.matmul(ps[:, 4 + u % 4, :], HT[:, k, v * P:(v + 1) * P], W[f][:, k, :],
                                           start=(k == 0), stop=(k == KD - 1))
                        mm.then_inc(s_op, 1)

            pe.wait_ge(s_x1, 2 * NT)
            pe.wait_ge(s_mta, NT)
            pe.wait_ge(s_mtd, NT)
            for t in range(NT):
                pe.wait_ge(s_hn2, t + 1)
                turn(lambda k: hn[:, t % 2, k * P:(k + 1) * P], t, s_tr2, s_h2a, s_h2d, 0)
                pe.wait_ge(s_h2a, t + 1)
                pe.wait_ge(s_h2d, t + 1)
                if t >= 2:
                    pe.wait_ge(s_lex, t - 1)
                for k in range(KD):
                    mm = pe.matmul(ps[:, 4 + t % 2, 0:NE], h2T[t % 2][:, k, :], wr[:, k, :],
                                   start=(k == 0), stop=(k == KD - 1))
                mm.then_inc(s_lg, 1)
                pe.wait_ge(s_aff, t + 1)
                if t >= 2:
                    pe.wait_ge(s_afc, t - 1)
                pe.transpose(ps[0:NE, 6 + t % 2, 0:P], st[:, 96 + 16 * (t % 2):112 + 16 * (t % 2)],
                             ident[:]).then_inc(s_afT, 1)
            pe.wait_ge(s_top, 1)
            pe.wait_ge(s_afc, NT)
            pe.transpose(ps[0:CAP, 0, 0:NE], topf, ident[0:NE, 0:NE])
            pe.transpose(ps[0:CAP, 0, 32:32 + NE], topv, ident[0:NE, 0:NE]).then_inc(s_topT, 1)
            pe.wait_ge(s_route, 1)

            def turn_rows(e, half, after):
                if half == 0:
                    pe.wait_ge(s_gat, 16 * (e + 1))
                else:
                    pe.wait_ge(s_xtl, 2 * e + 1)
                for k in range(4 * half, 4 * half + 4):
                    mm = pe.transpose(ps[:, 7, (k % 4) * CAP:(k % 4 + 1) * CAP],
                                      XE[0:CAP, k * P:(k + 1) * P], ident[0:CAP, 0:CAP])
                mm.then_inc(s_xtp, 1)

            def products(out, parts, rhs_h, rhs_l, first, last):
                hi, lo = parts
                pe.matmul(out, hi, rhs_h, start=first, stop=False)
                pe.matmul(out, lo, rhs_h, start=False, stop=False)
                return pe.matmul(out, hi, rhs_l, start=False, stop=last)

            def use_tile(i, n):
                kind, q, part_ = TILES[n]
                c = n % CONV
                pe.wait_ge(s_wl, i * NTI + (n + 1))
                if kind in "gu":
                    h_, l_ = (w[:, c, :].rearrange("p (k f) -> p k f", k=4) for w in (wh, wl))
                    b = (0 if kind == "g" else 2) + q % 2
                    j = q // NS
                    for k in range(4):
                        kk = 4 * part_ + k
                        mm = products(ps[0:CAP, b, :], (XTh[j][:, kk, :], XTl[j][:, kk, :]),
                                      h_[:, k, :], l_[:, k, :], kk == 0, kk == KD - 1)
                else:
                    h_, l_ = (w[:, c, :].rearrange("p (f d) -> p f d", f=2) for w in (wh, wl))
                    s = q % NS
                    for f in range(2):
                        ff = 2 * part_ + f
                        for half in range(2):
                            d = slice(half * 512, (half + 1) * 512)
                            mm = products(ps[0:CAP, 4 + half, :], (gTh[:, ff, :], gTl[:, ff, :]),
                                          h_[:, f, d], l_[:, f, d], s == 0 and ff == 0,
                                          s == NS - 1 and ff == FC - 1)
                mm.then_inc(s_used, 1)

            def turn_hidden(i, q):
                pe.wait_ge(s_hid, 8 * i + (q + 1))
                if q >= 1:
                    pe.wait_ge(s_gtl, 8 * i + q)
                for f in range(FC):
                    mm = pe.transpose(ps[:, 6, f * CAP:(f + 1) * CAP], hid[0:CAP, f * P:(f + 1) * P],
                                      ident[0:CAP, 0:CAP])
                mm.then_inc(s_hT, 1)

            def pair(i, last):
                for q in range(2 * NS):
                    if q % NS == 0:
                        pe.wait_ge(s_xtl, 4 * i + 2 * (q // NS) + 2)
                    if q >= 2:
                        pe.wait_ge(s_hid, 8 * i + (q - 1))
                    use_tile(i, place["g", q, 0])
                    use_tile(i, place["g", q, 1])
                    if q >= 1:
                        turn_hidden(i, q - 1)
                    turns = q % NS == 1 and not (last and q > NS)
                    if turns:
                        turn_rows(2 * i + (q // NS + 1), 0, None)
                    use_tile(i, place["u", q, 0])
                    use_tile(i, place["u", q, 1])
                    if turns:
                        turn_rows(2 * i + (q // NS + 1), 1, None)
                    if q >= 1:
                        pe.wait_ge(s_gtl, 8 * i + q)
                        if q == NS + 1:
                            pe.wait_ge(s_yl, 4 * i + 2)
                        use_tile(i, place["d", q - 1, 0])
                        use_tile(i, place["d", q - 1, 1])
                turn_hidden(i, 2 * NS - 1)
                pe.wait_ge(s_gtl, 8 * i + 2 * NS)
                use_tile(i, place["d", 2 * NS - 1, 0])
                use_tile(i, place["d", 2 * NS - 1, 1])
                pe.wait_ge(s_sel, 2 * i + 2)
                pe.wait_ge(s_yl, 4 * i + 4)
                banks = (0, 1, 2, 3, 6, 7)
                for u in range(2 * NT):
                    t, half = u // 2, u % 2
                    if u >= len(banks):
                        pe.wait_ge(s_acc, 2 * NT * i + (u - len(banks) + 1))
                    for j in range(2):
                        for part_ in (Yh, Yl):
                            mm = pe.matmul(ps[:, banks[u % len(banks)], :], sel[j][0:CAP, t * P:(t + 1) * P],
                                           part_[j][0:CAP, half * 512:(half + 1) * 512],
                                           start=(j == 0 and part_ is Yh), stop=(j == 1 and part_ is Yl))
                    mm.then_inc(s_scat, 1)
                pe.wait_ge(s_acc, 2 * NT * i + 2 * NT)

            turn_rows(0, 0, None)
            turn_rows(0, 1, None)
            with pe.Fori(0, NPAIR - 1) as i:
                pair(i, False)
            pair(NPAIR - 1, True)

        @block.scalar
        def _(act):
            ch = Chain(act, s_act)
            act.wait_ge(s_lamd, 1)
            act.activation(nlam[:, 2:4], nlam[:, 0:2], ACT.Exp).then_inc(s_lame, 1)
            for t in range(NT + 1):
                if t < NT:
                    act.wait_ge(s_x[t], 16)
                    act.activation(junk1, X[:, t, :], ACT.Square, accum_out=st[:, t:t + 1]).then_inc(s_ss1, 1)
                    act.wait_ge(s_var1, t + 1)
                    act.activation(st[:, 16 + t:17 + t], st[:, 8 + t:9 + t], ACT.Sqrt).then_inc(s_rt1, 1)
                if t >= 1:
                    v = t - 1
                    act.wait_ge(s_tr1, 2 * v + 1)
                    act.copy(HT[:, 0:4, v * P:(v + 1) * P],
                             ps[:, 2 * (v % 2), :].rearrange("p (k c) -> p k c", k=4)).then_inc(s_ht_a, 1)

            for u, (kind, s, t) in enumerate(UNITS):
                b = u % 8
                act.wait_ge(s_unit, u + 1)
                if kind == "qk":
                    t0, n = (0, T_PROMPT) if t == 0 else (T_PROMPT, T_SAMPLE)
                    dst, sc = (Q, DK ** -0.5) if s < 2 else (K, 1.0)
                    for half in range(2):
                        h = 2 * (s % 2) + half
                        src = ps[half * DK:(half + 1) * DK, b, 0:n]
                        act.mul(dst[0:DK, h, t0:t0 + n], src, sc)
                        last = act.mul(dst[DK:P, h, t0:t0 + n], src, sc)
                    last.then_inc(s_free_a, 1)
                elif kind == "lr":
                    t0, n = (0, T_PROMPT) if t == 0 else (T_PROMPT, T_SAMPLE)
                    act.copy(lrT[:, t0:t0 + n], ps[0:2 * RANK, b, 0:n]).then_inc(s_free_a, 1)
                elif kind == "dqk":
                    v = s * NT + t
                    if v >= 2:
                        act.wait_ge(s_sumq, v - 1)
                    act.activation(sq[v % 2], ps[:, b, :], ACT.Square).then_inc(s_sq, 1)
                    act.wait_ge(s_varq, v + 1)
                    act.activation(st[:, 40 + 8 * (v % 2):48 + 8 * (v % 2)],
                                   st[:, 24 + 8 * (v % 2):32 + 8 * (v % 2)], ACT.Sqrt).then_inc(s_rtq, 1)
                elif kind == "rope":
                    dst = QT if s == 0 else KT
                    act.copy(dst[:, :, t * P:(t + 1) * P],
                             ps[:, b, :].rearrange("p (h c) -> p h c", h=HEADS)).then_inc(s_free_a, 1)
                else:
                    dst = {3: V, 4: VD, 5: OG}[s]
                    act.copy(dst[:, t, :], ps[:, b, :]).then_inc(s_free_a, 1)

            for h in range(HEADS):
                act.wait_ge(s_absz, h + 1)
                ch.link(act.activation(zT2, zT2, ACT.Exp, scale=-1.0))
                act.activation(zT2, zT2, ACT.Ln, bias=1.0).then_inc(s_sp, 1)
                act.wait_ge(s_dmid, h + 1)
                if h >= 1:
                    act.wait_ge(s_sc, 2 * h)
                act.activation(qtil, zT1, ACT.Exp, scale=1.0 / TAU)
                act.activation(ktil, zT1, ACT.Exp, scale=-1.0 / TAU).then_inc(s_e1, 1)
                if h >= 1:
                    act.wait_ge(s_o, 2 * h)
                act.activation(qhat, cum, ACT.Exp, scale=1.0 / TAU).then_inc(s_e3, 1)
                act.wait_ge(s_dlast, h + 1)
                if h >= 1:
                    act.wait_ge(s_kt, 2 * h)
                    act.wait_ge(s_st, 2 * h)
                act.activation(khat, zT2, ACT.Exp, scale=1.0 / TAU).then_inc(s_e4, 1)
                act.activation(decay, blast, ACT.Exp, scale=1.0 / TAU).then_inc(s_dec, 1)
                for g, (t0, n) in enumerate(GROUPS):
                    act.wait_ge(s_kt, 2 * h + g + 1)
                    if h >= 1:
                        act.wait_ge(s_u, 2 * (h - 1) + g + 1)
                    act.copy(khT[:, t0:t0 + n, :], ps[:, 4 + g, 0:n * P]
                             .rearrange("p (t c) -> p t c", t=n)).then_inc(s_ktc, 1)
                for g, (t0, n) in enumerate(GROUPS):
                    act.wait_ge(s_o, 2 * h + g + 1)
                    act.copy(OA[:, t0:t0 + n, h * DV:(h + 1) * DV], ps[:, 4 + g, 0:n * P]
                             .rearrange("p (t c) -> p t c", t=n)).then_inc(s_oc, 1)

            for i in range(len(ATT) + 2):
                if i < len(ATT):
                    g, h, t = ATT[i]
                    n = GROUPS[g][1] * P
                    act.wait_ge(s_mx, i + 1)
                    if i >= 2:
                        act.wait_ge(s_w, i - 1)
                    for m in range(2):
                        act.activation(prob[i % 2][:, m, 0:n], ps[:, 2 * (i % 2) + m, 0:n], ACT.Exp,
                                       bias=st[:, 56 + 2 * (i % 2) + m:57 + 2 * (i % 2) + m],
                                       accum_out=st[:, 60 + 2 * (i % 2) + m:61 + 2 * (i % 2) + m]).then_inc(s_p, 1)
                if 1 <= i <= len(ATT):
                    v = i - 1
                    n = GROUPS[ATT[v][0]][1]
                    act.wait_ge(s_wt, v + 1)
                    if v >= 2:
                        act.wait_ge(s_pv, v - 1)
                    act.copy(wT[v % 2][:, 0:n, :], ps[:, 4 + v % 2, 0:n * P]
                             .rearrange("p (t c) -> p t c", t=n)).then_inc(s_wtc, 1)
                if i >= 2:
                    v = i - 2
                    g, h, t = ATT[v]
                    act.wait_ge(s_pv, v + 1)
                    act.copy(OD[:, GROUPS[g][0] + t, h * DV:(h + 1) * DV], ps[:, 6 + v % 2, 0:DV])\
                        .then_inc(s_pvc, 1)

            act.wait_ge(s_w, len(ATT))
            act.activation(tmpE, OG, ACT.Exp, scale=-1.0).then_inc(s_ego, 1)
            act.wait_ge(s_vare, 1)
            act.activation(st[:, 112:160], st[:, 64:112], ACT.Sqrt).then_inc(s_rte, 1)
            for t in range(NT):
                act.wait_ge(s_mt, 2 * t + 1)
                act.copy(HT[:, 0:4, t * P:(t + 1) * P],
                         ps[:, 2 * (t % 2), :].rearrange("p (k c) -> p k c", k=4)).then_inc(s_mta, 1)

            for t in range(NT):
                act.wait_ge(s_x1, 2 * (t + 1))
                act.activation(junk, X[:, t, :], ACT.Square, accum_out=st[:, t:t + 1]).then_inc(s_ss2, 1)
                act.wait_ge(s_var2, t + 1)
                act.activation(st[:, 16 + t:17 + t], st[:, 8 + t:9 + t], ACT.Sqrt).then_inc(s_rt2, 1)
            for t in range(NT):
                act.wait_ge(s_tr2, 2 * t + 1)
                if t >= 2:
                    act.wait_ge(s_lg, t - 1)
                act.copy(h2T[t % 2][:, 0:4, :],
                         ps[:, 2 * (t % 2), :].rearrange("p (k c) -> p k c", k=4)).then_inc(s_h2a, 1)
                act.wait_ge(s_lmx, t + 1)
                act.activation(st[:, 64 + 16 * (t % 2):80 + 16 * (t % 2)], ps[:, 4 + t % 2, 0:NE], ACT.Exp,
                               bias=st[:, 56 + t % 2:57 + t % 2],
                               accum_out=st[:, 58 + t % 2:59 + t % 2]).then_inc(s_lex, 1)

            def split(i, n):
                act.wait_ge(s_land[n % RAW], i * (16 * NTI // RAW) + 16 * (n // RAW + 1))
                if not (isinstance(i, int) and i == 0 and n < CONV):
                    act.wait_ge(s_used, i * NTI + (n - CONV + 1))
                act.copy(wh[:, n % CONV, :], raw[:, n % RAW, :]).then_inc(s_wh, 1)

            def xt_copy(e, half, j):
                act.wait_ge(s_xtp, 2 * e + (half + 1))
                act.copy(XTh[j][:, 4 * half:4 * half + 4, :],
                         ps[:, 7, 0:4 * CAP].rearrange("p (k c) -> p k c", k=4)).then_inc(s_xth, 1)

            def y_copy(i, j):
                act.wait_ge(s_sel, 2 * i + (j + 1))
                act.wait_ge(*tile_used(i, "d", NS * (j + 1) - 1))
                for half in range(2):
                    act.mul(Yh[j][0:CAP, half * 512:(half + 1) * 512], ps[0:CAP, 4 + half, :],
                            cur[0:CAP, 1:2]).then_inc(s_yh, 1)

            def pair(i, last):
                for n in range(NTI):
                    kind, q, part_ = TILES[n]
                    if part_ == 0 and kind == "u" and q >= 1:
                        act.wait_ge(s_hT, 8 * i + q)
                        act.copy(gTh[:], ps[:, 6, 0:FC * CAP].rearrange("p (f c) -> p f c", f=FC))\
                            .then_inc(s_gth, 1)
                    turns = kind in "ud" and q % NS == (1 if kind == "u" else 0) and part_ == 0 \
                        and (kind == "u" or q % NS == 0) and not (last and q >= NS)
                    if turns:
                        e = 2 * i + (q // NS + 1)
                        xt_copy(e, 0 if kind == "u" else 1, (q // NS + 1) % 2)
                    if n >= 1 and TILES[n - 1][0] == "u" and TILES[n - 1][2] == 1:
                        qq = TILES[n - 1][1]
                        act.wait_ge(*tile_used(i, "u", qq))
                        act.activation(hid[0:CAP], ps[0:CAP, qq % 2, :], ACT.Silu).then_inc(s_silu, 1)
                    if n >= 1 and TILES[n - 1] == ("d", NS - 1, 1):
                        y_copy(i, 0)
                    if n == place["d", 2 * NS - 1, 0]:
                        act.wait_ge(s_hT, 8 * i + 2 * NS)
                        act.copy(gTh[:], ps[:, 6, 0:FC * CAP].rearrange("p (f c) -> p f c", f=FC))\
                            .then_inc(s_gth, 1)
                    if not (last and n + AHEAD >= NTI):
                        split(i, n + AHEAD) if n + AHEAD < NTI else split(i + 1, n + AHEAD - NTI)
                y_copy(i, 1)

            xt_copy(0, 0, 0)
            xt_copy(0, 1, 0)
            for n in range(AHEAD):
                split(0, n)
            with act.Fori(0, NPAIR - 1) as i:
                pair(i, False)
            pair(NPAIR - 1, True)

        @block.vector
        def _(dve):
            ch = Chain(dve, s_dve)
            dve.wait_ge(s_const, 16 * NCONST)
            for s in range(2):
                for ab in range(2):
                    m = 2 * s + ab
                    dve.tensor_tensor(tabs[:, m, :, :], tabs[:, m, :, :],
                                      gains[:, m, :].unsqueeze(1).broadcast_to([P, 4, DK]),
                                      ALU.mult).then_inc(s_tab, 1)
            ch.mark(dve.tensor_tensor_reduce(lamv[:, 0, :], lamv[:, 0, :], lamv[:, 1, :], 1.0, 0.0,
                                             ALU.mult, ALU.add, nlam[:, 0:1]))
            dve.tensor_tensor_reduce(lamv[:, 2, :], lamv[:, 2, :], lamv[:, 3, :], 1.0, 0.0,
                                     ALU.mult, ALU.add, nlam[:, 1:2]).then_inc(s_lamd, 1)
            ch.mark(dve.tensor_scalar(og_gain[:, 1, :], og_gain[:, 1, :], 1.0 - LAM_INIT, None, ALU.mult))
            dve.wait_ge(s_lame, 1)
            ch.link(dve.tensor_tensor(nlam[:, 0:1], nlam[:, 3:4], nlam[:, 2:3], ALU.subtract))
            ch.mark(dve.tensor_scalar(nlam[:, 0:1], nlam[:, 0:1], -LAM_INIT, None, ALU.add))

            for t in range(NT + 1):
                if t < NT:
                    dve.wait_ge(s_ss1, t + 1)
                    dve.tensor_scalar(st[:, 8 + t:9 + t], st[:, t:t + 1], 1.0 / D, EPS, ALU.mult, ALU.add)\
                        .then_inc(s_var1, 1)
                    dve.wait_ge(s_rt1, t + 1)
                    ch.link(dve.reciprocal(st[:, 16 + t:17 + t], st[:, 16 + t:17 + t]))
                    if t >= 2:
                        dve.wait_ge(s_tr1, 2 * (t - 1))
                    dve.scalar_tensor_tensor(hn[:, t % 2, :], X[:, t, :], st[:, 16 + t:17 + t], gnorm[:],
                                             ALU.mult, ALU.mult).then_inc(s_hn1, 1)
                if t >= 1:
                    v = t - 1
                    dve.wait_ge(s_tr1, 2 * v + 2)
                    dve.tensor_copy(HT[:, 4:8, v * P:(v + 1) * P],
                                    ps[:, 2 * (v % 2) + 1, :].rearrange("p (k c) -> p k c", k=4))\
                        .then_inc(s_ht_d, 1)

            def rope_add(v):
                dve.wait_ge(s_swap, 2 * (v + 1))
                dve.tensor_tensor(t1[v % 2], t1[v % 2], t2[v % 2], ALU.add).then_inc(s_rope, 1)

            dve.wait_ge(s_tab, 4)
            for u, (kind, s, t) in enumerate(UNITS):
                if kind != "dqk":
                    continue
                v = s * NT + t
                pos = t if t < 2 else t - 2
                b8 = 8 * (v % 2)
                dve.wait_ge(s_sq, v + 1)
                dve.tensor_reduce(st[:, 24 + b8:32 + b8], sq[v % 2].rearrange("p (m c) -> p m c", m=8),
                                  AX_X, ALU.add).then_inc(s_sumq, 1)
                dve.wait_ge(s_sumq, v + 1)
                dve.tensor_scalar(st[:, 24 + b8:32 + b8], st[:, 24 + b8:32 + b8], 1.0 / DK, EPS,
                                  ALU.mult, ALU.add).then_inc(s_varq, 1)
                if v >= 1:
                    rope_add(v - 1)
                dve.wait_ge(s_rtq, v + 1)
                ch.link(dve.reciprocal(st[:, 40 + b8:48 + b8], st[:, 40 + b8:48 + b8]))
                if v >= 2:
                    dve.wait_ge(s_swap, 2 * (v - 1))
                dve.tensor_tensor(yr[v % 2].rearrange("p (m c) -> p m c", m=8),
                                  ps[:, u % 8, :].rearrange("p (m c) -> p m c", m=8),
                                  st[:, 40 + b8:48 + b8].unsqueeze(2).broadcast_to([P, 8, DK]),
                                  ALU.mult).then_inc(s_free_d, 1)
                dve.wait_ge(s_free_d, v + 1)
                if v >= 2:
                    dve.wait_ge(s_unit, UNITS.index(("rope", (v - 2) // NT, (v - 2) % NT)) + 1)
                ch.link(dve.tensor_tensor(t1[v % 2].rearrange("p (m c) -> p m c", m=8),
                                          yr[v % 2].rearrange("p (m c) -> p m c", m=8),
                                          tabs[:, 2 * s, pos, :].unsqueeze(1).broadcast_to([P, 8, DK]),
                                          ALU.mult))
            rope_add(2 * NT - 1)

            dve.wait_ge(s_z, 1)
            ch.mark(dve.memset(Ssb, 0.0))
            ch.link(dve.memset(states, 0.0))
            by_chunk = lambda x: x.rearrange("p (n c) -> p n c", n=NCH)
            for h in range(HEADS):
                if h >= 1:
                    dve.wait_ge(s_e1, h)
                for g, (t0, n) in enumerate(GROUPS):
                    dve.wait_ge(s_z, 2 * h + g + 1)
                    dve.tensor_scalar(zT1[:, t0 * P:(t0 + n) * P], ps[:, g, 0:n * P], bg[:, h:h + 1], None,
                                      ALU.add).then_inc(s_zb, 1)
                dve.wait_ge(s_zb, 2 * h + 2)
                if h >= 1:
                    dve.wait_ge(s_e4, h)
                dve.scalar_tensor_tensor(zT2, zT1, -1.0, zT1, ALU.mult, ALU.max).then_inc(s_absz, 1)
                dve.wait_ge(s_sp, h + 1)
                ch.link(dve.scalar_tensor_tensor(zT2, zT1, 0.0, zT2, ALU.min, ALU.subtract))
                if h >= 1:
                    dve.wait_ge(s_e3, h)
                    dve.wait_ge(s_dlast, h)
                dve.tensor_tensor_scan(cum[0:DK], scanm[0:DK], zT2[0:DK], 0.0, ALU.mult, ALU.add)
                dve.tensor_tensor_scan(cum[DK:P, ::-1], scanm[DK:P, ::-1], zT2[DK:P, ::-1], 0.0,
                                       ALU.mult, ALU.add).then_inc(s_cum, 1)
                dve.wait_ge(s_cum, h + 1)
                if h >= 1:
                    dve.wait_ge(s_dec, h)
                dve.tensor_copy(bmid[0:DK], by_chunk(cum)[0:DK, :, CHUNK // 2 - 1])
                dve.tensor_copy(bmid[DK:P], by_chunk(cum)[DK:P, :, CHUNK // 2])
                dve.tensor_copy(blast[0:DK], by_chunk(cum)[0:DK, :, CHUNK - 1])
                dve.tensor_copy(blast[DK:P], by_chunk(cum)[DK:P, :, 0]).then_inc(s_mid, 1)
                dve.wait_ge(s_mid, h + 1)
                dve.tensor_tensor(by_chunk(zT1), by_chunk(cum), bmid.unsqueeze(2).broadcast_to([P, NCH, CHUNK]),
                                  ALU.subtract).then_inc(s_dmid, 1)
                dve.wait_ge(s_e1, h + 1)
                dve.tensor_tensor(qtil, qtil, Q[:, h, :], ALU.mult).then_inc(s_qt, 1)
                dve.tensor_tensor(ktil, ktil, K[:, h, :], ALU.mult).then_inc(s_qt, 1)
                for g, (t0, n) in enumerate(GROUPS):
                    dve.wait_ge(s_sc, 2 * h + g + 1)
                    if h >= 1:
                        dve.wait_ge(s_o, 2 * (h - 1) + g + 1)
                    for d in range(2):
                        last = dve.copy_predicated(Ssb[:, t0:t0 + n, :],
                                                   pmask[:, d, :].unsqueeze(1).broadcast_to([P, n, P]),
                                                   ps[:, 2 + d, 0:n * P].rearrange("p (t c) -> p t c", t=n))
                        if d == 0:
                            ch.link(last)
                    last.then_inc(s_pred, 1)
                    dve.wait_ge(s_u, 2 * h + g + 1)
                    dve.wait_ge(s_dec, h + 1)
                    c0, nc_ = 2 * t0, 2 * n
                    for m in range(nc_ - 1):
                        for d, c, nxt in ((0, c0 + m, c0 + m + 1), (1, c0 + nc_ - 1 - m, c0 + nc_ - 2 - m)):
                            r = slice(d * DK, (d + 1) * DK)
                            t = c // 2 - t0
                            last = dve.scalar_tensor_tensor(states[r, nxt, :], states[r, c, :], decay[r, c:c + 1],
                                                            ps[r, 6 + c % 2, t * P:(t + 1) * P],
                                                            ALU.mult, ALU.add)
                        if m < nc_ - 2:
                            ch.link(last)
                    last.then_inc(s_st, 1)

            for i in range(len(ATT) + 1):
                if i < len(ATT):
                    n = GROUPS[ATT[i][0]][1] * P
                    b = 2 * (i % 2)
                    dve.wait_ge(s_s, i + 1)
                    if i >= 2:
                        dve.wait_ge(s_p, 2 * (i - 1))
                    dve.tensor_reduce(st[:, 56 + b:58 + b], ps[:, b:b + 2, 0:n], AX_X, ALU.max, negate=True)\
                        .then_inc(s_mx, 1)
                if i >= 1:
                    v = i - 1
                    n = GROUPS[ATT[v][0]][1] * P
                    b = 2 * (v % 2)
                    dve.wait_ge(s_p, 2 * v + 2)
                    ch.link(dve.reciprocal(st[:, 160 + b:162 + b], st[:, 60 + b:62 + b]))
                    ch.link(dve.tensor_tensor(st[:, 164 + b:165 + b], st[:, 161 + b:162 + b], nlam[:, 0:1],
                                              ALU.mult))
                    if v >= 2:
                        dve.wait_ge(s_wt, v - 1)
                    ch.link(dve.tensor_scalar(wmix[v % 2][:, 0:n], prob[v % 2][:, 1, 0:n],
                                              st[:, 164 + b:165 + b], None, ALU.mult))
                    dve.scalar_tensor_tensor(wmix[v % 2][:, 0:n], prob[v % 2][:, 0, 0:n],
                                             st[:, 160 + b:161 + b], wmix[v % 2][:, 0:n],
                                             ALU.mult, ALU.add).then_inc(s_w, 1)

            dve.wait_ge(s_oc, 2 * HEADS)
            dve.wait_ge(s_pvc, len(ATT))
            square = QT.rearrange("p h t -> p (h t)")
            sums = st[:, 64:112].rearrange("p (t m) -> p t m", t=NT)
            roots = st[:, 112:160].rearrange("p (t m) -> p t m", t=NT)
            fl = lambda x: x.rearrange("p t n -> p (t n)")
            for m, o_ in enumerate((OA, OD)):
                ch.link(dve.tensor_tensor(square, fl(o_), fl(o_), ALU.mult))
                ch.link(dve.tensor_reduce(sums[:, :, 4 * m:4 * m + 4],
                                          square.rearrange("p (t h c) -> p t h c", t=NT, h=HEADS),
                                          AX_X, ALU.add))
            dve.tensor_scalar(st[:, 64:112], st[:, 64:112], 1.0 / DV, EPS, ALU.mult, ALU.add).then_inc(s_vare, 1)
            dve.wait_ge(s_ego, 1)
            ch.link(dve.tensor_scalar(fl(tmpE), fl(tmpE), 1.0, None, ALU.add))
            ch.link(dve.reciprocal(fl(tmpE), fl(tmpE)))
            ch.link(dve.tensor_tensor(fl(tmpE), fl(tmpE), fl(OG), ALU.mult))
            dve.wait_ge(s_rte, 1)
            ch.link(dve.reciprocal(st[:, 112:160], st[:, 112:160]))
            for m, o_ in enumerate((OA, OD)):
                o4 = o_.rearrange("p t (h c) -> p t h c", h=HEADS)
                ch.link(dve.tensor_tensor(o4, o4, roots[:, :, 4 * m:4 * m + 4].unsqueeze(3)
                                          .broadcast_to([P, NT, HEADS, DV]), ALU.mult))
                o3 = fl(o_).rearrange("p (m c) -> p m c", c=DV)
                ins = dve.tensor_tensor(o3, o3, og_gain[:, m, :].unsqueeze(1)
                                        .broadcast_to([P, NT * HEADS, DV]), ALU.mult)
                if m == 0:
                    ch.link(ins)
                    ins = dve.tensor_tensor(fl(o_), fl(o_), fl(tmpE), ALU.mult)
                ins.then_inc(s_mix, 1)

            for t in range(NT + 1):
                if t < NT:
                    dve.wait_ge(s_mt, 2 * t + 2)
                    dve.tensor_copy(HT[:, 4:8, t * P:(t + 1) * P],
                                    ps[:, 2 * (t % 2) + 1, :].rearrange("p (k c) -> p k c", k=4))\
                        .then_inc(s_mtd, 1)
                if t >= 1:
                    for f in range(2):
                        u = 2 * (t - 1) + f
                        dve.wait_ge(s_op, u + 1)
                        x = X[:, t - 1, f * 512:(f + 1) * 512]
                        dve.tensor_tensor(x, x, ps[:, 4 + u % 4, :], ALU.add).then_inc(s_x1, 1)

            for t in range(NT):
                dve.wait_ge(s_ss2, t + 1)
                dve.tensor_scalar(st[:, 8 + t:9 + t], st[:, t:t + 1], 1.0 / D, EPS, ALU.mult, ALU.add)\
                    .then_inc(s_var2, 1)
            dve.wait_ge(s_rt2, NT)
            ch.link(dve.reciprocal(st[:, 16:16 + NT], st[:, 16:16 + NT]))
            dve.wait_ge(s_late, 32)
            for t in range(NT):
                if t >= 2:
                    dve.wait_ge(s_h2w[t % 2], 16 * (t // 2))
                    dve.wait_ge(s_tr2, 2 * (t - 1))
                dve.scalar_tensor_tensor(hn[:, t % 2, :], X[:, t, :], st[:, 16 + t:17 + t], gnorm[:],
                                         ALU.mult, ALU.mult).then_inc(s_hn2, 1)
                dve.wait_ge(s_tr2, 2 * t + 2)
                if t >= 2:
                    dve.wait_ge(s_lg, t - 1)
                dve.tensor_copy(h2T[t % 2][:, 4:8, :],
                                ps[:, 2 * (t % 2) + 1, :].rearrange("p (k c) -> p k c", k=4)).then_inc(s_h2d, 1)
                dve.wait_ge(s_lg, t + 1)
                b = t % 2
                dve.tensor_reduce(st[:, 56 + b:57 + b], ps[:, 4 + b, 0:NE], AX_X, ALU.max, negate=True)\
                    .then_inc(s_lmx, 1)
                dve.wait_ge(s_lex, t + 1)
                ch.link(dve.reciprocal(st[:, 58 + b:59 + b], st[:, 58 + b:59 + b]))
                if t >= 2:
                    dve.wait_ge(s_afT, t - 1)
                dve.tensor_scalar(st[:, 96 + 16 * b:112 + 16 * b], st[:, 64 + 16 * b:80 + 16 * b],
                                  st[:, 58 + b:59 + b], None, ALU.mult).then_inc(s_aff, 1)
                dve.wait_ge(s_afT, t + 1)
                dve.tensor_copy(aff[:, t * P:(t + 1) * P], ps[0:NE, 6 + b, 0:P]).then_inc(s_afc, 1)

            dve.wait_ge(s_afc, NT)
            for lo, n, c0, cap in ((0, T_PROMPT, 0, CAP_P), (T_PROMPT, T_SAMPLE, CAP_P, CAP_S)):
                row = aff[:, lo:lo + n]
                for c in range(c0, c0 + cap, 8):
                    ch.link(dve.max(topv[:, c:c + 8], row))
                    ch.link(dve.max_index(topi[:, c:c + 8], topv[:, c:c + 8], row))
                    ch.link(dve.match_replace(row, topv[:, c:c + 8], row, -1.0))
            ch.link(dve.tensor_copy(topf, topi))
            dve.tensor_scalar(topf[:, CAP_P:CAP], topf[:, CAP_P:CAP], float(T_PROMPT), None, ALU.add)\
                .then_inc(s_top, 1)
            dve.wait_ge(s_topT, 1)
            ch.mark(dve.tensor_copy(gidx[0:CAP, 0:NE], ps[0:CAP, 0, 0:NE]))
            ch.mark(dve.tensor_copy(grow[0:CAP, :], ps[0:CAP, 0, 0:NE]))
            dve.tensor_copy(gate[0:CAP, :], ps[0:CAP, 0, 32:32 + NE]).then_inc(s_route, 1)
            dve.wait_ge(s_route, 1)
            dve.tensor_copy(idx_col[0:CAP, 0:1], gidx[0:CAP, 0:1]).then_inc(s_icol, 1)

            def split(i, n):
                dve.wait_ge(s_wh, i * NTI + (n + 1))
                dve.tensor_tensor(wl[:, n % CONV, :], raw[:, n % RAW, :], wh[:, n % CONV, :].bitcast(F32),
                                  ALU.subtract).then_inc(s_wl, 1)

            def xt_copy(e, half, j):
                dve.wait_ge(s_xth, 2 * e + (half + 1))
                dve.tensor_tensor(XTl[j][:, 4 * half:4 * half + 4, :],
                                  ps[:, 7, 0:4 * CAP].rearrange("p (k c) -> p k c", k=4),
                                  XTh[j][:, 4 * half:4 * half + 4, :].bitcast(F32), ALU.subtract).then_inc(s_xtl, 1)

            def y_copy(i, j):
                for half in range(2):
                    c = slice(half * 512, (half + 1) * 512)
                    dve.wait_ge(s_yh, 4 * i + (2 * j + half + 1))
                    dve.scalar_tensor_tensor(Yl[j][0:CAP, c], ps[0:CAP, 4 + half, :], cur[0:CAP, 1:2],
                                             Yh[j][0:CAP, c].bitcast(F32), ALU.mult, ALU.subtract).then_inc(s_yl, 1)

            def next_rows(i, j):
                dve.wait_ge(s_gat, 32 * i + 16 * (j + 1))
                dve.tensor_copy(idx_col[0:CAP, 0:1], gidx[0:CAP, bass.ds(2 * i + (j + 1), 1)])\
                    .then_inc(s_icol, 1)

            def selection(i, j):
                ch.mark(dve.tensor_copy(cur[0:CAP, 0:1], grow[0:CAP, bass.ds(2 * i + j, 1)]))
                ch.link(dve.tensor_copy(cur[0:CAP, 1:2], gate[0:CAP, bass.ds(2 * i + j, 1)]))
                dve.tensor_scalar(sel[j][0:CAP], iota[0:CAP], cur[0:CAP, 0:1], None, ALU.is_equal)\
                    .then_inc(s_sel, 1)

            def pair(i, last):
                for n in range(NTI):
                    kind, q, part_ = TILES[n]
                    if n == 0:
                        next_rows(i, 0)
                        selection(i, 0)
                    if part_ == 0 and kind == "u" and q >= 1:
                        dve.wait_ge(s_gth, 8 * i + q)
                        dve.tensor_tensor(gTl[:], ps[:, 6, 0:FC * CAP].rearrange("p (f c) -> p f c", f=FC),
                                          gTh[:].bitcast(F32), ALU.subtract).then_inc(s_gtl, 1)
                    turns = kind in "ud" and q % NS == (1 if kind == "u" else 0) and part_ == 0 \
                        and (kind == "u" or q % NS == 0) and not (last and q >= NS)
                    if turns:
                        e = 2 * i + (q // NS + 1)
                        xt_copy(e, 0 if kind == "u" else 1, (q // NS + 1) % 2)
                        if kind == "d" and q == 0 and not last:
                            next_rows(i, 1)
                    if n >= 1 and TILES[n - 1][0] == "u" and TILES[n - 1][2] == 1:
                        qq = TILES[n - 1][1]
                        dve.wait_ge(s_silu, 8 * i + (qq + 1))
                        dve.tensor_tensor(hid[0:CAP], hid[0:CAP], ps[0:CAP, 2 + qq % 2, :], ALU.mult)\
                            .then_inc(s_hid, 1)
                    if n >= 1 and TILES[n - 1] == ("d", NS - 1, 1):
                        y_copy(i, 0)
                        dve.wait_ge(s_yl, 4 * i + 2)
                        selection(i, 1)
                    if n == place["d", 2 * NS - 1, 0]:
                        dve.wait_ge(s_gth, 8 * i + 2 * NS)
                        dve.tensor_tensor(gTl[:], ps[:, 6, 0:FC * CAP].rearrange("p (f c) -> p f c", f=FC),
                                          gTh[:].bitcast(F32), ALU.subtract).then_inc(s_gtl, 1)
                    if not (last and n + AHEAD >= NTI):
                        split(i, n + AHEAD) if n + AHEAD < NTI else split(i + 1, n + AHEAD - NTI)
                y_copy(i, 1)
                banks = (0, 1, 2, 3, 6, 7)
                for u in range(2 * NT):
                    dve.wait_ge(s_scat, 2 * NT * i + (u + 1))
                    x = X[:, u // 2, (u % 2) * 512:(u % 2 + 1) * 512]
                    dve.tensor_tensor(x, x, ps[:, banks[u % len(banks)], :], ALU.add).then_inc(s_acc, 1)

            xt_copy(0, 0, 0)
            xt_copy(0, 1, 0)
            for n in range(AHEAD):
                split(0, n)
            steps = 4
            n0 = ch.n
            with dve.Fori(0, NPAIR - 1) as i:
                ch.base = i * steps
                pair(i, False)
            assert ch.n - n0 == steps
            ch.n, ch.base = n0 + (NPAIR - 1) * steps, 0
            pair(NPAIR - 1, True)


_INPUTS = ("x_prompt", "x_sample", "norm1_g", "w_in", "gla_wg_f", "gla_bg_f", "gla_wg_b", "gla_bg_b",
           "gla_norm_g", "qk_norm_q", "qk_norm_k", "lambda_q1", "lambda_k1", "lambda_q2", "lambda_k2",
           "diff_norm_g", "w_out", "norm2_g", "w_router", "w_gate", "w_up", "w_down")


def shape_constants():
    f = np.float32
    inv = np.power(f(10000.0), -np.arange(0, DK, 2, dtype=f) / f(DK)).astype(f)
    ang = np.arange(T_SAMPLE, dtype=f)[:, None] * inv[None, :]
    cos, sin = np.cos(ang).astype(f), np.sin(ang).astype(f)
    A = np.concatenate([cos, cos], 1).reshape(4, P, DK).transpose(1, 0, 2)
    B = np.concatenate([-sin, sin], 1).reshape(4, P, DK).transpose(1, 0, 2)
    sc = f(DK ** -0.5)
    rot = np.stack([A * sc, B * sc, A, B], 1).reshape(P, -1)
    scan = np.ones((P, TOK), f)
    scan[:DK, ::CHUNK] = 0
    scan[DK:, CHUNK - 1::CHUNK] = 0
    key, qry = np.arange(P)[:, None], np.arange(P)[None, :]
    same = (key // CHUNK) == (qry // CHUNK)
    mask = np.concatenate([same & (qry >= key), same & (qry < key)], 1).astype(np.uint32)
    return {"ident": np.eye(P, dtype=f), "rot": np.ascontiguousarray(rot), "scan_mask": scan,
            "pair_mask": mask, "iota": np.broadcast_to(np.arange(TOK, dtype=f), (P, TOK)).copy()}


def kernel(**inputs):
    import concourse.bacc as bacc
    from concourse.bass_utils import run_bass_kernel_spmd

    nc = bacc.Bacc("TRN2", target_bir_lowering=False, num_devices=1)
    arrays, aps = {}, {}
    data = {n: np.ascontiguousarray(inputs[n]) for n in _INPUTS}
    data.update(shape_constants())
    for name, x in data.items():
        arrays[f"in_{name}"] = x
        aps[name] = nc.dram_tensor(f"in_{name}", x.shape, mybir.dt.from_np(x.dtype), kind="ExternalInput").ap()
    y_prompt = nc.dram_tensor("y_prompt", (1, T_PROMPT, D), F32, kind="ExternalOutput").ap()
    y_sample = nc.dram_tensor("y_sample", (1, T_SAMPLE, D), F32, kind="ExternalOutput").ap()
    h2 = nc.dram_tensor("h2_rows", (TOK, D), F32, kind="Internal").ap()
    build(nc, aps, y_prompt, y_sample, h2)
    r = run_bass_kernel_spmd(nc, [arrays], core_ids=[0])
    return r.results[0]["y_prompt"], r.results[0]["y_sample"]
```

```python
from contextlib import ExitStack

import numpy as np

import concourse.bass as bass
from concourse import mybir
from concourse.alu_op_type import AluOpType as ALU

ACT = mybir.ActivationFunctionType
F32 = mybir.dt.float32
F32R = mybir.dt.float32r
U32 = mybir.dt.uint32
AX_X = mybir.AxisListType.X

P = 128
D = 1024
KD = D // P
T_PROMPT, T_SAMPLE = 256, 512
TOK = T_PROMPT + T_SAMPLE
NT = TOK // P
GROUPS = ((0, 2), (2, 4))
HEADS = 4
DK, DV = 64, 128
RANK = 16
CHUNK = 64
NCH = TOK // CHUNK
SL = 512
C_QK, C_V, C_OG, C_LR = 0, 512, 1024, 1536
C_DQ, C_DK, C_DV = 1568, 2080, 2592
SLICES = (C_QK, C_DQ, C_DK, C_V, C_DV, C_OG)
EPS = 1e-6
TAU = 16.0
LAM_INIT = 0.2
NE = 16
FE = 2 * D
CAP_P, CAP_S = 2 * T_PROMPT // NE, 2 * T_SAMPLE // NE
CAP = CAP_P + CAP_S
NPAIR = NE // 2
FS = 512
NS = FE // FS
FC = FS // P
RAW = 8
CONV = 4
AHEAD = 3
TW = 2048


def tile_plan():
    plan = []
    for c in range(4):
        plan += [("qk", c, 0), ("qk", c, 1)]
    plan += [("lr", 0, 0), ("lr", 0, 1)]
    body = [("dqk", s, t) for s in range(2) for t in range(NT)]
    body += [("tok", s, t) for s in range(3, 6) for t in range(NT)]
    lag = 3
    for n, u in enumerate(body):
        plan.append(u)
        if n >= lag and n - lag < 2 * NT:
            v = n - lag
            plan.append(("rope", v // NT, v % NT))
    return plan


def evacuated_by(kind):
    return "dve" if kind == "dqk" else "act"


def weight_plan():
    order = []
    for q in range(2 * NS):
        order += [("g", q, 0), ("g", q, 1), ("u", q, 0), ("u", q, 1)]
        if q >= 1:
            order += [("d", q - 1, 0), ("d", q - 1, 1)]
    return order + [("d", 2 * NS - 1, 0), ("d", 2 * NS - 1, 1)]


class Chain:

    def __init__(self, eng, sem):
        self.eng, self.sem, self.n, self.base = eng, sem, 0, 0

    def mark(self, ins):
        self.n += 1
        return ins.then_inc(self.sem, 1)

    def own(self):
        self.eng.wait_ge(self.sem, self.base + self.n)

    def link(self, ins):
        self.mark(ins)
        self.own()


def build(nc, a, y_prompt, y_sample, h2_dram):
    ctx = ExitStack()
    with ctx:
        def sb(name, shape, dt=F32):
            return ctx.enter_context(nc.sbuf_tensor(name, shape, dt))

        def sem(name):
            return ctx.enter_context(nc.semaphore(name))

        ps = ctx.enter_context(nc.psum_tensor("ps", [P, 8, 512], F32))

        span = 210304
        sb("whole", [P, span // 4])
        origin = nc.sbuf_base - span

        def at(name, off, shape, dt=F32):
            return nc.alloc_sbuf_tensor_at(name, shape, dt, offset=origin + off)

        ring = at("ring", 0, [P, 8, 4096])
        wh = at("wh", 0, [P, CONV, TW], F32R)
        wl = at("wl", 32768, [P, CONV, TW], F32R)
        raw = at("raw", 65536, [P, RAW, TW])
        X = at("X", 131072, [P, NT, D])
        HT = at("HT", 155648, [P, KD, TOK])
        Yh = [at(f"Yh{j}", 155648 + 8192 * j, [P, D], F32R) for j in range(2)]
        Yl = [at(f"Yl{j}", 159744 + 8192 * j, [P, D], F32R) for j in range(2)]
        gTh = at("gTh", 172032, [P, FC, CAP], F32R)
        gTl = at("gTl", 173568, [P, FC, CAP], F32R)
        hid = at("hid", 175104, [P, FS])
        XTh = [at("XTh0", 177152, [P, KD, CAP], F32R), at("XTh1", 199680, [P, KD, CAP], F32R)]
        hn = at("hn", 180224, [P, 2, D])
        XE = at("XE", 180224, [P, D])
        sel = [at("sel0", 184320, [P, TOK], F32R), at("sel1", 196608, [P, TOK], F32R)]
        gnorm = at("gnorm", 188416, [P, D])
        XTl = [at("XTl0", 188416, [P, KD, CAP], F32R), at("XTl1", 205824, [P, KD, CAP], F32R)]
        tabs = at("tabs", 192512, [P, 4, 4, DK])
        wlr = at("wlr", 196608, [P, KD, 2 * RANK])
        wg = at("wg", 197632, [2 * RANK, HEADS, P])
        lrT = at("lrT", 199680, [2 * RANK, TOK])
        scanm = at("scanm", 202752, [P, TOK])
        pmask = at("pmask", 205824, [P, 2, P], U32)
        og_gain = at("og_gain", 206848, [P, 2, DV])
        wr = at("wr", 207872, [P, KD, NE])
        ident = at("ident", 208896, [P, P])
        st = at("st", 209408, [P, 192])
        bg = at("bg", 210176, [P, HEADS])
        nlam = at("nlam", 210208, [P, 4])
        idx_col = at("idx_col", 210240, [P, 2], U32)
        cur = at("cur", 210272, [P, 2])

        flat = ring[:].rearrange("p r n -> p (r n)")

        def part(off, n, base=flat):
            return base[:, off:off + n]

        W = [ring[:, s, :].rearrange("p (k n) -> p k n", k=KD) for s in range(2)]
        o = 2 * 4096
        Q = part(o, 3072).rearrange("p (h t) -> p h t", h=HEADS); o += 3072
        K = part(o, 3072).rearrange("p (h t) -> p h t", h=HEADS); o += 3072
        V = part(o, 3072).rearrange("p (t n) -> p t n", t=NT); o += 3072
        VD = part(o, 3072).rearrange("p (t n) -> p t n", t=NT); o += 3072
        OG = part(o, 3072).rearrange("p (t n) -> p t n", t=NT); o += 3072
        QT = part(o, 3072).rearrange("p (h t) -> p h t", h=HEADS); o += 3072
        KT = part(o, 3072).rearrange("p (h t) -> p h t", h=HEADS); o += 3072
        OA = part(o, 3072).rearrange("p (t n) -> p t n", t=NT); o += 3072
        assert o == 8 * 4096
        OD = K.rearrange("p h t -> p (h t)").rearrange("p (t n) -> p t n", t=NT)
        oaf = OA.rearrange("p t n -> p (t n)")
        hnf = hn[:].rearrange("p b n -> p (b n)")
        sq = [part(0, SL, oaf), part(SL, SL, oaf)]
        yr = [part(2 * SL, SL, oaf), part(3 * SL, SL, oaf)]
        t1 = [part(4 * SL, SL, oaf), part(5 * SL, SL, oaf)]
        t2 = [part(0, SL, hnf), part(SL, SL, hnf)]
        gains = OG[:, 0, 0:256].rearrange("p (m d) -> p m d", m=4)
        lamv = OG[:, 0, 256:512].rearrange("p (m d) -> p m d", m=4)
        zT1, zT2, cum = (part(n * TOK, TOK) for n in range(3))
        htf = HT[:].rearrange("p k t -> p (k t)")
        qtil, ktil, qhat, khat, khT, states = ([], [], [], [], [], [])
        for basis, o in ((flat, 3 * TOK), (htf, 0)):
            for made in (qtil, ktil, qhat, khat):
                made.append(part(o, TOK, basis)); o += TOK
            khT.append(part(o, TOK, basis).rearrange("p (t c) -> p t c", t=NT)); o += TOK
            states.append(part(o, NCH * DV, basis).rearrange("p (n e) -> p n e", n=NCH)); o += NCH * DV
            assert o <= (2 * 4096 if basis is flat else 7 * TOK)
        Ssb = [part(0, TOK, hnf).rearrange("p (t c) -> p t c", t=NT),
               part(7 * TOK, TOK, htf).rearrange("p (t c) -> p t c", t=NT)]
        bmid = part(TOK, NCH, hnf)
        blast = part(TOK + NCH, NCH, hnf)
        decay = [part(TOK + (2 + n) * NCH, NCH, hnf) for n in range(2)]
        qf = Q.rearrange("p h t -> p (h t)")
        prob = [part(0, 1024, qf).rearrange("p (m n) -> p m n", m=2),
                part(1024, 1024, qf).rearrange("p (m n) -> p m n", m=2)]
        wmix = [part(2048, 512, qf), part(2560, 512, qf)]
        wT = [part(1024, 512, hnf).rearrange("p (t c) -> p t c", t=4),
              part(1536, 512, hnf).rearrange("p (t c) -> p t c", t=4)]
        square = [part(0, SL, hnf), part(SL, SL, hnf)]
        h2T = [part(n * D, D, qf).rearrange("p (k c) -> p k c", k=KD) for n in range(2)]
        junk = part(2 * D, D, qf)
        junk1 = ring[:, 6, 0:1024]
        iota = scanm[:]
        tabf = tabs[:].rearrange("p a b c -> p (a b c)")
        aff = lrT[0:NE, :]
        topv = part(0, CAP, tabf)[0:NE]
        topf = part(CAP, CAP, tabf)[0:NE]
        topi = part(2 * CAP, CAP, tabf)[0:NE].bitcast(U32)
        gidx = part(3 * CAP, NE + 1, tabf).bitcast(U32)
        grow = part(3 * CAP + 24, NE, tabf)
        gate = part(3 * CAP + 48, NE, tabf)

        s_x = [sem(f"x_loaded{t}") for t in range(NT)]
        s_const = sem("constants_loaded")
        s_wlr, s_wg = sem("lowrank_weights_loaded"), sem("gate_weights_loaded")
        s_win = [sem(f"projection_slice_loaded{i}") for i in range(2)]
        s_wout = sem("w_out_loaded")
        s_late = sem("late_constants_loaded")
        s_dve, s_act, s_pool = sem("dve_step"), sem("act_step"), sem("pool_step")
        s_ss1, s_var1, s_rt1, s_hn1, s_tr1 = (sem(n) for n in
            ("squares1", "variance1", "root1", "normed1", "transposed1"))
        s_ht_a, s_ht_d = sem("ht_from_act"), sem("ht_from_dve")
        s_unit, s_free_a, s_free_d = sem("unit_in_psum"), sem("unit_copied_by_act"), sem("unit_copied_by_dve")
        s_sq, s_sumq, s_varq, s_rtq, s_swap, s_rope = (sem(n) for n in
            ("squares_qk", "sums_qk", "variance_qk", "root_qk", "swapped_half", "roped"))
        s_tab = sem("rotary_tables_ready")
        s_z, s_zb, s_absz, s_sp, s_cum, s_mid, s_dmid, s_dlast = (sem(n) for n in
            ("gate_logits", "gate_bias_added", "abs_logits", "softplus", "cumsum_done", "mid_last_copied",
             "minus_mid", "last_minus"))
        s_e1, s_e3, s_e4, s_dec = sem("exp_mid"), sem("exp_cum"), sem("exp_last"), sem("decay_ready")
        s_qt, s_qh, s_kh = sem("scores_factors"), sem("inter_queries"), sem("state_keys")
        s_kt, s_ktc, s_sc, s_pred, s_u, s_st, s_o, s_oc = (sem(n) for n in
            ("keys_turned", "keys_copied", "gla_scores", "gla_masked", "state_updates", "states_done",
             "gla_out", "gla_out_copied"))
        s_s, s_mx, s_p, s_w, s_wt, s_wtc, s_pv, s_pvc = (sem(n) for n in
            ("scores", "row_max", "exps", "weights_mixed", "weights_turned", "weights_copied", "attn_out",
             "attn_out_copied"))
        s_c, s_cm = sem("mix_factor"), sem("second_map_scaled")
        s_ego, s_vare, s_rte, s_mix = sem("exp_gate"), sem("variance_heads"), sem("root_heads"), sem("mixed")
        s_mt, s_mta, s_mtd, s_op, s_x1 = (sem(n) for n in
            ("mix_turned", "mixT_from_act", "mixT_from_dve", "out_projected", "residual_added"))
        s_ss2, s_var2, s_rt2, s_hn2, s_tr2, s_h2a, s_h2d = (sem(n) for n in
            ("squares2", "variance2", "root2", "normed2", "h2_turned", "h2T_from_act",
             "h2T_from_dve"))
        s_h2w = [sem(f"h2_stored{b}") for b in range(2)]
        s_lg, s_lmx, s_lex, s_aff, s_afT, s_afc = (sem(n) for n in
            ("router_logits", "router_max", "router_exp", "affinity", "affinity_turned", "affinity_copied"))
        s_top, s_topT, s_route = sem("top_ready"), sem("top_turned"), sem("routes_ready")
        s_lamd, s_lame = sem("lambda_dots"), sem("lambda_exps")
        s_land = [sem(f"weight_tile_landed{i}") for i in range(RAW)]
        s_wh, s_wl, s_used = sem("tile_high_part"), sem("tile_low_part"), sem("tile_used")
        s_icol, s_gat, s_xtp, s_xth, s_xtl = (sem(n) for n in
            ("index_column", "rows_gathered", "rows_turned", "xT_high", "xT_low"))
        s_silu, s_hid, s_hT, s_gth, s_gtl = (sem(n) for n in
            ("silu_of_gate", "hidden_ready", "hidden_turned", "hiddenT_high", "hiddenT_low"))
        s_yh, s_yl, s_sel, s_scat, s_acc = (sem(n) for n in
            ("y_high", "y_low", "selection_ready", "scattered", "accumulated"))
        s_out = sem("output_stored")

        UNITS = tile_plan()
        NCONST = 20

        def slice_end(n):
            mine = [u for u, (kind, s, t) in enumerate(UNITS)
                    if (0 if kind == "qk" else s + 1 if kind == "dqk" else s if kind == "tok" else -1) == n]
            return mine[-1] + 1

        def freed_count(u):
            who = evacuated_by(UNITS[u][0])
            n = sum(evacuated_by(k[0]) == who for k in UNITS[:u + 1])
            return (s_free_d if who == "dve" else s_free_a), n

        n_free_a = sum(evacuated_by(k[0]) == "act" for k in UNITS)
        n_free_d = len(UNITS) - n_free_a

        TILES = weight_plan()
        NTI = len(TILES)
        assert NTI % RAW == 0 and NTI % CONV == 0
        place = {t: n for n, t in enumerate(TILES)}

        def tile_used(i, kind, q):
            return s_used, NTI * i + (place[kind, q, 1] + 1)

        ATT = [(g, h, t) for g in range(2) for t in range(GROUPS[g][1]) for h in range(HEADS)]

        block = ctx.enter_context(nc.Block())

        @block.sync
        def _(sp):
            for t in range(NT):
                src = a["x_prompt"][0] if t < 2 else a["x_sample"][0]
                r = t if t < 2 else t - 2
                sp.dma_start(X[:, t, :], src[r * P:(r + 1) * P, :]).then_inc(s_x[t], 16)

            def load_slice(n):
                if n >= 2:
                    sp.wait_ge(s_unit, slice_end(n - 2))
                sp.dma_start(W[n % 2], a["w_in"][0][:, SLICES[n]:SLICES[n] + SL]
                             .rearrange("(k p) n -> p k n", p=P)).then_inc(s_win[n % 2], 16)

            load_slice(0)
            sp.dma_start(wlr[:], a["w_in"][0][:, C_LR:C_LR + 2 * RANK]
                         .rearrange("(k p) n -> p k n", p=P)).then_inc(s_wlr, 16)
            for n in range(1, len(SLICES)):
                load_slice(n)
            sp.wait_ge(s_o, 2 * HEADS)
            for f in range(2):
                sp.dma_start(W[f], a["w_out"][0][:, f * SL:(f + 1) * SL]
                             .rearrange("(k p) n -> p k n", p=P)).then_inc(s_wout, 16)
            sp.wait_ge(s_hn1, NT)
            sp.dma_start(gnorm[:], a["norm2_g"][0:1, :].broadcast_to([P, D])).then_inc(s_late, 16)
            sp.wait_ge(s_cum, HEADS)
            sp.dma_start(iota, a["iota"]).then_inc(s_late, 16)

            def load_tile(i, n):
                kind, q, part_ = TILES[n]
                e, s = 2 * i + q // NS, q % NS
                rows, cols = (slice(s * FS + part_ * 256, s * FS + part_ * 256 + 256), slice(0, D)) \
                    if kind == "d" else (slice(part_ * 512, part_ * 512 + 512), slice(s * FS, (s + 1) * FS))
                w = a[{"g": "w_gate", "u": "w_up", "d": "w_down"}[kind]][0]
                src = w[e, rows, cols] if isinstance(e, int) else \
                    w[bass.ds(e, 1), rows, cols].rearrange("a r c -> (a r) c")
                sp.dma_start(raw[:, n % RAW, :].rearrange("p (k c) -> p k c", k=2 if kind == "d" else 4),
                             src.rearrange("(k p) c -> p k c", p=P)).then_inc(s_land[n % RAW], 16)

            for t in range(NT):
                if t == NT - 2:
                    sp.wait_ge(s_mt, 2 * NT)
                    for n in range(RAW):
                        load_tile(0, n)
                sp.wait_ge(s_hn2, t + 1)
                sp.dma_start(h2_dram[t * P:(t + 1) * P, :], hn[:, t % 2, :]).then_inc(s_h2w[t % 2], 16)
            with sp.Fori(0, NPAIR - 1) as i:
                for n in range(RAW, NTI + RAW):
                    sp.wait_ge(s_wl, i * NTI + (n - RAW + 1))
                    load_tile(i if n < NTI else i + 1, n % NTI)
            for n in range(RAW, NTI):
                sp.wait_ge(s_wl, (NPAIR - 1) * NTI + n - RAW + 1)
                load_tile(NPAIR - 1, n)
            for t in range(NT):
                sp.wait_ge(s_acc, NPAIR * 2 * NT - (2 * NT) + 2 * (t + 1))
                dst = y_prompt[0] if t < 2 else y_sample[0]
                r = t if t < 2 else t - 2
                sp.dma_start(dst[r * P:(r + 1) * P, :], X[:, t, :]).then_inc(s_out, 16)
            sp.wait_ge(s_out, 16 * NT)
            for b in range(2):
                sp.wait_ge(s_h2w[b], 16 * (NT // 2))

        @block.gpsimd
        def _(pool):
            ch = Chain(pool, s_pool)
            ch.link(pool.memset(wg[:], 0.0))
            pool.dma_start(wg[0:RANK, :, 0:DK], a["gla_wg_f"][0].rearrange("r (h d) -> r h d", h=HEADS))\
                .then_inc(s_wg, 16)
            pool.dma_start(wg[RANK:2 * RANK, :, DK:P], a["gla_wg_b"][0].rearrange("r (h d) -> r h d", h=HEADS))\
                .then_inc(s_wg, 16)

            pool.wait_ge(s_tab, 4)
            for v in range(2 * NT):
                s, t = v // NT, v % NT
                pos = t if t < 2 else t - 2
                y3 = yr[v % 2].rearrange("p (m c) -> p m c", m=8)
                o3 = t2[v % 2].rearrange("p (m c) -> p m c", m=8)
                B = tabs[:, 2 * s + 1, pos, :]
                pool.wait_ge(s_free_d, v + 1)
                if v >= 2:
                    pool.wait_ge(s_rope, v - 1)
                for lo, hi in ((0, 32), (32, 0)):
                    pool.tensor_tensor(o3[:, :, lo:lo + 32], y3[:, :, hi:hi + 32],
                                       B[:, lo:lo + 32].unsqueeze(1).broadcast_to([P, 8, 32]),
                                       ALU.mult).then_inc(s_swap, 1)

            for h in range(HEADS):
                pool.wait_ge(s_mid, h + 1)
                if h >= 1:
                    pool.wait_ge(s_e4, h)
                pool.tensor_tensor(zT2.rearrange("p (n c) -> p n c", n=NCH),
                                   blast.unsqueeze(2).broadcast_to([P, NCH, CHUNK]),
                                   cum.rearrange("p (n c) -> p n c", n=NCH), ALU.subtract).then_inc(s_dlast, 1)
                pool.wait_ge(s_e3, h + 1)
                pool.tensor_tensor(qhat[h % 2], qhat[h % 2], Q[:, h, :], ALU.mult).then_inc(s_qh, 1)
                pool.wait_ge(s_e4, h + 1)
                pool.tensor_tensor(khat[h % 2], khat[h % 2], K[:, h, :], ALU.mult).then_inc(s_kh, 1)

            def gather(n):
                pool.wait_ge(s_icol, n)
                pool.nop(nofuse=True)
                pool.indirect_dma_start(out=XE[0:CAP, :], out_offset=None, in_=h2_dram,
                                        in_offset=bass.IndirectOffsetOnAxis(ap=idx_col[0:CAP, 0:1], axis=0))\
                    .then_inc(s_gat, 16)
            for b in range(2):
                pool.wait_ge(s_h2w[b], 16 * (NT // 2))
            gather(1)
            with pool.Fori(0, NPAIR - 1) as i:
                for j in range(2):
                    gather(2 * i + (j + 2))
            gather(NE)

        @block.tensor
        def _(pe):
            def bank(b):
                return ps[:, b, :]

            pe.wait_ge(s_const, 16 * NCONST)
            for t in range(NT):
                pe.wait_ge(s_hn1, t + 1)
                if t >= 2:
                    pe.wait_ge(s_ht_a, t - 1)
                    pe.wait_ge(s_ht_d, t - 1)
                for k in range(KD):
                    mm = pe.transpose(ps[:, 2 * (t % 2) + k // 4, (k % 4) * P:(k % 4 + 1) * P],
                                      hn[:, t % 2, k * P:(k + 1) * P], ident[:])
                    if k % 4 == 3:
                        mm.then_inc(s_tr1, 1)
            pe.wait_ge(s_ht_a, NT)
            pe.wait_ge(s_ht_d, NT)

            for u, (kind, s, t) in enumerate(UNITS):
                b = u % 8
                if u >= 8:
                    pe.wait_ge(*freed_count(u - 8))
                if kind == "qk":
                    if s == 0 and t == 0:
                        pe.wait_ge(s_win[0], 16)
                    t0, n = (0, T_PROMPT) if t == 0 else (T_PROMPT, T_SAMPLE)
                    for k in range(KD):
                        mm = pe.matmul(ps[:, b, 0:n], W[0][:, k, s * P:(s + 1) * P], HT[:, k, t0:t0 + n],
                                       start=(k == 0), stop=(k == KD - 1))
                    mm.then_inc(s_unit, 1)
                elif kind == "lr":
                    if t == 0:
                        pe.wait_ge(s_wlr, 16)
                    t0, n = (0, T_PROMPT) if t == 0 else (T_PROMPT, T_SAMPLE)
                    for k in range(KD):
                        mm = pe.matmul(ps[0:2 * RANK, b, 0:n], wlr[:, k, :], HT[:, k, t0:t0 + n],
                                       start=(k == 0), stop=(k == KD - 1))
                    mm.then_inc(s_unit, 1)
                elif kind == "rope":
                    v = s * NT + t
                    pe.wait_ge(s_rope, v + 1)
                    for h in range(HEADS):
                        mm = pe.transpose(ps[:, b, h * P:(h + 1) * P], t1[v % 2][:, h * P:(h + 1) * P], ident[:])
                    mm.then_inc(s_unit, 1)
                else:
                    n = s + 1 if kind == "dqk" else s
                    if t == 0:
                        pe.wait_ge(s_win[n % 2], 16 * (n // 2 + 1))
                    for k in range(KD):
                        mm = pe.matmul(bank(b), HT[:, k, t * P:(t + 1) * P], W[n % 2][:, k, :],
                                       start=(k == 0), stop=(k == KD - 1))
                    mm.then_inc(s_unit, 1)

            pe.wait_ge(s_free_a, n_free_a)
            pe.wait_ge(s_free_d, n_free_d)
            pe.wait_ge(s_wg, 32)
            def gate_logits(h):
                if h >= 1:
                    pe.wait_ge(s_zb, 2 * h)
                for g, (t0, n) in enumerate(GROUPS):
                    pe.matmul(ps[:, g, 0:n * P], wg[:, h, :], lrT[:, t0 * P:(t0 + n) * P],
                              start=True, stop=True).then_inc(s_z, 1)

            gate_logits(0)
            for h in range(HEADS):
                b = h % 2
                if h + 1 < HEADS:
                    gate_logits(h + 1)

                def scores(g):
                    t0, n = GROUPS[g]
                    if 2 * h + g >= 1:
                        pe.wait_ge(s_pred, 2 * h + g)
                    for d in range(2):
                        for t in range(n):
                            c = slice((t0 + t) * P, (t0 + t + 1) * P)
                            mm = pe.matmul(ps[:, 2 + d, t * P:(t + 1) * P], ktil[b][d * DK:(d + 1) * DK, c],
                                           qtil[b][d * DK:(d + 1) * DK, c], start=True, stop=True)
                    mm.then_inc(s_sc, 1)

                def updates(g):
                    t0, n = GROUPS[g]
                    pe.wait_ge(s_ktc, 2 * h + g + 1)
                    if 2 * h + g >= 1:
                        pe.wait_ge(s_st, 2 * h + g)
                    for odd in range(2):
                        r = slice(odd * CHUNK, (odd + 1) * CHUNK)
                        for t in range(n):
                            mm = pe.matmul(ps[:, 6 + odd, t * P:(t + 1) * P], khT[b][r, t0 + t, :],
                                           V[r, t0 + t, h * DV:(h + 1) * DV], start=True, stop=True)
                    mm.then_inc(s_u, 1)

                def outputs(g):
                    t0, n = GROUPS[g]
                    pe.wait_ge(s_pred, 2 * h + g + 1)
                    pe.wait_ge(s_st, 2 * h + g + 1)
                    pe.wait_ge(s_qh, h + 1)
                    for t in range(n):
                        o = ps[:, 4 + g, t * P:(t + 1) * P]
                        pe.matmul(o, Ssb[b][:, t0 + t, :], V[:, t0 + t, h * DV:(h + 1) * DV],
                                  start=(t == 0), stop=False, skip_group_check=True)
                        for odd in range(2):
                            c = 2 * (t0 + t) + odd
                            mm = pe.matmul(ps[odd * CHUNK:(odd + 1) * CHUNK, 4 + g, t * P:(t + 1) * P],
                                           qhat[b][:, c * CHUNK:(c + 1) * CHUNK], states[b][:, c, :],
                                           start=False, stop=True, skip_group_check=True)
                    mm.then_inc(s_o, 1)

                pe.wait_ge(s_qt, 2 * (h + 1))
                scores(0)
                pe.wait_ge(s_kh, h + 1)
                for g, (t0, n) in enumerate(GROUPS):
                    if h >= 1:
                        pe.wait_ge(s_oc, 2 * (h - 1) + g + 1)
                    for t in range(n):
                        mm = pe.transpose(ps[:, 4 + g, t * P:(t + 1) * P],
                                          khat[b][:, (t0 + t) * P:(t0 + t + 1) * P], ident[:])
                    mm.then_inc(s_kt, 1)
                updates(0)
                scores(1)
                updates(1)
                outputs(0)
                outputs(1)

            pe.wait_ge(s_oc, 2 * HEADS)
            for i in range(len(ATT) + 3):
                if i < len(ATT):
                    g, h, t = ATT[i]
                    t0, n = GROUPS[g]
                    if i >= 3:
                        pe.wait_ge(s_p, 2 * (i - 2))
                    for m in range(2):
                        r = slice(m * DK, (m + 1) * DK)
                        mm = pe.matmul(ps[:, 2 * (i % 3) + m, 0:n * P],
                                       QT[r, h, (t0 + t) * P:(t0 + t + 1) * P],
                                       KT[r, h, t0 * P:(t0 + n) * P], start=True, stop=True)
                    mm.then_inc(s_s, 1)
                if 2 <= i < len(ATT) + 2:
                    v = i - 2
                    n = GROUPS[ATT[v][0]][1]
                    pe.wait_ge(s_w, v + 1)
                    if v >= 1:
                        pe.wait_ge(s_wtc, v)
                    for k in range(n):
                        mm = pe.transpose(ps[:, 6, k * P:(k + 1) * P],
                                          wmix[v % 2][:, k * P:(k + 1) * P], ident[:])
                    mm.then_inc(s_wt, 1)
                if i >= 3:
                    v = i - 3
                    g, h, t = ATT[v]
                    t0, n = GROUPS[g]
                    pe.wait_ge(s_wtc, v + 1)
                    if v >= 1:
                        pe.wait_ge(s_pvc, v)
                    for k in range(n):
                        mm = pe.matmul(ps[:, 7, 0:DV], wT[v % 2][:, k, :],
                                       VD[:, t0 + k, h * DV:(h + 1) * DV], start=(k == 0), stop=(k == n - 1))
                    mm.then_inc(s_pv, 1)

            def turn(src, b0, done):
                for k in range(KD):
                    mm = pe.transpose(ps[:, b0 + k // 4, (k % 4) * P:(k % 4 + 1) * P], src(k), ident[:])
                    if k % 4 == 3:
                        mm.then_inc(done, 1)

            for t in range(NT + 3):
                if t < NT:
                    pe.wait_ge(s_mix, 2 * t + 2)
                    if t >= 1:
                        pe.wait_ge(s_mta, t)
                        pe.wait_ge(s_mtd, t)
                    turn(lambda k: (OA if k < 4 else OD)[:, t, (k % 4) * P:(k % 4 + 1) * P], 0, s_mt)
                if 1 <= t <= NT:
                    v = t - 1
                    if v == 0:
                        pe.wait_ge(s_wout, 32)
                        pe.wait_ge(s_pvc, len(ATT))
                        pe.wait_ge(s_wtc, len(ATT))
                    pe.wait_ge(s_mta, v + 1)
                    pe.wait_ge(s_mtd, v + 1)
                    for f in range(2):
                        u = 2 * v + f
                        if u >= 3:
                            pe.wait_ge(s_x1, u - 2)
                        for k in range(KD):
                            mm = pe.matmul(ps[:, 4 + u % 3, :], HT[:, k, v * P:(v + 1) * P], W[f][:, k, :],
                                           start=(k == 0), stop=(k == KD - 1))
                        mm.then_inc(s_op, 1)
                if 2 <= t <= NT + 1:
                    v = t - 2
                    pe.wait_ge(s_hn2, v + 1)
                    if v >= 1:
                        pe.wait_ge(s_h2a, v)
                        pe.wait_ge(s_h2d, v)
                    turn(lambda k: hn[:, v % 2, k * P:(k + 1) * P], 2, s_tr2)
                if t >= 3:
                    v = t - 3
                    pe.wait_ge(s_h2a, v + 1)
                    pe.wait_ge(s_h2d, v + 1)
                    for k in range(KD):
                        mm = pe.matmul(ps[:, 7, v * NE:(v + 1) * NE], h2T[v % 2][:, k, :], wr[:, k, :],
                                       start=(k == 0), stop=(k == KD - 1))
                    mm.then_inc(s_lg, 1)
            pe.wait_ge(s_aff, 1)
            for t in range(NT):
                mm = pe.transpose(ps[0:NE, 4 + t // 4, (t % 4) * P:(t % 4 + 1) * P],
                                  st[:, 64 + NE * t:64 + NE * (t + 1)], ident[:])
            mm.then_inc(s_afT, 1)
            pe.wait_ge(s_top, 1)
            pe.transpose(ps[0:CAP, 0, 0:NE], topf, ident[0:NE, 0:NE])
            pe.transpose(ps[0:CAP, 0, 32:32 + NE], topv, ident[0:NE, 0:NE]).then_inc(s_topT, 1)
            pe.wait_ge(s_route, 1)

            def turn_rows(e, half, after):
                if half == 0:
                    pe.wait_ge(s_gat, 16 * (e + 1))
                else:
                    pe.wait_ge(s_xtl, 2 * e + 1)
                for k in range(4 * half, 4 * half + 4):
                    mm = pe.transpose(ps[:, 7, (k % 4) * CAP:(k % 4 + 1) * CAP],
                                      XE[0:CAP, k * P:(k + 1) * P], ident[0:CAP, 0:CAP])
                mm.then_inc(s_xtp, 1)

            def products(out, parts, rhs_h, rhs_l, first, last):
                hi, lo = parts
                pe.matmul(out, hi, rhs_h, start=first, stop=False)
                pe.matmul(out, lo, rhs_h, start=False, stop=False)
                return pe.matmul(out, hi, rhs_l, start=False, stop=last)

            def use_tile(i, n):
                kind, q, part_ = TILES[n]
                c = n % CONV
                pe.wait_ge(s_wl, i * NTI + (n + 1))
                if kind in "gu":
                    h_, l_ = (w[:, c, :].rearrange("p (k f) -> p k f", k=4) for w in (wh, wl))
                    b = (0 if kind == "g" else 2) + q % 2
                    j = q // NS
                    for k in range(4):
                        kk = 4 * part_ + k
                        mm = products(ps[0:CAP, b, :], (XTh[j][:, kk, :], XTl[j][:, kk, :]),
                                      h_[:, k, :], l_[:, k, :], kk == 0, kk == KD - 1)
                else:
                    h_, l_ = (w[:, c, :].rearrange("p (f d) -> p f d", f=2) for w in (wh, wl))
                    s = q % NS
                    for f in range(2):
                        ff = 2 * part_ + f
                        for half in range(2):
                            d = slice(half * 512, (half + 1) * 512)
                            mm = products(ps[0:CAP, 4 + half, :], (gTh[:, ff, :], gTl[:, ff, :]),
                                          h_[:, f, d], l_[:, f, d], s == 0 and ff == 0,
                                          s == NS - 1 and ff == FC - 1)
                mm.then_inc(s_used, 1)

            def turn_hidden(i, q):
                pe.wait_ge(s_hid, 8 * i + (q + 1))
                if q >= 1:
                    pe.wait_ge(s_gtl, 8 * i + q)
                for f in range(FC):
                    mm = pe.transpose(ps[:, 6, f * CAP:(f + 1) * CAP], hid[0:CAP, f * P:(f + 1) * P],
                                      ident[0:CAP, 0:CAP])
                mm.then_inc(s_hT, 1)

            def pair(i, last):
                for q in range(2 * NS):
                    if q % NS == 0:
                        pe.wait_ge(s_xtl, 4 * i + 2 * (q // NS) + 2)
                    if q >= 2:
                        pe.wait_ge(s_hid, 8 * i + (q - 1))
                    use_tile(i, place["g", q, 0])
                    use_tile(i, place["g", q, 1])
                    if q >= 1:
                        turn_hidden(i, q - 1)
                    turns = q % NS == 1 and not (last and q > NS)
                    if turns:
                        turn_rows(2 * i + (q // NS + 1), 0, None)
                    use_tile(i, place["u", q, 0])
                    use_tile(i, place["u", q, 1])
                    if turns:
                        turn_rows(2 * i + (q // NS + 1), 1, None)
                    if q >= 1:
                        pe.wait_ge(s_gtl, 8 * i + q)
                        if q == NS + 1:
                            pe.wait_ge(s_yl, 4 * i + 2)
                        use_tile(i, place["d", q - 1, 0])
                        use_tile(i, place["d", q - 1, 1])
                turn_hidden(i, 2 * NS - 1)
                pe.wait_ge(s_gtl, 8 * i + 2 * NS)
                use_tile(i, place["d", 2 * NS - 1, 0])
                use_tile(i, place["d", 2 * NS - 1, 1])
                pe.wait_ge(s_sel, 2 * i + 2)
                pe.wait_ge(s_yl, 4 * i + 4)
                banks = (0, 1, 2, 3, 6, 7)
                for u in range(2 * NT):
                    t, half = u // 2, u % 2
                    if u >= len(banks):
                        pe.wait_ge(s_acc, 2 * NT * i + (u - len(banks) + 1))
                    for j in range(2):
                        for part_ in (Yh, Yl):
                            mm = pe.matmul(ps[:, banks[u % len(banks)], :], sel[j][0:CAP, t * P:(t + 1) * P],
                                           part_[j][0:CAP, half * 512:(half + 1) * 512],
                                           start=(j == 0 and part_ is Yh), stop=(j == 1 and part_ is Yl))
                    mm.then_inc(s_scat, 1)
                pe.wait_ge(s_acc, 2 * NT * i + 2 * NT)

            turn_rows(0, 0, None)
            turn_rows(0, 1, None)
            with pe.Fori(0, NPAIR - 1) as i:
                pair(i, False)
            pair(NPAIR - 1, True)

        @block.scalar
        def _(act):
            ch = Chain(act, s_act)
            n = 0
            for dst, src in (
                (gnorm[:], a["norm1_g"][0:1, :].broadcast_to([P, D])),
                (ident[:], a["ident"]),
                (tabs[:].rearrange("p a b c -> p (a b c)"), a["rot"]),
                (scanm[:], a["scan_mask"]),
                (pmask[:].rearrange("p a b -> p (a b)"), a["pair_mask"]),
                (wr[:], a["w_router"][0].rearrange("(k p) e -> p k e", p=P)),
                (og_gain[:, 0, :], a["gla_norm_g"][0:1, :].broadcast_to([P, DV])),
                (og_gain[:, 1, :], a["diff_norm_g"][0:1, :].broadcast_to([P, DV])),
                (bg[0:DK, :], a["gla_bg_f"][0].rearrange("(h d) -> d h", d=DK)),
                (bg[DK:P, :], a["gla_bg_b"][0].rearrange("(h d) -> d h", d=DK)),
            ):
                with nc.allow_non_contiguous_dma(reason="256 gate biases, one a partition and head"):
                    act.dma_start(dst, src).then_inc(s_const, 16)
                n += 1
            for m, name in enumerate(("lambda_q1", "lambda_k1", "lambda_q2", "lambda_k2")):
                act.dma_start(lamv[:, m, :], a[name][0:1, :].broadcast_to([P, DK])).then_inc(s_const, 16)
                n += 1
            for m, name in ((0, "qk_norm_q"), (2, "qk_norm_k")):
                act.dma_start(gains[:, m, :], a[name][0:1, :].broadcast_to([P, DK])).then_inc(s_const, 16)
                for lo, hi in ((0, 32), (32, 0)):
                    act.dma_start(gains[:, m + 1, lo:lo + 32], a[name][0:1, hi:hi + 32].broadcast_to([P, 32]))\
                        .then_inc(s_const, 16)
                n += 3
            assert n == NCONST
            act.wait_ge(s_lamd, 1)
            act.activation(nlam[:, 2:4], nlam[:, 0:2], ACT.Exp).then_inc(s_lame, 1)
            for t in range(NT + 1):
                if t < NT:
                    act.wait_ge(s_x[t], 16)
                    act.activation(junk1, X[:, t, :], ACT.Square, accum_out=st[:, t:t + 1]).then_inc(s_ss1, 1)
                    act.wait_ge(s_var1, t + 1)
                    act.activation(st[:, 16 + t:17 + t], st[:, 8 + t:9 + t], ACT.Sqrt).then_inc(s_rt1, 1)
                if t >= 1:
                    v = t - 1
                    act.wait_ge(s_tr1, 2 * v + 1)
                    act.copy(HT[:, 0:4, v * P:(v + 1) * P],
                             ps[:, 2 * (v % 2), :].rearrange("p (k c) -> p k c", k=4)).then_inc(s_ht_a, 1)

            for u, (kind, s, t) in enumerate(UNITS):
                b = u % 8
                act.wait_ge(s_unit, u + 1)
                if kind == "qk":
                    t0, n = (0, T_PROMPT) if t == 0 else (T_PROMPT, T_SAMPLE)
                    dst, sc = (Q, DK ** -0.5) if s < 2 else (K, 1.0)
                    for half in range(2):
                        h = 2 * (s % 2) + half
                        src = ps[half * DK:(half + 1) * DK, b, 0:n]
                        act.mul(dst[0:DK, h, t0:t0 + n], src, sc)
                        last = act.mul(dst[DK:P, h, t0:t0 + n], src, sc)
                    last.then_inc(s_free_a, 1)
                elif kind == "lr":
                    t0, n = (0, T_PROMPT) if t == 0 else (T_PROMPT, T_SAMPLE)
                    act.copy(lrT[:, t0:t0 + n], ps[0:2 * RANK, b, 0:n]).then_inc(s_free_a, 1)
                elif kind == "dqk":
                    v = s * NT + t
                    if v >= 2:
                        act.wait_ge(s_sumq, v - 1)
                    act.activation(sq[v % 2], ps[:, b, :], ACT.Square).then_inc(s_sq, 1)
                    act.wait_ge(s_varq, v + 1)
                    act.activation(st[:, 40 + 8 * (v % 2):48 + 8 * (v % 2)],
                                   st[:, 24 + 8 * (v % 2):32 + 8 * (v % 2)], ACT.Sqrt).then_inc(s_rtq, 1)
                elif kind == "rope":
                    dst = QT if s == 0 else KT
                    act.copy(dst[:, :, t * P:(t + 1) * P],
                             ps[:, b, :].rearrange("p (h c) -> p h c", h=HEADS)).then_inc(s_free_a, 1)
                else:
                    dst = {3: V, 4: VD, 5: OG}[s]
                    act.copy(dst[:, t, :], ps[:, b, :]).then_inc(s_free_a, 1)

            def softplus(h):
                act.wait_ge(s_absz, h + 1)
                ch.link(act.activation(zT2, zT2, ACT.Exp, scale=-1.0))
                act.activation(zT2, zT2, ACT.Ln, bias=1.0).then_inc(s_sp, 1)

            def factors(h):
                b = h % 2
                act.wait_ge(s_dmid, h + 1)
                if h >= 2:
                    act.wait_ge(s_sc, 2 * (h - 1))
                act.activation(qtil[b], zT1, ACT.Exp, scale=1.0 / TAU)
                act.activation(ktil[b], zT1, ACT.Exp, scale=-1.0 / TAU).then_inc(s_e1, 1)
                if h >= 2:
                    act.wait_ge(s_o, 2 * (h - 1))
                act.activation(qhat[b], cum, ACT.Exp, scale=1.0 / TAU).then_inc(s_e3, 1)
                act.wait_ge(s_dlast, h + 1)
                if h >= 2:
                    act.wait_ge(s_kt, 2 * (h - 1))
                    act.wait_ge(s_st, 2 * (h - 1))
                act.activation(khat[b], zT2, ACT.Exp, scale=1.0 / TAU).then_inc(s_e4, 1)
                act.activation(decay[b], blast, ACT.Exp, scale=1.0 / TAU).then_inc(s_dec, 1)

            softplus(0)
            factors(0)
            for h in range(HEADS):
                for g, (t0, n) in enumerate(GROUPS):
                    act.wait_ge(s_kt, 2 * h + g + 1)
                    if h >= 2:
                        act.wait_ge(s_u, 2 * (h - 2) + g + 1)
                    act.copy(khT[h % 2][:, t0:t0 + n, :], ps[:, 4 + g, 0:n * P]
                             .rearrange("p (t c) -> p t c", t=n)).then_inc(s_ktc, 1)
                if h + 1 < HEADS:
                    softplus(h + 1)
                    factors(h + 1)
                else:
                    act.wait_ge(s_free_a, n_free_a)
                    act.activation(OG, OG, ACT.Silu).then_inc(s_ego, 1)
                for g, (t0, n) in enumerate(GROUPS):
                    act.wait_ge(s_o, 2 * h + g + 1)
                    act.copy(OA[:, t0:t0 + n, h * DV:(h + 1) * DV], ps[:, 4 + g, 0:n * P]
                             .rearrange("p (t c) -> p t c", t=n)).then_inc(s_oc, 1)

            for i in range(len(ATT) + 3):
                if i < len(ATT):
                    g, h, t = ATT[i]
                    n = GROUPS[g][1] * P
                    act.wait_ge(s_mx, i + 1)
                    if i >= 2:
                        act.wait_ge(s_w, i - 1)
                    for m in range(2):
                        act.activation(prob[i % 2][:, m, 0:n], ps[:, 2 * (i % 3) + m, 0:n], ACT.Exp,
                                       bias=st[:, 56 + 2 * (i % 2) + m:57 + 2 * (i % 2) + m],
                                       accum_out=st[:, 60 + 2 * (i % 2) + m:61 + 2 * (i % 2) + m]).then_inc(s_p, 1)
                if 1 <= i <= len(ATT):
                    v = i - 1
                    n = GROUPS[ATT[v][0]][1] * P
                    b = 2 * (v % 2)
                    act.wait_ge(s_c, v + 1)
                    if v >= 2:
                        act.wait_ge(s_wt, v - 1)
                    act.mul(wmix[v % 2][:, 0:n], prob[v % 2][:, 1, 0:n], st[:, 164 + b:165 + b]).then_inc(s_cm, 1)
                if 2 <= i < len(ATT) + 2:
                    v = i - 2
                    n = GROUPS[ATT[v][0]][1]
                    act.wait_ge(s_wt, v + 1)
                    if v >= 2:
                        act.wait_ge(s_pv, v - 1)
                    act.copy(wT[v % 2][:, 0:n, :], ps[:, 6, 0:n * P]
                             .rearrange("p (t c) -> p t c", t=n)).then_inc(s_wtc, 1)
                if i >= 3:
                    v = i - 3
                    g, h, t = ATT[v]
                    act.wait_ge(s_pv, v + 1)
                    act.copy(OD[:, GROUPS[g][0] + t, h * DV:(h + 1) * DV], ps[:, 7, 0:DV]).then_inc(s_pvc, 1)

            act.wait_ge(s_vare, 1)
            act.activation(st[:, 112:160], st[:, 64:112], ACT.Sqrt).then_inc(s_rte, 1)
            for t in range(NT + 2):
                if t < NT:
                    act.wait_ge(s_mt, 2 * t + 1)
                    act.copy(HT[:, 0:4, t * P:(t + 1) * P],
                             ps[:, 0, :].rearrange("p (k c) -> p k c", k=4)).then_inc(s_mta, 1)
                if 1 <= t <= NT:
                    v = t - 1
                    act.wait_ge(s_x1, 2 * (v + 1))
                    act.activation(junk, X[:, v, :], ACT.Square, accum_out=st[:, v:v + 1]).then_inc(s_ss2, 1)
                    act.wait_ge(s_var2, v + 1)
                    act.activation(st[:, 16 + v:17 + v], st[:, 8 + v:9 + v], ACT.Sqrt).then_inc(s_rt2, 1)
                if t >= 2:
                    v = t - 2
                    act.wait_ge(s_tr2, 2 * v + 1)
                    if v >= 2:
                        act.wait_ge(s_lg, v - 1)
                    act.copy(h2T[v % 2][:, 0:4, :],
                             ps[:, 2, :].rearrange("p (k c) -> p k c", k=4)).then_inc(s_h2a, 1)
            act.wait_ge(s_lmx, 1)
            act.activation(st[:, 64:160], st[:, 64:160], ACT.Exp).then_inc(s_lex, 1)

            def split(i, n):
                act.wait_ge(s_land[n % RAW], i * (16 * NTI // RAW) + 16 * (n // RAW + 1))
                if not (isinstance(i, int) and i == 0 and n < CONV):
                    act.wait_ge(s_used, i * NTI + (n - CONV + 1))
                act.copy(wh[:, n % CONV, :], raw[:, n % RAW, :]).then_inc(s_wh, 1)

            def xt_copy(e, half, j):
                act.wait_ge(s_xtp, 2 * e + (half + 1))
                act.copy(XTh[j][:, 4 * half:4 * half + 4, :],
                         ps[:, 7, 0:4 * CAP].rearrange("p (k c) -> p k c", k=4)).then_inc(s_xth, 1)

            def y_copy(i, j):
                act.wait_ge(s_sel, 2 * i + (j + 1))
                act.wait_ge(*tile_used(i, "d", NS * (j + 1) - 1))
                for half in range(2):
                    act.mul(Yh[j][0:CAP, half * 512:(half + 1) * 512], ps[0:CAP, 4 + half, :],
                            cur[0:CAP, 1:2]).then_inc(s_yh, 1)

            def pair(i, last):
                for n in range(NTI):
                    kind, q, part_ = TILES[n]
                    if part_ == 0 and kind == "u" and q >= 1:
                        act.wait_ge(s_hT, 8 * i + q)
                        act.copy(gTh[:], ps[:, 6, 0:FC * CAP].rearrange("p (f c) -> p f c", f=FC))\
                            .then_inc(s_gth, 1)
                    turns = kind in "ud" and q % NS == (1 if kind == "u" else 0) and part_ == 0 \
                        and (kind == "u" or q % NS == 0) and not (last and q >= NS)
                    if turns:
                        e = 2 * i + (q // NS + 1)
                        xt_copy(e, 0 if kind == "u" else 1, (q // NS + 1) % 2)
                    if n >= 1 and TILES[n - 1][0] == "u" and TILES[n - 1][2] == 1:
                        qq = TILES[n - 1][1]
                        act.wait_ge(*tile_used(i, "u", qq))
                        act.activation(hid[0:CAP], ps[0:CAP, qq % 2, :], ACT.Silu).then_inc(s_silu, 1)
                    if n >= 1 and TILES[n - 1] == ("d", NS - 1, 1):
                        y_copy(i, 0)
                    if n == place["d", 2 * NS - 1, 0]:
                        act.wait_ge(s_hT, 8 * i + 2 * NS)
                        act.copy(gTh[:], ps[:, 6, 0:FC * CAP].rearrange("p (f c) -> p f c", f=FC))\
                            .then_inc(s_gth, 1)
                    if not (last and n + AHEAD >= NTI):
                        split(i, n + AHEAD) if n + AHEAD < NTI else split(i + 1, n + AHEAD - NTI)
                y_copy(i, 1)

            xt_copy(0, 0, 0)
            xt_copy(0, 1, 0)
            for n in range(AHEAD):
                split(0, n)
            with act.Fori(0, NPAIR - 1) as i:
                pair(i, False)
            pair(NPAIR - 1, True)

        @block.vector
        def _(dve):
            ch = Chain(dve, s_dve)
            dve.wait_ge(s_const, 16 * NCONST)
            for s in range(2):
                for ab in range(2):
                    m = 2 * s + ab
                    dve.tensor_tensor(tabs[:, m, :, :], tabs[:, m, :, :],
                                      gains[:, m, :].unsqueeze(1).broadcast_to([P, 4, DK]),
                                      ALU.mult).then_inc(s_tab, 1)
            ch.mark(dve.tensor_tensor_reduce(lamv[:, 0, :], lamv[:, 0, :], lamv[:, 1, :], 1.0, 0.0,
                                             ALU.mult, ALU.add, nlam[:, 0:1]))
            dve.tensor_tensor_reduce(lamv[:, 2, :], lamv[:, 2, :], lamv[:, 3, :], 1.0, 0.0,
                                     ALU.mult, ALU.add, nlam[:, 1:2]).then_inc(s_lamd, 1)
            ch.mark(dve.tensor_scalar(og_gain[:, 1, :], og_gain[:, 1, :], 1.0 - LAM_INIT, None, ALU.mult))
            dve.wait_ge(s_lame, 1)
            ch.link(dve.tensor_tensor(nlam[:, 0:1], nlam[:, 3:4], nlam[:, 2:3], ALU.subtract))
            ch.mark(dve.tensor_scalar(nlam[:, 0:1], nlam[:, 0:1], -LAM_INIT, None, ALU.add))

            for t in range(NT + 1):
                if t < NT:
                    dve.wait_ge(s_ss1, t + 1)
                    dve.tensor_scalar(st[:, 8 + t:9 + t], st[:, t:t + 1], 1.0 / D, EPS, ALU.mult, ALU.add)\
                        .then_inc(s_var1, 1)
                    dve.wait_ge(s_rt1, t + 1)
                    ch.link(dve.reciprocal(st[:, 16 + t:17 + t], st[:, 16 + t:17 + t]))
                    if t >= 2:
                        dve.wait_ge(s_tr1, 2 * (t - 1))
                    dve.scalar_tensor_tensor(hn[:, t % 2, :], X[:, t, :], st[:, 16 + t:17 + t], gnorm[:],
                                             ALU.mult, ALU.mult).then_inc(s_hn1, 1)
                if t >= 1:
                    v = t - 1
                    dve.wait_ge(s_tr1, 2 * v + 2)
                    dve.tensor_copy(HT[:, 4:8, v * P:(v + 1) * P],
                                    ps[:, 2 * (v % 2) + 1, :].rearrange("p (k c) -> p k c", k=4))\
                        .then_inc(s_ht_d, 1)

            def rope_add(v):
                dve.wait_ge(s_swap, 2 * (v + 1))
                dve.tensor_tensor(t1[v % 2], t1[v % 2], t2[v % 2], ALU.add).then_inc(s_rope, 1)

            dve.wait_ge(s_tab, 4)
            for u, (kind, s, t) in enumerate(UNITS):
                if kind != "dqk":
                    continue
                v = s * NT + t
                pos = t if t < 2 else t - 2
                b8 = 8 * (v % 2)
                dve.wait_ge(s_sq, v + 1)
                dve.tensor_reduce(st[:, 24 + b8:32 + b8], sq[v % 2].rearrange("p (m c) -> p m c", m=8),
                                  AX_X, ALU.add).then_inc(s_sumq, 1)
                dve.wait_ge(s_sumq, v + 1)
                dve.tensor_scalar(st[:, 24 + b8:32 + b8], st[:, 24 + b8:32 + b8], 1.0 / DK, EPS,
                                  ALU.mult, ALU.add).then_inc(s_varq, 1)
                if v >= 1:
                    rope_add(v - 1)
                dve.wait_ge(s_rtq, v + 1)
                ch.link(dve.reciprocal(st[:, 40 + b8:48 + b8], st[:, 40 + b8:48 + b8]))
                if v >= 2:
                    dve.wait_ge(s_swap, 2 * (v - 1))
                dve.tensor_tensor(yr[v % 2].rearrange("p (m c) -> p m c", m=8),
                                  ps[:, u % 8, :].rearrange("p (m c) -> p m c", m=8),
                                  st[:, 40 + b8:48 + b8].unsqueeze(2).broadcast_to([P, 8, DK]),
                                  ALU.mult).then_inc(s_free_d, 1)
                dve.wait_ge(s_free_d, v + 1)
                if v >= 2:
                    dve.wait_ge(s_unit, UNITS.index(("rope", (v - 2) // NT, (v - 2) % NT)) + 1)
                ch.link(dve.tensor_tensor(t1[v % 2].rearrange("p (m c) -> p m c", m=8),
                                          yr[v % 2].rearrange("p (m c) -> p m c", m=8),
                                          tabs[:, 2 * s, pos, :].unsqueeze(1).broadcast_to([P, 8, DK]),
                                          ALU.mult))
            rope_add(2 * NT - 1)

            dve.wait_ge(s_z, 1)
            for b in range(2):
                ch.mark(dve.memset(Ssb[b], 0.0))
                ch.link(dve.memset(states[b], 0.0))
            by_chunk = lambda x: x.rearrange("p (n c) -> p n c", n=NCH)

            def logits(h):
                if h >= 1:
                    dve.wait_ge(s_e1, h)
                for g, (t0, n) in enumerate(GROUPS):
                    dve.wait_ge(s_z, 2 * h + g + 1)
                    dve.tensor_scalar(zT1[:, t0 * P:(t0 + n) * P], ps[:, g, 0:n * P], bg[:, h:h + 1], None,
                                      ALU.add).then_inc(s_zb, 1)
                dve.wait_ge(s_zb, 2 * h + 2)
                if h >= 1:
                    dve.wait_ge(s_e4, h)
                dve.scalar_tensor_tensor(zT2, zT1, -1.0, zT1, ALU.mult, ALU.max).then_inc(s_absz, 1)

            def sums(h):
                dve.wait_ge(s_sp, h + 1)
                ch.link(dve.scalar_tensor_tensor(zT2, zT1, 0.0, zT2, ALU.min, ALU.subtract))
                if h >= 1:
                    dve.wait_ge(s_e3, h)
                    dve.wait_ge(s_dlast, h)
                dve.tensor_tensor_scan(cum[0:DK], scanm[0:DK], zT2[0:DK], 0.0, ALU.mult, ALU.add)
                dve.tensor_tensor_scan(cum[DK:P, ::-1], scanm[DK:P, ::-1], zT2[DK:P, ::-1], 0.0,
                                       ALU.mult, ALU.add).then_inc(s_cum, 1)
                dve.wait_ge(s_cum, h + 1)
                if h >= 1:
                    dve.wait_ge(s_dec, h)
                dve.tensor_copy(bmid[0:DK], by_chunk(cum)[0:DK, :, CHUNK // 2 - 1])
                dve.tensor_copy(bmid[DK:P], by_chunk(cum)[DK:P, :, CHUNK // 2])
                dve.tensor_copy(blast[0:DK], by_chunk(cum)[0:DK, :, CHUNK - 1])
                dve.tensor_copy(blast[DK:P], by_chunk(cum)[DK:P, :, 0]).then_inc(s_mid, 1)
                dve.wait_ge(s_mid, h + 1)
                dve.tensor_tensor(by_chunk(zT1), by_chunk(cum), bmid.unsqueeze(2).broadcast_to([P, NCH, CHUNK]),
                                  ALU.subtract).then_inc(s_dmid, 1)

            def score_factors(h):
                dve.wait_ge(s_e1, h + 1)
                dve.tensor_tensor(qtil[h % 2], qtil[h % 2], Q[:, h, :], ALU.mult).then_inc(s_qt, 1)
                dve.tensor_tensor(ktil[h % 2], ktil[h % 2], K[:, h, :], ALU.mult).then_inc(s_qt, 1)

            def mask(h, g):
                t0, n = GROUPS[g]
                dve.wait_ge(s_sc, 2 * h + g + 1)
                if h >= 2:
                    dve.wait_ge(s_o, 2 * (h - 2) + g + 1)
                for d in range(2):
                    last = dve.copy_predicated(Ssb[h % 2][:, t0:t0 + n, :],
                                               pmask[:, d, :].unsqueeze(1).broadcast_to([P, n, P]),
                                               ps[:, 2 + d, 0:n * P].rearrange("p (t c) -> p t c", t=n))
                    if d == 0:
                        ch.link(last)
                last.then_inc(s_pred, 1)

            def carry(h, g):
                t0, n = GROUPS[g]
                b = h % 2
                dve.wait_ge(s_u, 2 * h + g + 1)
                dve.wait_ge(s_dec, h + 1)
                if h >= 2:
                    dve.wait_ge(s_o, 2 * (h - 2) + g + 1)
                c0, nc_ = 2 * t0, 2 * n
                for m in range(nc_ - 1):
                    for d, c, nxt in ((0, c0 + m, c0 + m + 1), (1, c0 + nc_ - 1 - m, c0 + nc_ - 2 - m)):
                        r = slice(d * DK, (d + 1) * DK)
                        t = c // 2 - t0
                        last = dve.scalar_tensor_tensor(states[b][r, nxt, :], states[b][r, c, :],
                                                        decay[b][r, c:c + 1],
                                                        ps[r, 6 + c % 2, t * P:(t + 1) * P], ALU.mult, ALU.add)
                    if m < nc_ - 2:
                        ch.link(last)
                last.then_inc(s_st, 1)

            logits(0)
            sums(0)
            score_factors(0)
            for h in range(HEADS):
                more = h + 1 < HEADS
                if more:
                    logits(h + 1)
                mask(h, 0)
                if more:
                    sums(h + 1)
                carry(h, 0)
                mask(h, 1)
                if more:
                    score_factors(h + 1)
                carry(h, 1)

            hsums = st[:, 64:112].rearrange("p (t m) -> p t m", t=NT)
            roots = st[:, 112:160].rearrange("p (t m) -> p t m", t=NT)
            heads = lambda x: x.rearrange("p (h c) -> p h c", h=HEADS)

            def head_squares(o_, m, t):
                ch.link(dve.tensor_tensor(square[m], o_[:, t, :], o_[:, t, :], ALU.mult))

            def head_sums(o_, m, t):
                ch.mark(dve.tensor_reduce(hsums[:, t, 4 * m:4 * m + 4], heads(square[m]), AX_X, ALU.add))

            def head_gain(o_, m, t):
                ch.mark(dve.tensor_tensor(heads(o_[:, t, :]), heads(o_[:, t, :]),
                                          og_gain[:, m, :].unsqueeze(1).broadcast_to([P, HEADS, DV]), ALU.mult))

            def head_gate(t):
                ch.own()
                ch.mark(dve.tensor_tensor(OA[:, t, :], OA[:, t, :], OG[:, t, :], ALU.mult))

            def beside(i):
                if i == 0:
                    dve.wait_ge(s_oc, 2 * HEADS)
                    dve.wait_ge(s_ego, 1)
                if i < 4 * NT:
                    t = i // 4
                    ch.own()
                    (head_squares, head_sums, head_gain, lambda o_, m, t: head_gate(t))[i % 4](OA, 0, t)
                if i >= 7 and (i - 7) % 4 == 0 and (i - 7) // 4 < NT:
                    t = (i - 7) // 4
                    dve.wait_ge(s_pvc, 4 * (t + 1))
                    head_squares(OD, 1, t)
                    head_sums(OD, 1, t)
                    head_gain(OD, 1, t)

            for i in range(len(ATT) + 1):
                if i < len(ATT):
                    n = GROUPS[ATT[i][0]][1] * P
                    b, b3 = 2 * (i % 2), 2 * (i % 3)
                    dve.wait_ge(s_s, i + 1)
                    if i >= 2:
                        dve.wait_ge(s_p, 2 * (i - 1))
                    dve.tensor_reduce(st[:, 56 + b:58 + b], ps[:, b3:b3 + 2, 0:n], AX_X, ALU.max, negate=True)\
                        .then_inc(s_mx, 1)
                if i >= 1:
                    v = i - 1
                    n = GROUPS[ATT[v][0]][1] * P
                    b = 2 * (v % 2)
                    dve.wait_ge(s_p, 2 * v + 2)
                    ch.link(dve.reciprocal(st[:, 160 + b:162 + b], st[:, 60 + b:62 + b]))
                    dve.tensor_tensor(st[:, 164 + b:165 + b], st[:, 161 + b:162 + b], nlam[:, 0:1],
                                      ALU.mult).then_inc(s_c, 1)
                    beside(v)
                    dve.wait_ge(s_cm, v + 1)
                    dve.scalar_tensor_tensor(wmix[v % 2][:, 0:n], prob[v % 2][:, 0, 0:n],
                                             st[:, 160 + b:161 + b], wmix[v % 2][:, 0:n],
                                             ALU.mult, ALU.add).then_inc(s_w, 1)
            beside(4 * NT + 3)
            ch.own()
            dve.tensor_scalar(st[:, 64:112], st[:, 64:112], 1.0 / DV, EPS, ALU.mult, ALU.add).then_inc(s_vare, 1)
            dve.wait_ge(s_rte, 1)
            ch.link(dve.reciprocal(st[:, 112:160], st[:, 112:160]))

            def scale_heads(t):
                for m, o_ in enumerate((OA, OD)):
                    dve.tensor_tensor(heads(o_[:, t, :]), heads(o_[:, t, :]),
                                      roots[:, t, 4 * m:4 * m + 4].unsqueeze(2).broadcast_to([P, HEADS, DV]),
                                      ALU.mult).then_inc(s_mix, 1)

            scale_heads(0)
            for t in range(NT + 2):
                if t + 1 < NT:
                    scale_heads(t + 1)
                if t < NT:
                    dve.wait_ge(s_mt, 2 * t + 2)
                    dve.tensor_copy(HT[:, 4:8, t * P:(t + 1) * P],
                                    ps[:, 1, :].rearrange("p (k c) -> p k c", k=4)).then_inc(s_mtd, 1)
                if 1 <= t <= NT:
                    v = t - 1
                    for f in range(2):
                        u = 2 * v + f
                        dve.wait_ge(s_op, u + 1)
                        x = X[:, v, f * 512:(f + 1) * 512]
                        dve.tensor_tensor(x, x, ps[:, 4 + u % 3, :], ALU.add).then_inc(s_x1, 1)
                    dve.wait_ge(s_ss2, v + 1)
                    dve.tensor_scalar(st[:, 8 + v:9 + v], st[:, v:v + 1], 1.0 / D, EPS, ALU.mult, ALU.add)\
                        .then_inc(s_var2, 1)
                    dve.wait_ge(s_rt2, v + 1)
                    ch.link(dve.reciprocal(st[:, 16 + v:17 + v], st[:, 16 + v:17 + v]))
                    if v == 0:
                        dve.wait_ge(s_late, 32)
                    if v >= 2:
                        dve.wait_ge(s_h2w[v % 2], 16 * (v // 2))
                        dve.wait_ge(s_tr2, 2 * (v - 1))
                    dve.scalar_tensor_tensor(hn[:, v % 2, :], X[:, v, :], st[:, 16 + v:17 + v], gnorm[:],
                                             ALU.mult, ALU.mult).then_inc(s_hn2, 1)
                if t >= 2:
                    v = t - 2
                    dve.wait_ge(s_tr2, 2 * v + 2)
                    if v >= 2:
                        dve.wait_ge(s_lg, v - 1)
                    dve.tensor_copy(h2T[v % 2][:, 4:8, :],
                                    ps[:, 3, :].rearrange("p (k c) -> p k c", k=4)).then_inc(s_h2d, 1)

            aff_tok = st[:, 64:160].rearrange("p (t e) -> p t e", t=NT)
            logit = ps[:, 7, 0:NT * NE].rearrange("p (t e) -> p t e", t=NT)
            stat = st[:, 24:24 + NT]
            dve.wait_ge(s_lg, NT)
            ch.link(dve.tensor_reduce(stat, logit, AX_X, ALU.max))
            dve.tensor_tensor(aff_tok, logit, stat.unsqueeze(2).broadcast_to([P, NT, NE]), ALU.subtract)\
                .then_inc(s_lmx, 1)
            dve.wait_ge(s_lex, 1)
            ch.link(dve.tensor_reduce(stat, aff_tok, AX_X, ALU.add))
            ch.link(dve.reciprocal(stat, stat))
            dve.tensor_tensor(aff_tok, aff_tok, stat.unsqueeze(2).broadcast_to([P, NT, NE]), ALU.mult)\
                .then_inc(s_aff, 1)
            dve.wait_ge(s_afT, 1)
            dve.tensor_copy(aff[:, 0:4 * P], ps[0:NE, 4, :]).then_inc(s_afc, 1)
            dve.tensor_copy(aff[:, 4 * P:TOK], ps[0:NE, 5, 0:2 * P]).then_inc(s_afc, 1)

            dve.wait_ge(s_afc, 2)
            for lo, n, c0, cap in ((0, T_PROMPT, 0, CAP_P), (T_PROMPT, T_SAMPLE, CAP_P, CAP_S)):
                row = aff[:, lo:lo + n]
                for c in range(c0, c0 + cap, 8):
                    ch.link(dve.max(topv[:, c:c + 8], row))
                    ch.link(dve.max_index(topi[:, c:c + 8], topv[:, c:c + 8], row))
                    ch.link(dve.match_replace(row, topv[:, c:c + 8], row, -1.0))
            ch.link(dve.tensor_copy(topf, topi))
            dve.tensor_scalar(topf[:, CAP_P:CAP], topf[:, CAP_P:CAP], float(T_PROMPT), None, ALU.add)\
                .then_inc(s_top, 1)
            dve.wait_ge(s_topT, 1)
            ch.mark(dve.tensor_copy(gidx[0:CAP, 0:NE], ps[0:CAP, 0, 0:NE]))
            ch.mark(dve.tensor_copy(grow[0:CAP, :], ps[0:CAP, 0, 0:NE]))
            dve.tensor_copy(gate[0:CAP, :], ps[0:CAP, 0, 32:32 + NE]).then_inc(s_route, 1)
            dve.wait_ge(s_route, 1)
            dve.tensor_copy(idx_col[0:CAP, 0:1], gidx[0:CAP, 0:1]).then_inc(s_icol, 1)

            def split(i, n):
                dve.wait_ge(s_wh, i * NTI + (n + 1))
                dve.tensor_tensor(wl[:, n % CONV, :], raw[:, n % RAW, :], wh[:, n % CONV, :].bitcast(F32),
                                  ALU.subtract).then_inc(s_wl, 1)

            def xt_copy(e, half, j):
                dve.wait_ge(s_xth, 2 * e + (half + 1))
                dve.tensor_tensor(XTl[j][:, 4 * half:4 * half + 4, :],
                                  ps[:, 7, 0:4 * CAP].rearrange("p (k c) -> p k c", k=4),
                                  XTh[j][:, 4 * half:4 * half + 4, :].bitcast(F32), ALU.subtract).then_inc(s_xtl, 1)

            def y_copy(i, j):
                for half in range(2):
                    c = slice(half * 512, (half + 1) * 512)
                    dve.wait_ge(s_yh, 4 * i + (2 * j + half + 1))
                    dve.scalar_tensor_tensor(Yl[j][0:CAP, c], ps[0:CAP, 4 + half, :], cur[0:CAP, 1:2],
                                             Yh[j][0:CAP, c].bitcast(F32), ALU.mult, ALU.subtract).then_inc(s_yl, 1)

            def next_rows(i, j):
                dve.wait_ge(s_gat, 32 * i + 16 * (j + 1))
                dve.tensor_copy(idx_col[0:CAP, 0:1], gidx[0:CAP, bass.ds(2 * i + (j + 1), 1)])\
                    .then_inc(s_icol, 1)

            def selection(i, j):
                ch.mark(dve.tensor_copy(cur[0:CAP, 0:1], grow[0:CAP, bass.ds(2 * i + j, 1)]))
                ch.link(dve.tensor_copy(cur[0:CAP, 1:2], gate[0:CAP, bass.ds(2 * i + j, 1)]))
                dve.tensor_scalar(sel[j][0:CAP], iota[0:CAP], cur[0:CAP, 0:1], None, ALU.is_equal)\
                    .then_inc(s_sel, 1)

            def pair(i, last):
                for n in range(NTI):
                    kind, q, part_ = TILES[n]
                    if n == 0:
                        next_rows(i, 0)
                        selection(i, 0)
                    if part_ == 0 and kind == "u" and q >= 1:
                        dve.wait_ge(s_gth, 8 * i + q)
                        dve.tensor_tensor(gTl[:], ps[:, 6, 0:FC * CAP].rearrange("p (f c) -> p f c", f=FC),
                                          gTh[:].bitcast(F32), ALU.subtract).then_inc(s_gtl, 1)
                    turns = kind in "ud" and q % NS == (1 if kind == "u" else 0) and part_ == 0 \
                        and (kind == "u" or q % NS == 0) and not (last and q >= NS)
                    if turns:
                        e = 2 * i + (q // NS + 1)
                        xt_copy(e, 0 if kind == "u" else 1, (q // NS + 1) % 2)
                        if kind == "d" and q == 0 and not last:
                            next_rows(i, 1)
                    if n >= 1 and TILES[n - 1][0] == "u" and TILES[n - 1][2] == 1:
                        qq = TILES[n - 1][1]
                        dve.wait_ge(s_silu, 8 * i + (qq + 1))
                        dve.tensor_tensor(hid[0:CAP], hid[0:CAP], ps[0:CAP, 2 + qq % 2, :], ALU.mult)\
                            .then_inc(s_hid, 1)
                    if n >= 1 and TILES[n - 1] == ("d", NS - 1, 1):
                        y_copy(i, 0)
                        dve.wait_ge(s_yl, 4 * i + 2)
                        selection(i, 1)
                    if n == place["d", 2 * NS - 1, 0]:
                        dve.wait_ge(s_gth, 8 * i + 2 * NS)
                        dve.tensor_tensor(gTl[:], ps[:, 6, 0:FC * CAP].rearrange("p (f c) -> p f c", f=FC),
                                          gTh[:].bitcast(F32), ALU.subtract).then_inc(s_gtl, 1)
                    if not (last and n + AHEAD >= NTI):
                        split(i, n + AHEAD) if n + AHEAD < NTI else split(i + 1, n + AHEAD - NTI)
                y_copy(i, 1)
                banks = (0, 1, 2, 3, 6, 7)
                for u in range(2 * NT):
                    dve.wait_ge(s_scat, 2 * NT * i + (u + 1))
                    x = X[:, u // 2, (u % 2) * 512:(u % 2 + 1) * 512]
                    dve.tensor_tensor(x, x, ps[:, banks[u % len(banks)], :], ALU.add).then_inc(s_acc, 1)

            xt_copy(0, 0, 0)
            xt_copy(0, 1, 0)
            for n in range(AHEAD):
                split(0, n)
            steps = 4
            n0 = ch.n
            with dve.Fori(0, NPAIR - 1) as i:
                ch.base = i * steps
                pair(i, False)
            assert ch.n - n0 == steps
            ch.n, ch.base = n0 + (NPAIR - 1) * steps, 0
            pair(NPAIR - 1, True)


_INPUTS = ("x_prompt", "x_sample", "norm1_g", "w_in", "gla_wg_f", "gla_bg_f", "gla_wg_b", "gla_bg_b",
           "gla_norm_g", "qk_norm_q", "qk_norm_k", "lambda_q1", "lambda_k1", "lambda_q2", "lambda_k2",
           "diff_norm_g", "w_out", "norm2_g", "w_router", "w_gate", "w_up", "w_down")


def shape_constants():
    f = np.float32
    inv = np.power(f(10000.0), -np.arange(0, DK, 2, dtype=f) / f(DK)).astype(f)
    ang = np.arange(T_SAMPLE, dtype=f)[:, None] * inv[None, :]
    cos, sin = np.cos(ang).astype(f), np.sin(ang).astype(f)
    A = np.concatenate([cos, cos], 1).reshape(4, P, DK).transpose(1, 0, 2)
    B = np.concatenate([-sin, sin], 1).reshape(4, P, DK).transpose(1, 0, 2)
    sc = f(DK ** -0.5)
    rot = np.stack([A * sc, B * sc, A, B], 1).reshape(P, -1)
    scan = np.ones((P, TOK), f)
    scan[:DK, ::CHUNK] = 0
    scan[DK:, CHUNK - 1::CHUNK] = 0
    key, qry = np.arange(P)[:, None], np.arange(P)[None, :]
    same = (key // CHUNK) == (qry // CHUNK)
    mask = np.concatenate([same & (qry >= key), same & (qry < key)], 1).astype(np.uint32)
    return {"ident": np.eye(P, dtype=f), "rot": np.ascontiguousarray(rot), "scan_mask": scan,
            "pair_mask": mask, "iota": np.broadcast_to(np.arange(TOK, dtype=f), (P, TOK)).copy()}


def kernel(**inputs):
    import concourse.bacc as bacc
    from concourse.bass_utils import run_bass_kernel_spmd

    nc = bacc.Bacc("TRN2", target_bir_lowering=False, num_devices=1)
    arrays, aps = {}, {}
    data = {n: np.ascontiguousarray(inputs[n]) for n in _INPUTS}
    data.update(shape_constants())
    for name, x in data.items():
        arrays[f"in_{name}"] = x
        aps[name] = nc.dram_tensor(f"in_{name}", x.shape, mybir.dt.from_np(x.dtype), kind="ExternalInput").ap()
    y_prompt = nc.dram_tensor("y_prompt", (1, T_PROMPT, D), F32, kind="ExternalOutput").ap()
    y_sample = nc.dram_tensor("y_sample", (1, T_SAMPLE, D), F32, kind="ExternalOutput").ap()
    h2 = nc.dram_tensor("h2_rows", (TOK, D), F32, kind="Internal").ap()
    build(nc, aps, y_prompt, y_sample, h2)
    r = run_bass_kernel_spmd(nc, [arrays], core_ids=[0])
    return r.results[0]["y_prompt"], r.results[0]["y_sample"]
```

```python
from contextlib import ExitStack

import numpy as np

import concourse.bass as bass
from concourse import mybir
from concourse.alu_op_type import AluOpType as ALU

ACT = mybir.ActivationFunctionType
F32 = mybir.dt.float32
F32R = mybir.dt.float32r
U32 = mybir.dt.uint32
AX_X = mybir.AxisListType.X

P = 128
D = 1024
KD = D // P
T_PROMPT, T_SAMPLE = 256, 512
TOK = T_PROMPT + T_SAMPLE
NT = TOK // P
GROUPS = ((0, 2), (2, 4))
HEADS = 4
DK, DV = 64, 128
RANK = 16
CHUNK = 64
NCH = TOK // CHUNK
SL = 512
C_QK, C_V, C_OG, C_LR = 0, 512, 1024, 1536
C_DQ, C_DK, C_DV = 1568, 2080, 2592
SLICES = (C_QK, C_DQ, C_DK, C_V, C_DV, C_OG)
EPS = 1e-6
TAU = 16.0
LAM_INIT = 0.2
NE = 16
FE = 2 * D
CAP_P, CAP_S = 2 * T_PROMPT // NE, 2 * T_SAMPLE // NE
CAP = CAP_P + CAP_S
NPAIR = NE // 2
FS = 512
NS = FE // FS
FC = FS // P
RAW = 8
CONV = 4
AHEAD = 3
TW = 2048


def tile_plan():
    plan = []
    for c in range(4):
        plan += [("qk", c, 0), ("qk", c, 1)]
    plan += [("lr", 0, 0), ("lr", 0, 1)]
    body = [("dqk", s, t) for s in range(2) for t in range(NT)]
    body += [("tok", s, t) for s in range(3, 6) for t in range(NT)]
    lag = 3
    for n, u in enumerate(body):
        plan.append(u)
        if u == ("tok", 4, NT - 1):
            plan += [("gate", 0, 0), ("gate", 0, 1)]
        if n >= lag and n - lag < 2 * NT:
            v = n - lag
            plan.append(("rope", v // NT, v % NT))
    return plan


def evacuated_by(kind):
    return {"dqk": "dve", "gate": "bias"}.get(kind, "act")


def weight_plan():
    order = []
    for q in range(2 * NS):
        order += [("g", q, 0), ("g", q, 1), ("u", q, 0), ("u", q, 1)]
        if q >= 1:
            order += [("d", q - 1, 0), ("d", q - 1, 1)]
    return order + [("d", 2 * NS - 1, 0), ("d", 2 * NS - 1, 1)]


class Chain:

    def __init__(self, eng, sem):
        self.eng, self.sem, self.n, self.base = eng, sem, 0, 0

    def mark(self, ins):
        self.n += 1
        return ins.then_inc(self.sem, 1)

    def own(self):
        self.eng.wait_ge(self.sem, self.base + self.n)

    def link(self, ins):
        self.mark(ins)
        self.own()


def build(nc, a, y_prompt, y_sample, h2_dram):
    ctx = ExitStack()
    with ctx:
        def sb(name, shape, dt=F32):
            return ctx.enter_context(nc.sbuf_tensor(name, shape, dt))

        def sem(name):
            return ctx.enter_context(nc.semaphore(name))

        ps = ctx.enter_context(nc.psum_tensor("ps", [P, 8, 512], F32))

        span = 210304
        sb("whole", [P, span // 4])
        origin = nc.sbuf_base - span

        def at(name, off, shape, dt=F32):
            return nc.alloc_sbuf_tensor_at(name, shape, dt, offset=origin + off)

        ring = at("ring", 0, [P, 8, 4096])
        wh = at("wh", 0, [P, CONV, TW], F32R)
        wl = at("wl", 32768, [P, CONV, TW], F32R)
        raw = at("raw", 65536, [P, RAW, TW])
        X = at("X", 131072, [P, NT, D])
        HT = at("HT", 155648, [P, KD, TOK])
        HTh = at("HTh", 155648, [P, KD, TOK], F32R)
        HTl = at("HTl", 131072, [P, NT, KD, P], F32R)
        MTl = at("MTl", 69632, [P, NT, KD, P], F32R)
        woh0v = at("woh0v", 57344, [P, 6, SL], F32R)
        woh0t = at("woh0t", 192512, [P, 2, SL], F32R)
        woh1 = at("woh1", 94208, [P, KD, SL], F32R)
        wih = at("wih", 0, [P, KD, SL], F32R)
        wil = at("wil", 16384, [P, KD, SL], F32R)
        wil_og = at("wil_og", 81920, [P, 6, SL], F32R)
        wil_oa = at("wil_oa", 118784, [P, 6, SL], F32R)
        wil_gn = at("wil_gn", 188416, [P, 2, SL], F32R)
        wlrh = at("wlrh", 94208, [P, KD, 2 * RANK], F32R)
        wlrl = at("wlrl", 196608, [P, KD, 2 * RANK], F32R)
        Yh = [at(f"Yh{j}", 155648 + 8192 * j, [P, D], F32R) for j in range(2)]
        Yl = [at(f"Yl{j}", 159744 + 8192 * j, [P, D], F32R) for j in range(2)]
        gTh = at("gTh", 172032, [P, FC, CAP], F32R)
        gTl = at("gTl", 173568, [P, FC, CAP], F32R)
        hid = at("hid", 175104, [P, FS])
        XTh = [at("XTh0", 177152, [P, KD, CAP], F32R), at("XTh1", 199680, [P, KD, CAP], F32R)]
        hn = at("hn", 180224, [P, 2, D])
        XE = at("XE", 180224, [P, D])
        sel = [at("sel0", 184320, [P, TOK], F32R), at("sel1", 196608, [P, TOK], F32R)]
        gnorm = at("gnorm", 188416, [P, D])
        XTl = [at("XTl0", 188416, [P, KD, CAP], F32R), at("XTl1", 205824, [P, KD, CAP], F32R)]
        tabs = at("tabs", 192512, [P, 4, 4, DK])
        wlr = at("wlr", 196608, [P, KD, 2 * RANK])
        wg = at("wg", 197632, [2 * RANK, HEADS, P])
        lrT = at("lrT", 199680, [2 * RANK, TOK])
        scanm = at("scanm", 202752, [P, TOK])
        pmask = at("pmask", 205824, [P, 2, P], U32)
        og_gain = at("og_gain", 206848, [P, 2, DV])
        wr = at("wr", 207872, [P, KD, NE])
        ident = at("ident", 208896, [P, P])
        st = at("st", 209408, [P, 192])
        bg = at("bg", 210176, [P, HEADS])
        nlam = at("nlam", 210208, [P, 4])
        idx_col = at("idx_col", 210240, [P, 2], U32)
        cur = at("cur", 210272, [P, 2])

        flat = ring[:].rearrange("p r n -> p (r n)")

        def part(off, n, base=flat):
            return base[:, off:off + n]

        W = [ring[:, s, :].rearrange("p (k n) -> p k n", k=KD) for s in range(2)]
        o = 2 * 4096
        Q = part(o, 3072).rearrange("p (h t) -> p h t", h=HEADS); o += 3072
        K = part(o, 3072).rearrange("p (h t) -> p h t", h=HEADS); o += 3072
        V = part(o, 3072).rearrange("p (t n) -> p t n", t=NT); o += 3072
        VD = part(o, 3072).rearrange("p (t n) -> p t n", t=NT); o += 3072
        OG = part(o, 3072).rearrange("p (t n) -> p t n", t=NT); o += 3072
        QT = part(o, 3072).rearrange("p (h t) -> p h t", h=HEADS); o += 3072
        KT = part(o, 3072).rearrange("p (h t) -> p h t", h=HEADS); o += 3072
        OA = part(o, 3072).rearrange("p (t n) -> p t n", t=NT); o += 3072
        assert o == 8 * 4096
        OD = K.rearrange("p h t -> p (h t)").rearrange("p (t n) -> p t n", t=NT)
        oaf = OA.rearrange("p t n -> p (t n)")
        hnf = hn[:].rearrange("p b n -> p (b n)")
        sq = [part(0, SL, oaf), part(SL, SL, oaf)]
        yr = [part(2 * SL, SL, oaf), part(3 * SL, SL, oaf)]
        t1 = [part(4 * SL, SL, oaf), part(5 * SL, SL, oaf)]
        t2 = [part(0, SL, hnf), part(SL, SL, hnf)]
        gains = OG[:, 0, 0:256].rearrange("p (m d) -> p m d", m=4)
        lamv = OG[:, 0, 256:512].rearrange("p (m d) -> p m d", m=4)
        tabf = tabs[:].rearrange("p a b c -> p (a b c)")
        htf = HT[:].rearrange("p k t -> p (k t)")
        zT1, zT2, cum = (part(4096 + n * TOK, TOK) for n in range(3))
        qtil = [part(4096 + 3 * TOK, TOK), part(0, TOK, htf)]
        ktil = [part(4096 + 4 * TOK, TOK), part(TOK, TOK, htf)]
        qhat = [part(0, TOK, tabf), part(2 * TOK, TOK, htf)]
        khat = [part(2 * D - TOK, TOK, hnf), part(3 * TOK, TOK, htf)]
        khT = [part(0, TOK).rearrange("p (t c) -> p t c", t=NT),
               part(4 * TOK, TOK, htf).rearrange("p (t c) -> p t c", t=NT)]
        states = [part(TOK, NCH * DV).rearrange("p (n e) -> p n e", n=NCH),
                  part(5 * TOK, NCH * DV, htf).rearrange("p (n e) -> p n e", n=NCH)]
        Ssb = [part(0, TOK, hnf).rearrange("p (t c) -> p t c", t=NT),
               part(7 * TOK, TOK, htf).rearrange("p (t c) -> p t c", t=NT)]
        bmid = part(TOK, NCH, hnf)
        blast = part(TOK + NCH, NCH, hnf)
        decay = [part(TOK + (2 + n) * NCH, NCH, hnf) for n in range(2)]
        qf = Q.rearrange("p h t -> p (h t)")
        prob = [part(0, 1024, qf).rearrange("p (m n) -> p m n", m=2),
                part(1024, 1024, qf).rearrange("p (m n) -> p m n", m=2),
                part(0, 1024, htf).rearrange("p (m n) -> p m n", m=2)]
        wmix = [part(2048, 512, qf), part(2560, 512, qf)]
        wT = [part(1024, 512, hnf).rearrange("p (t c) -> p t c", t=4),
              part(1536, 512, hnf).rearrange("p (t c) -> p t c", t=4)]
        square = [part(0, SL, hnf), part(SL, SL, hnf)]
        h2T = [part(n * D, D, qf).rearrange("p (k c) -> p k c", k=KD) for n in range(2)]
        junk = part(2 * D, D, qf)
        junk1 = ring[:, 6, 0:1024]
        iota = scanm[:]
        aff = lrT[0:NE, :]
        topv = part(0, CAP, tabf)[0:NE]
        topf = part(CAP, CAP, tabf)[0:NE]
        topi = part(2 * CAP, CAP, tabf)[0:NE].bitcast(U32)
        gidx = part(3 * CAP, NE + 1, tabf).bitcast(U32)
        grow = part(3 * CAP + 24, NE, tabf)
        gate = part(3 * CAP + 48, NE, tabf)

        def slice_raw(n, k):
            if n % 2 == 0:
                return W[1][:, k, :]
            if k < 6:
                return (OA if n == len(SLICES) - 1 else OG)[:, k, :]
            return gnorm[:, (k - 6) * SL:(k - 5) * SL]

        def slice_low(n, k):
            if n % 2 == 0:
                return wil[:, k, :]
            if k < 6:
                return (wil_oa if n == len(SLICES) - 1 else wil_og)[:, k, :]
            return wil_gn[:, k - 6, :]

        def wout_high(f, k):
            return woh1[:, k, :] if f else woh0v[:, k, :] if k < 6 else woh0t[:, k - 6, :]

        wout_low = (wih, wil)

        s_x = [sem(f"x_loaded{t}") for t in range(NT)]
        s_const = sem("constants_loaded")
        s_wlr, s_wg = sem("lowrank_weights_loaded"), sem("gate_weights_loaded")
        s_win = [sem(f"projection_slice_loaded{i}") for i in range(2)]
        s_wih, s_wil = sem("slice_high_part"), sem("slice_low_part")
        s_lrh, s_lrl = sem("lowrank_high_part"), sem("lowrank_low_part")
        s_wout = sem("w_out_loaded")
        s_woh, s_wol = sem("w_out_high_part"), sem("w_out_low_part")
        s_late = sem("late_constants_loaded")
        s_dve, s_act, s_pool = sem("dve_step"), sem("act_step"), sem("pool_step")
        s_ss1, s_var1, s_rt1, s_hn1, s_tr1 = (sem(n) for n in
            ("squares1", "variance1", "root1", "normed1", "transposed1"))
        s_ht_a, s_ht_d = sem("ht_from_act"), sem("ht_from_dve")
        s_unit, s_free_a, s_free_d = sem("unit_in_psum"), sem("unit_copied_by_act"), sem("unit_copied_by_dve")
        s_sq, s_sumq, s_varq, s_rtq, s_swap, s_rope = (sem(n) for n in
            ("squares_qk", "sums_qk", "variance_qk", "root_qk", "swapped_half", "roped"))
        s_tab = sem("rotary_tables_ready")
        s_z, s_zb, s_absz, s_sp, s_cum, s_mid, s_dmid, s_dlast = (sem(n) for n in
            ("gate_logits", "gate_bias_added", "abs_logits", "softplus", "cumsum_done", "mid_last_copied",
             "minus_mid", "last_minus"))
        s_e1, s_e3, s_e4, s_dec = sem("exp_mid"), sem("exp_cum"), sem("exp_last"), sem("decay_ready")
        s_qt, s_qh, s_kh = sem("scores_factors"), sem("inter_queries"), sem("state_keys")
        s_kt, s_ktc, s_sc, s_pred, s_u, s_st, s_o, s_oc = (sem(n) for n in
            ("keys_turned", "keys_copied", "gla_scores", "gla_masked", "state_updates", "states_done",
             "gla_out", "gla_out_copied"))
        s_s, s_mx, s_p, s_w, s_wt, s_wtc, s_pv, s_pvc = (sem(n) for n in
            ("scores", "row_max", "exps", "weights_mixed", "weights_turned", "weights_copied", "attn_out",
             "attn_out_copied"))
        s_c, s_cm = sem("mix_factor"), sem("second_map_scaled")
        s_ego, s_vare, s_rte, s_mix = sem("exp_gate"), sem("variance_heads"), sem("root_heads"), sem("mixed")
        s_mt, s_mta, s_mtd, s_op, s_x1 = (sem(n) for n in
            ("mix_turned", "mixT_from_act", "mixT_from_dve", "out_projected", "residual_added"))
        s_ss2, s_var2, s_rt2, s_hn2, s_tr2, s_h2a, s_h2d = (sem(n) for n in
            ("squares2", "variance2", "root2", "normed2", "h2_turned", "h2T_from_act",
             "h2T_from_dve"))
        s_h2w = [sem(f"h2_stored{b}") for b in range(2)]
        s_lg, s_lmx, s_lex, s_aff, s_afT, s_afc = (sem(n) for n in
            ("router_logits", "router_max", "router_exp", "affinity", "affinity_turned", "affinity_copied"))
        s_top, s_topT, s_route = sem("top_ready"), sem("top_turned"), sem("routes_ready")
        s_lamd, s_lame = sem("lambda_dots"), sem("lambda_exps")
        s_land = [sem(f"weight_tile_landed{i}") for i in range(RAW)]
        s_wh, s_wl, s_used = sem("tile_high_part"), sem("tile_low_part"), sem("tile_used")
        s_icol, s_gat, s_xtp, s_xth, s_xtl = (sem(n) for n in
            ("index_column", "rows_gathered", "rows_turned", "xT_high", "xT_low"))
        s_silu, s_hid, s_hT, s_gth, s_gtl = (sem(n) for n in
            ("silu_of_gate", "hidden_ready", "hidden_turned", "hiddenT_high", "hiddenT_low"))
        s_yh, s_yl, s_sel, s_scat, s_acc = (sem(n) for n in
            ("y_high", "y_low", "selection_ready", "scattered", "accumulated"))
        s_out = sem("output_stored")

        UNITS = tile_plan()
        NCONST = 20

        def slice_end(n):
            mine = [u for u, (kind, s, t) in enumerate(UNITS)
                    if (0 if kind == "qk" else s + 1 if kind == "dqk" else s if kind == "tok" else -1) == n]
            return mine[-1] + 1

        def slice_loaded(n):
            return s_win[n % 2], 16 * (1 + n % 2) * (n // 2 + 1)

        def freed_count(u):
            who = evacuated_by(UNITS[u][0])
            n = sum(evacuated_by(k[0]) == who for k in UNITS[:u + 1])
            return {"dve": s_free_d, "act": s_free_a, "bias": s_zb}[who], n

        LR_COPIED = sum(evacuated_by(k[0]) == "act" for k in UNITS[:UNITS.index(("lr", 0, 1)) + 1])
        NEXT_SLICE = {slice_end(n - 1): n for n in range(1, len(SLICES))}

        n_free_a = sum(evacuated_by(k[0]) == "act" for k in UNITS)
        n_free_d = sum(evacuated_by(k[0]) == "dve" for k in UNITS)

        TILES = weight_plan()
        NTI = len(TILES)
        assert NTI % RAW == 0 and NTI % CONV == 0
        place = {t: n for n, t in enumerate(TILES)}

        def tile_used(i, kind, q):
            return s_used, NTI * i + (place[kind, q, 1] + 1)

        ATT = [(g, h, t) for g in range(2) for t in range(GROUPS[g][1]) for h in range(HEADS)]

        block = ctx.enter_context(nc.Block())

        @block.sync
        def _(sp):
            for t in range(NT):
                src = a["x_prompt"][0] if t < 2 else a["x_sample"][0]
                r = t if t < 2 else t - 2
                sp.dma_start(X[:, t, :], src[r * P:(r + 1) * P, :]).then_inc(s_x[t], 16)

            def load_slice(n):
                if n >= 2:
                    sp.wait_ge(s_unit, slice_end(n - 2))
                src = a["w_in"][0][:, SLICES[n]:SLICES[n] + SL].rearrange("(k p) n -> p k n", p=P)
                if n % 2 == 0:
                    sp.dma_start(W[1], src).then_inc(s_win[0], 16)
                else:
                    sp.dma_start((OA if n == len(SLICES) - 1 else OG), src[:, 0:6, :]).then_inc(s_win[1], 16)
                    sp.dma_start(gnorm[:].rearrange("p (k n) -> p k n", k=2), src[:, 6:8, :])\
                        .then_inc(s_win[1], 16)

            load_slice(0)
            sp.dma_start(wlr[:], a["w_in"][0][:, C_LR:C_LR + 2 * RANK]
                         .rearrange("(k p) n -> p k n", p=P)).then_inc(s_wlr, 16)
            sp.wait_ge(s_hn1, NT)
            sp.wait_ge(s_tab, 4)
            sp.wait_ge(s_lamd, 1)
            for n in range(1, len(SLICES)):
                load_slice(n)
            sp.wait_ge(s_unit, len(UNITS))
            for t in range(NT):
                src = a["x_prompt"][0] if t < 2 else a["x_sample"][0]
                r = t if t < 2 else t - 2
                sp.dma_start(X[:, t, :], src[r * P:(r + 1) * P, :]).then_inc(s_x[t], 16)
            sp.wait_ge(s_o, 2 * HEADS)
            for f in range(2):
                sp.dma_start(W[f], a["w_out"][0][:, f * SL:(f + 1) * SL]
                             .rearrange("(k p) n -> p k n", p=P)).then_inc(s_wout, 16)
            sp.dma_start(gnorm[:], a["norm2_g"][0:1, :].broadcast_to([P, D])).then_inc(s_late, 16)
            sp.wait_ge(s_cum, HEADS)
            sp.dma_start(iota, a["iota"]).then_inc(s_late, 16)

            def load_tile(i, n):
                kind, q, part_ = TILES[n]
                e, s = 2 * i + q // NS, q % NS
                rows, cols = (slice(s * FS + part_ * 256, s * FS + part_ * 256 + 256), slice(0, D)) \
                    if kind == "d" else (slice(part_ * 512, part_ * 512 + 512), slice(s * FS, (s + 1) * FS))
                w = a[{"g": "w_gate", "u": "w_up", "d": "w_down"}[kind]][0]
                src = w[e, rows, cols] if isinstance(e, int) else \
                    w[bass.ds(e, 1), rows, cols].rearrange("a r c -> (a r) c")
                sp.dma_start(raw[:, n % RAW, :].rearrange("p (k c) -> p k c", k=2 if kind == "d" else 4),
                             src.rearrange("(k p) c -> p k c", p=P)).then_inc(s_land[n % RAW], 16)

            for t in range(NT):
                if t == NT - 2:
                    sp.wait_ge(s_op, 2 * NT)
                    for n in range(RAW):
                        load_tile(0, n)
                sp.wait_ge(s_hn2, t + 1)
                sp.dma_start(h2_dram[t * P:(t + 1) * P, :], hn[:, t % 2, :]).then_inc(s_h2w[t % 2], 16)
            with sp.Fori(0, NPAIR - 1) as i:
                for n in range(RAW, NTI + RAW):
                    sp.wait_ge(s_wl, i * NTI + (n - RAW + 1))
                    load_tile(i if n < NTI else i + 1, n % NTI)
            for n in range(RAW, NTI):
                sp.wait_ge(s_wl, (NPAIR - 1) * NTI + n - RAW + 1)
                load_tile(NPAIR - 1, n)
            for t in range(NT):
                sp.wait_ge(s_acc, NPAIR * 2 * NT - (2 * NT) + 2 * (t + 1))
                dst = y_prompt[0] if t < 2 else y_sample[0]
                r = t if t < 2 else t - 2
                sp.dma_start(dst[r * P:(r + 1) * P, :], X[:, t, :]).then_inc(s_out, 16)
            sp.wait_ge(s_out, 16 * NT)
            for b in range(2):
                sp.wait_ge(s_h2w[b], 16 * (NT // 2))

        @block.gpsimd
        def _(pool):
            ch = Chain(pool, s_pool)
            ch.link(pool.memset(wg[:], 0.0))
            pool.dma_start(wg[0:RANK, :, 0:DK], a["gla_wg_f"][0].rearrange("r (h d) -> r h d", h=HEADS))\
                .then_inc(s_wg, 16)
            pool.dma_start(wg[RANK:2 * RANK, :, DK:P], a["gla_wg_b"][0].rearrange("r (h d) -> r h d", h=HEADS))\
                .then_inc(s_wg, 16)

            pool.wait_ge(s_tab, 4)
            for v in range(2 * NT):
                s, t = v // NT, v % NT
                pos = t if t < 2 else t - 2
                y3 = yr[v % 2].rearrange("p (m c) -> p m c", m=8)
                o3 = t2[v % 2].rearrange("p (m c) -> p m c", m=8)
                B = tabs[:, 2 * s + 1, pos, :]
                pool.wait_ge(s_free_d, v + 1)
                if v >= 2:
                    pool.wait_ge(s_rope, v - 1)
                for lo, hi in ((0, 32), (32, 0)):
                    pool.tensor_tensor(o3[:, :, lo:lo + 32], y3[:, :, hi:hi + 32],
                                       B[:, lo:lo + 32].unsqueeze(1).broadcast_to([P, 8, 32]),
                                       ALU.mult).then_inc(s_swap, 1)

            for h in range(HEADS):
                pool.wait_ge(s_mid, h + 1)
                if h >= 1:
                    pool.wait_ge(s_e4, h)
                pool.tensor_tensor(zT2.rearrange("p (n c) -> p n c", n=NCH),
                                   blast.unsqueeze(2).broadcast_to([P, NCH, CHUNK]),
                                   cum.rearrange("p (n c) -> p n c", n=NCH), ALU.subtract).then_inc(s_dlast, 1)
                pool.wait_ge(s_e3, h + 1)
                pool.tensor_tensor(qhat[h % 2], qhat[h % 2], Q[:, h, :], ALU.mult).then_inc(s_qh, 1)
                pool.wait_ge(s_e4, h + 1)
                pool.tensor_tensor(khat[h % 2], khat[h % 2], K[:, h, :], ALU.mult).then_inc(s_kh, 1)

            def gather(n):
                pool.wait_ge(s_icol, n)
                pool.nop(nofuse=True)
                pool.indirect_dma_start(out=XE[0:CAP, :], out_offset=None, in_=h2_dram,
                                        in_offset=bass.IndirectOffsetOnAxis(ap=idx_col[0:CAP, 0:1], axis=0))\
                    .then_inc(s_gat, 16)
            for b in range(2):
                pool.wait_ge(s_h2w[b], 16 * (NT // 2))
            gather(1)
            with pool.Fori(0, NPAIR - 1) as i:
                for j in range(2):
                    gather(2 * i + (j + 2))
            gather(NE)

        @block.tensor
        def _(pe):
            def bank(b):
                return ps[:, b, :]

            pe.wait_ge(s_const, 16 * NCONST)
            for t in range(NT):
                pe.wait_ge(s_hn1, t + 1)
                if t >= 2:
                    pe.wait_ge(s_ht_d, 2 * (t - 1))
                for k in range(KD):
                    mm = pe.transpose(ps[:, 2 * (t % 2) + k // 4, (k % 4) * P:(k % 4 + 1) * P],
                                      hn[:, t % 2, k * P:(k + 1) * P], ident[:])
                    if k % 4 == 3:
                        mm.then_inc(s_tr1, 1)
            pe.wait_ge(s_ht_d, 2 * NT)

            def three(out, lh, ll, rh, rl, k):
                pe.matmul(out, lh, rh, start=(k == 0), stop=False)
                pe.matmul(out, ll, rh, start=False, stop=False)
                return pe.matmul(out, lh, rl, start=False, stop=(k == KD - 1))

            def slice_ready(n, k):
                pe.wait_ge(s_wih, KD * n + k + 1)
                pe.wait_ge(s_wil, KD * n + k + 1)

            for u, (kind, s, t) in enumerate(UNITS):
                b = u % 8
                if u >= 8:
                    pe.wait_ge(*freed_count(u - 8))
                if kind == "qk":
                    t0, n = GROUPS[t]
                    for k in range(KD):
                        if s == 0 and t == 0:
                            slice_ready(0, k)
                        mm = three(ps[:, b, 0:n * P].rearrange("p (t c) -> p t c", t=n),
                                   wih[:, k, s * P:(s + 1) * P], slice_low(0, k)[:, s * P:(s + 1) * P],
                                   HTh[:, k, t0 * P:(t0 + n) * P].rearrange("p (t c) -> p t c", t=n),
                                   HTl[:, t0:t0 + n, k, :], k)
                    mm.then_inc(s_unit, 1)
                elif kind == "lr":
                    if t == 0:
                        pe.wait_ge(s_lrh, 1)
                        pe.wait_ge(s_lrl, 1)
                    t0, n = GROUPS[t]
                    for k in range(KD):
                        mm = three(ps[0:2 * RANK, b, 0:n * P].rearrange("p (t c) -> p t c", t=n),
                                   wlrh[:, k, :], wlrl[:, k, :],
                                   HTh[:, k, t0 * P:(t0 + n) * P].rearrange("p (t c) -> p t c", t=n),
                                   HTl[:, t0:t0 + n, k, :], k)
                    mm.then_inc(s_unit, 1)
                elif kind == "gate":
                    t0, n = GROUPS[t]
                    if t == 0:
                        pe.wait_ge(s_wg, 32)
                        pe.wait_ge(s_free_a, LR_COPIED)
                    pe.matmul(ps[:, b, 0:n * P], wg[:, 0, :], lrT[:, t0 * P:(t0 + n) * P],
                              start=True, stop=True).then_inc(s_unit, 1)
                elif kind == "rope":
                    v = s * NT + t
                    pe.wait_ge(s_rope, v + 1)
                    for h in range(HEADS):
                        mm = pe.transpose(ps[:, b, h * P:(h + 1) * P], t1[v % 2][:, h * P:(h + 1) * P], ident[:])
                    mm.then_inc(s_unit, 1)
                else:
                    n = s + 1 if kind == "dqk" else s
                    for k in range(KD):
                        if t == 0:
                            slice_ready(n, k)
                        mm = three(bank(b), HTh[:, k, t * P:(t + 1) * P], HTl[:, t, k, :],
                                   wih[:, k, :], slice_low(n, k), k)
                    mm.then_inc(s_unit, 1)

            pe.wait_ge(s_free_a, n_free_a)
            pe.wait_ge(s_free_d, n_free_d)
            def gate_logits(h):
                pe.wait_ge(s_zb, 2 * h)
                for g, (t0, n) in enumerate(GROUPS):
                    pe.matmul(ps[:, g, 0:n * P], wg[:, h, :], lrT[:, t0 * P:(t0 + n) * P],
                              start=True, stop=True).then_inc(s_z, 1)

            for h in range(HEADS):
                b = h % 2
                if h + 1 < HEADS:
                    gate_logits(h + 1)

                def scores(g):
                    t0, n = GROUPS[g]
                    if 2 * h + g >= 1:
                        pe.wait_ge(s_pred, 2 * h + g)
                    for d in range(2):
                        for t in range(n):
                            c = slice((t0 + t) * P, (t0 + t + 1) * P)
                            mm = pe.matmul(ps[:, 2 + d, t * P:(t + 1) * P], ktil[b][d * DK:(d + 1) * DK, c],
                                           qtil[b][d * DK:(d + 1) * DK, c], start=True, stop=True)
                    mm.then_inc(s_sc, 1)

                def updates(g):
                    t0, n = GROUPS[g]
                    pe.wait_ge(s_ktc, 2 * h + g + 1)
                    if 2 * h + g >= 1:
                        pe.wait_ge(s_st, 2 * h + g)
                    for odd in range(2):
                        r = slice(odd * CHUNK, (odd + 1) * CHUNK)
                        for t in range(n):
                            mm = pe.matmul(ps[:, 6 + odd, t * P:(t + 1) * P], khT[b][r, t0 + t, :],
                                           V[r, t0 + t, h * DV:(h + 1) * DV], start=True, stop=True)
                    mm.then_inc(s_u, 1)

                def outputs(g):
                    t0, n = GROUPS[g]
                    pe.wait_ge(s_pred, 2 * h + g + 1)
                    pe.wait_ge(s_st, 2 * h + g + 1)
                    pe.wait_ge(s_qh, h + 1)
                    for t in range(n):
                        o = ps[:, 4 + g, t * P:(t + 1) * P]
                        pe.matmul(o, Ssb[b][:, t0 + t, :], V[:, t0 + t, h * DV:(h + 1) * DV],
                                  start=(t == 0), stop=False, skip_group_check=True)
                        for odd in range(2):
                            c = 2 * (t0 + t) + odd
                            mm = pe.matmul(ps[odd * CHUNK:(odd + 1) * CHUNK, 4 + g, t * P:(t + 1) * P],
                                           qhat[b][:, c * CHUNK:(c + 1) * CHUNK], states[b][:, c, :],
                                           start=False, stop=True, skip_group_check=True)
                    mm.then_inc(s_o, 1)

                pe.wait_ge(s_qt, 2 * (h + 1))
                scores(0)
                pe.wait_ge(s_kh, h + 1)
                for g, (t0, n) in enumerate(GROUPS):
                    if h >= 1:
                        pe.wait_ge(s_oc, 2 * (h - 1) + g + 1)
                    for t in range(n):
                        mm = pe.transpose(ps[:, 4 + g, t * P:(t + 1) * P],
                                          khat[b][:, (t0 + t) * P:(t0 + t + 1) * P], ident[:])
                    mm.then_inc(s_kt, 1)
                updates(0)
                scores(1)
                updates(1)
                outputs(0)
                outputs(1)

            pe.wait_ge(s_oc, 2 * HEADS)
            for i in range(len(ATT) + 4):
                if i < len(ATT):
                    g, h, t = ATT[i]
                    t0, n = GROUPS[g]
                    if i >= 3:
                        pe.wait_ge(s_p, 2 * (i - 2))
                    for m in range(2):
                        r = slice(m * DK, (m + 1) * DK)
                        mm = pe.matmul(ps[:, 2 * (i % 3) + m, 0:n * P],
                                       QT[r, h, (t0 + t) * P:(t0 + t + 1) * P],
                                       KT[r, h, t0 * P:(t0 + n) * P], start=True, stop=True)
                    mm.then_inc(s_s, 1)
                if 3 <= i < len(ATT) + 3:
                    v = i - 3
                    n = GROUPS[ATT[v][0]][1]
                    pe.wait_ge(s_w, v + 1)
                    if v >= 1:
                        pe.wait_ge(s_wtc, v)
                    for k in range(n):
                        mm = pe.transpose(ps[:, 6, k * P:(k + 1) * P],
                                          wmix[v % 2][:, k * P:(k + 1) * P], ident[:])
                    mm.then_inc(s_wt, 1)
                if i >= 4:
                    v = i - 4
                    g, h, t = ATT[v]
                    t0, n = GROUPS[g]
                    pe.wait_ge(s_wtc, v + 1)
                    if v >= 1:
                        pe.wait_ge(s_pvc, v)
                    for k in range(n):
                        mm = pe.matmul(ps[:, 7, 0:DV], wT[v % 2][:, k, :],
                                       VD[:, t0 + k, h * DV:(h + 1) * DV], start=(k == 0), stop=(k == n - 1))
                    mm.then_inc(s_pv, 1)

            def turn(src, b0, done):
                for k in range(KD):
                    mm = pe.transpose(ps[:, b0 + k // 4, (k % 4) * P:(k % 4 + 1) * P], src(k), ident[:])
                    if k % 4 == 3:
                        mm.then_inc(done, 1)

            for t in range(NT + 3):
                if t < NT:
                    pe.wait_ge(s_mix, 2 * t + 2)
                    if t >= 1:
                        pe.wait_ge(s_mtd, 2 * t)
                    turn(lambda k: (OA if k < 4 else OD)[:, t, (k % 4) * P:(k % 4 + 1) * P], 0, s_mt)
                if 1 <= t <= NT:
                    v = t - 1
                    if v == 0:
                        pe.wait_ge(s_pvc, len(ATT))
                        pe.wait_ge(s_wtc, len(ATT))
                    pe.wait_ge(s_mtd, 2 * (v + 1))
                    for f in range(2):
                        u = 2 * v + f
                        if u >= 3:
                            pe.wait_ge(s_x1, u - 2)
                        for k in range(KD):
                            if v == 0:
                                pe.wait_ge(s_woh, KD * f + k + 1)
                                pe.wait_ge(s_wol, KD * f + k + 1)
                            mm = three(ps[:, 4 + u % 3, :], HTh[:, k, v * P:(v + 1) * P], MTl[:, v, k, :],
                                       wout_high(f, k), wout_low[f][:, k, :], k)
                        mm.then_inc(s_op, 1)
                if 2 <= t <= NT + 1:
                    v = t - 2
                    pe.wait_ge(s_hn2, v + 1)
                    if v >= 1:
                        pe.wait_ge(s_h2a, v)
                        pe.wait_ge(s_h2d, v)
                    turn(lambda k: hn[:, v % 2, k * P:(k + 1) * P], 2, s_tr2)
                if t >= 3:
                    v = t - 3
                    pe.wait_ge(s_h2a, v + 1)
                    pe.wait_ge(s_h2d, v + 1)
                    for k in range(KD):
                        mm = pe.matmul(ps[:, 7, v * NE:(v + 1) * NE], h2T[v % 2][:, k, :], wr[:, k, :],
                                       start=(k == 0), stop=(k == KD - 1))
                    mm.then_inc(s_lg, 1)
            pe.wait_ge(s_aff, 1)
            for t in range(NT):
                mm = pe.transpose(ps[0:NE, 4 + t // 4, (t % 4) * P:(t % 4 + 1) * P],
                                  st[:, 64 + NE * t:64 + NE * (t + 1)], ident[:])
            mm.then_inc(s_afT, 1)
            pe.wait_ge(s_top, 1)
            pe.transpose(ps[0:CAP, 0, 0:NE], topf, ident[0:NE, 0:NE])
            pe.transpose(ps[0:CAP, 0, 32:32 + NE], topv, ident[0:NE, 0:NE]).then_inc(s_topT, 1)
            pe.wait_ge(s_route, 1)

            def turn_rows(e, half, after):
                if half == 0:
                    pe.wait_ge(s_gat, 16 * (e + 1))
                else:
                    pe.wait_ge(s_xtl, 2 * e + 1)
                for k in range(4 * half, 4 * half + 4):
                    mm = pe.transpose(ps[:, 7, (k % 4) * CAP:(k % 4 + 1) * CAP],
                                      XE[0:CAP, k * P:(k + 1) * P], ident[0:CAP, 0:CAP])
                mm.then_inc(s_xtp, 1)

            def products(out, parts, rhs_h, rhs_l, first, last):
                hi, lo = parts
                pe.matmul(out, hi, rhs_h, start=first, stop=False)
                pe.matmul(out, lo, rhs_h, start=False, stop=False)
                return pe.matmul(out, hi, rhs_l, start=False, stop=last)

            def use_tile(i, n):
                kind, q, part_ = TILES[n]
                c = n % CONV
                pe.wait_ge(s_wl, i * NTI + (n + 1))
                if kind in "gu":
                    h_, l_ = (w[:, c, :].rearrange("p (k f) -> p k f", k=4) for w in (wh, wl))
                    b = (0 if kind == "g" else 2) + q % 2
                    j = q // NS
                    for k in range(4):
                        kk = 4 * part_ + k
                        mm = products(ps[0:CAP, b, :], (XTh[j][:, kk, :], XTl[j][:, kk, :]),
                                      h_[:, k, :], l_[:, k, :], kk == 0, kk == KD - 1)
                else:
                    h_, l_ = (w[:, c, :].rearrange("p (f d) -> p f d", f=2) for w in (wh, wl))
                    s = q % NS
                    for f in range(2):
                        ff = 2 * part_ + f
                        for half in range(2):
                            d = slice(half * 512, (half + 1) * 512)
                            mm = products(ps[0:CAP, 4 + half, :], (gTh[:, ff, :], gTl[:, ff, :]),
                                          h_[:, f, d], l_[:, f, d], s == 0 and ff == 0,
                                          s == NS - 1 and ff == FC - 1)
                mm.then_inc(s_used, 1)

            def turn_hidden(i, q):
                pe.wait_ge(s_hid, 8 * i + (q + 1))
                if q >= 1:
                    pe.wait_ge(s_gtl, 8 * i + q)
                for f in range(FC):
                    mm = pe.transpose(ps[:, 6, f * CAP:(f + 1) * CAP], hid[0:CAP, f * P:(f + 1) * P],
                                      ident[0:CAP, 0:CAP])
                mm.then_inc(s_hT, 1)

            def pair(i, last):
                for q in range(2 * NS):
                    if q % NS == 0:
                        pe.wait_ge(s_xtl, 4 * i + 2 * (q // NS) + 2)
                    if q >= 2:
                        pe.wait_ge(s_hid, 8 * i + (q - 1))
                    use_tile(i, place["g", q, 0])
                    use_tile(i, place["g", q, 1])
                    if q >= 1:
                        turn_hidden(i, q - 1)
                    turns = q % NS == 1 and not (last and q > NS)
                    if turns:
                        turn_rows(2 * i + (q // NS + 1), 0, None)
                    use_tile(i, place["u", q, 0])
                    use_tile(i, place["u", q, 1])
                    if turns:
                        turn_rows(2 * i + (q // NS + 1), 1, None)
                    if q >= 1:
                        pe.wait_ge(s_gtl, 8 * i + q)
                        if q == NS + 1:
                            pe.wait_ge(s_yl, 4 * i + 2)
                        use_tile(i, place["d", q - 1, 0])
                        use_tile(i, place["d", q - 1, 1])
                turn_hidden(i, 2 * NS - 1)
                pe.wait_ge(s_gtl, 8 * i + 2 * NS)
                use_tile(i, place["d", 2 * NS - 1, 0])
                use_tile(i, place["d", 2 * NS - 1, 1])
                pe.wait_ge(s_sel, 2 * i + 2)
                pe.wait_ge(s_yl, 4 * i + 4)
                banks = (0, 1, 2, 3, 6, 7)
                for u in range(2 * NT):
                    t, half = u // 2, u % 2
                    if u >= len(banks):
                        pe.wait_ge(s_acc, 2 * NT * i + (u - len(banks) + 1))
                    for j in range(2):
                        for part_ in (Yh, Yl):
                            mm = pe.matmul(ps[:, banks[u % len(banks)], :], sel[j][0:CAP, t * P:(t + 1) * P],
                                           part_[j][0:CAP, half * 512:(half + 1) * 512],
                                           start=(j == 0 and part_ is Yh), stop=(j == 1 and part_ is Yl))
                    mm.then_inc(s_scat, 1)
                pe.wait_ge(s_acc, 2 * NT * i + 2 * NT)

            turn_rows(0, 0, None)
            turn_rows(0, 1, None)
            with pe.Fori(0, NPAIR - 1) as i:
                pair(i, False)
            pair(NPAIR - 1, True)

        @block.scalar
        def _(act):
            ch = Chain(act, s_act)
            n = 0
            for dst, src in (
                (gnorm[:], a["norm1_g"][0:1, :].broadcast_to([P, D])),
                (ident[:], a["ident"]),
                (tabs[:].rearrange("p a b c -> p (a b c)"), a["rot"]),
                (scanm[:], a["scan_mask"]),
                (pmask[:].rearrange("p a b -> p (a b)"), a["pair_mask"]),
                (wr[:], a["w_router"][0].rearrange("(k p) e -> p k e", p=P)),
                (og_gain[:, 0, :], a["gla_norm_g"][0:1, :].broadcast_to([P, DV])),
                (og_gain[:, 1, :], a["diff_norm_g"][0:1, :].broadcast_to([P, DV])),
                (bg[0:DK, :], a["gla_bg_f"][0].rearrange("(h d) -> d h", d=DK)),
                (bg[DK:P, :], a["gla_bg_b"][0].rearrange("(h d) -> d h", d=DK)),
            ):
                with nc.allow_non_contiguous_dma(reason="256 gate biases, one a partition and head"):
                    act.dma_start(dst, src).then_inc(s_const, 16)
                n += 1
            for m, name in enumerate(("lambda_q1", "lambda_k1", "lambda_q2", "lambda_k2")):
                act.dma_start(lamv[:, m, :], a[name][0:1, :].broadcast_to([P, DK])).then_inc(s_const, 16)
                n += 1
            for m, name in ((0, "qk_norm_q"), (2, "qk_norm_k")):
                act.dma_start(gains[:, m, :], a[name][0:1, :].broadcast_to([P, DK])).then_inc(s_const, 16)
                for lo, hi in ((0, 32), (32, 0)):
                    act.dma_start(gains[:, m + 1, lo:lo + 32], a[name][0:1, hi:hi + 32].broadcast_to([P, 32]))\
                        .then_inc(s_const, 16)
                n += 3
            assert n == NCONST

            def high_parts(n):
                if n >= 1:
                    act.wait_ge(s_unit, slice_end(n - 1))
                act.wait_ge(*slice_loaded(n))
                for k in range(KD):
                    act.copy(wih[:, k, :], slice_raw(n, k)).then_inc(s_wih, 1)

            high_parts(0)
            act.wait_ge(s_wlr, 16)
            act.copy(wlrh[:], wlr[:]).then_inc(s_lrh, 1)
            act.wait_ge(s_lamd, 1)
            act.activation(nlam[:, 2:4], nlam[:, 0:2], ACT.Exp).then_inc(s_lame, 1)
            for t in range(NT + 1):
                if t < NT:
                    act.wait_ge(s_x[t], 16)
                    act.activation(junk1, X[:, t, :], ACT.Square, accum_out=st[:, t:t + 1]).then_inc(s_ss1, 1)
                    act.wait_ge(s_var1, t + 1)
                    act.activation(st[:, 16 + t:17 + t], st[:, 8 + t:9 + t], ACT.Sqrt).then_inc(s_rt1, 1)
                if t >= 1:
                    v = t - 1
                    for f in range(2):
                        act.wait_ge(s_tr1, 2 * v + f + 1)
                        act.copy(HTh[:, 4 * f:4 * f + 4, v * P:(v + 1) * P],
                                 ps[:, 2 * (v % 2) + f, :].rearrange("p (k c) -> p k c", k=4)).then_inc(s_ht_a, 1)

            def softplus(h):
                act.wait_ge(s_absz, h + 1)
                ch.link(act.activation(zT2, zT2, ACT.Exp, scale=-1.0))
                act.activation(zT2, zT2, ACT.Ln, bias=1.0).then_inc(s_sp, 1)

            def factors(h):
                b = h % 2
                act.wait_ge(s_dmid, h + 1)
                if h >= 2:
                    act.wait_ge(s_sc, 2 * (h - 1))
                act.activation(qtil[b], zT1, ACT.Exp, scale=1.0 / TAU)
                act.activation(ktil[b], zT1, ACT.Exp, scale=-1.0 / TAU).then_inc(s_e1, 1)
                if h >= 2:
                    act.wait_ge(s_o, 2 * (h - 1))
                act.activation(qhat[b], cum, ACT.Exp, scale=1.0 / TAU).then_inc(s_e3, 1)
                act.wait_ge(s_dlast, h + 1)
                if h >= 2:
                    act.wait_ge(s_kt, 2 * (h - 1))
                    act.wait_ge(s_st, 2 * (h - 1))
                act.activation(khat[b], zT2, ACT.Exp, scale=1.0 / TAU).then_inc(s_e4, 1)
                act.activation(decay[b], blast, ACT.Exp, scale=1.0 / TAU).then_inc(s_dec, 1)

            for u, (kind, s, t) in enumerate(UNITS):
                b = u % 8
                act.wait_ge(s_unit, u + 1)
                if u + 1 in NEXT_SLICE:
                    high_parts(NEXT_SLICE[u + 1])
                if kind == "qk":
                    t0, n = (0, T_PROMPT) if t == 0 else (T_PROMPT, T_SAMPLE)
                    dst, sc = (Q, DK ** -0.5) if s < 2 else (K, 1.0)
                    for half in range(2):
                        h = 2 * (s % 2) + half
                        src = ps[half * DK:(half + 1) * DK, b, 0:n]
                        act.mul(dst[0:DK, h, t0:t0 + n], src, sc)
                        last = act.mul(dst[DK:P, h, t0:t0 + n], src, sc)
                    last.then_inc(s_free_a, 1)
                elif kind == "lr":
                    t0, n = (0, T_PROMPT) if t == 0 else (T_PROMPT, T_SAMPLE)
                    act.copy(lrT[:, t0:t0 + n], ps[0:2 * RANK, b, 0:n]).then_inc(s_free_a, 1)
                elif kind == "gate":
                    if t == 1:
                        softplus(0)
                        factors(0)
                elif kind == "dqk":
                    v = s * NT + t
                    if v >= 2:
                        act.wait_ge(s_sumq, v - 1)
                    act.activation(sq[v % 2], ps[:, b, :], ACT.Square).then_inc(s_sq, 1)
                    act.wait_ge(s_varq, v + 1)
                    act.activation(st[:, 40 + 8 * (v % 2):48 + 8 * (v % 2)],
                                   st[:, 24 + 8 * (v % 2):32 + 8 * (v % 2)], ACT.Sqrt).then_inc(s_rtq, 1)
                elif kind == "rope":
                    dst = QT if s == 0 else KT
                    act.copy(dst[:, :, t * P:(t + 1) * P],
                             ps[:, b, :].rearrange("p (h c) -> p h c", h=HEADS)).then_inc(s_free_a, 1)
                else:
                    dst = {3: V, 4: VD, 5: OG}[s]
                    act.copy(dst[:, t, :], ps[:, b, :]).then_inc(s_free_a, 1)

            for h in range(HEADS):
                for g, (t0, n) in enumerate(GROUPS):
                    act.wait_ge(s_kt, 2 * h + g + 1)
                    if h >= 2:
                        act.wait_ge(s_u, 2 * (h - 2) + g + 1)
                    act.copy(khT[h % 2][:, t0:t0 + n, :], ps[:, 4 + g, 0:n * P]
                             .rearrange("p (t c) -> p t c", t=n)).then_inc(s_ktc, 1)
                if h + 1 < HEADS:
                    softplus(h + 1)
                    factors(h + 1)
                else:
                    act.wait_ge(s_free_a, n_free_a)
                    act.activation(OG, OG, ACT.Silu).then_inc(s_ego, 1)
                for g, (t0, n) in enumerate(GROUPS):
                    act.wait_ge(s_o, 2 * h + g + 1)
                    act.copy(OA[:, t0:t0 + n, h * DV:(h + 1) * DV], ps[:, 4 + g, 0:n * P]
                             .rearrange("p (t c) -> p t c", t=n)).then_inc(s_oc, 1)

            def wout_high_part(f, k):
                act.wait_ge(s_wout, 32)
                act.copy(wout_high(f, k), W[f][:, k, :]).then_inc(s_woh, 1)

            for i in range(len(ATT) + 4):
                if i < len(ATT):
                    g, h, t = ATT[i]
                    n = GROUPS[g][1] * P
                    act.wait_ge(s_mx, i + 1)
                    if i >= 3:
                        act.wait_ge(s_w, i - 2)
                    for m in range(2):
                        act.activation(prob[i % 3][:, m, 0:n], ps[:, 2 * (i % 3) + m, 0:n], ACT.Exp,
                                       bias=st[:, 56 + 2 * (i % 2) + m:57 + 2 * (i % 2) + m],
                                       accum_out=st[:, 60 + 2 * (i % 2) + m:61 + 2 * (i % 2) + m]).then_inc(s_p, 1)
                if 1 <= i <= len(ATT):
                    v = i - 1
                    n = GROUPS[ATT[v][0]][1] * P
                    b = 2 * (v % 2)
                    act.wait_ge(s_c, v + 1)
                    if v >= 2:
                        act.wait_ge(s_wt, v - 1)
                    act.mul(wmix[v % 2][:, 0:n], prob[v % 3][:, 1, 0:n], st[:, 164 + b:165 + b]).then_inc(s_cm, 1)
                if 3 <= i < len(ATT) + 3:
                    v = i - 3
                    n = GROUPS[ATT[v][0]][1]
                    act.wait_ge(s_wt, v + 1)
                    if v >= 2:
                        act.wait_ge(s_pv, v - 1)
                    act.copy(wT[v % 2][:, 0:n, :], ps[:, 6, 0:n * P]
                             .rearrange("p (t c) -> p t c", t=n)).then_inc(s_wtc, 1)
                if i >= 4:
                    v = i - 4
                    g, h, t = ATT[v]
                    act.wait_ge(s_pv, v + 1)
                    act.copy(OD[:, GROUPS[g][0] + t, h * DV:(h + 1) * DV], ps[:, 7, 0:DV]).then_inc(s_pvc, 1)
                if 6 <= i < 6 + 2 * KD and i % 2 == 0:
                    wout_high_part(0, (i - 6) // 2)

            act.wait_ge(s_vare, 1)
            act.activation(st[:, 112:160], st[:, 64:112], ACT.Sqrt).then_inc(s_rte, 1)
            act.wait_ge(s_s, len(ATT))
            for k in range(KD):
                wout_high_part(1, k)
            for t in range(NT + 2):
                if t < NT:
                    for f in range(2):
                        act.wait_ge(s_mt, 2 * t + f + 1)
                        act.copy(HTh[:, 4 * f:4 * f + 4, t * P:(t + 1) * P],
                                 ps[:, f, :].rearrange("p (k c) -> p k c", k=4)).then_inc(s_mta, 1)
                if 1 <= t <= NT:
                    v = t - 1
                    act.wait_ge(s_x1, 2 * (v + 1))
                    act.activation(junk, X[:, v, :], ACT.Square, accum_out=st[:, v:v + 1]).then_inc(s_ss2, 1)
                    act.wait_ge(s_var2, v + 1)
                    act.activation(st[:, 16 + v:17 + v], st[:, 8 + v:9 + v], ACT.Sqrt).then_inc(s_rt2, 1)
                if t >= 2:
                    v = t - 2
                    act.wait_ge(s_tr2, 2 * v + 1)
                    if v >= 2:
                        act.wait_ge(s_lg, v - 1)
                    act.copy(h2T[v % 2][:, 0:4, :],
                             ps[:, 2, :].rearrange("p (k c) -> p k c", k=4)).then_inc(s_h2a, 1)
            act.wait_ge(s_lmx, 1)
            act.activation(st[:, 64:160], st[:, 64:160], ACT.Exp).then_inc(s_lex, 1)

            def split(i, n):
                act.wait_ge(s_land[n % RAW], i * (16 * NTI // RAW) + 16 * (n // RAW + 1))
                if not (isinstance(i, int) and i == 0 and n < CONV):
                    act.wait_ge(s_used, i * NTI + (n - CONV + 1))
                act.copy(wh[:, n % CONV, :], raw[:, n % RAW, :]).then_inc(s_wh, 1)

            def xt_copy(e, half, j):
                act.wait_ge(s_xtp, 2 * e + (half + 1))
                act.copy(XTh[j][:, 4 * half:4 * half + 4, :],
                         ps[:, 7, 0:4 * CAP].rearrange("p (k c) -> p k c", k=4)).then_inc(s_xth, 1)

            def y_copy(i, j):
                act.wait_ge(s_sel, 2 * i + (j + 1))
                act.wait_ge(*tile_used(i, "d", NS * (j + 1) - 1))
                for half in range(2):
                    act.mul(Yh[j][0:CAP, half * 512:(half + 1) * 512], ps[0:CAP, 4 + half, :],
                            cur[0:CAP, 1:2]).then_inc(s_yh, 1)

            def pair(i, last):
                for n in range(NTI):
                    kind, q, part_ = TILES[n]
                    if part_ == 0 and kind == "u" and q >= 1:
                        act.wait_ge(s_hT, 8 * i + q)
                        act.copy(gTh[:], ps[:, 6, 0:FC * CAP].rearrange("p (f c) -> p f c", f=FC))\
                            .then_inc(s_gth, 1)
                    turns = kind in "ud" and q % NS == (1 if kind == "u" else 0) and part_ == 0 \
                        and (kind == "u" or q % NS == 0) and not (last and q >= NS)
                    if turns:
                        e = 2 * i + (q // NS + 1)
                        xt_copy(e, 0 if kind == "u" else 1, (q // NS + 1) % 2)
                    if n >= 1 and TILES[n - 1][0] == "u" and TILES[n - 1][2] == 1:
                        qq = TILES[n - 1][1]
                        act.wait_ge(*tile_used(i, "u", qq))
                        act.activation(hid[0:CAP], ps[0:CAP, qq % 2, :], ACT.Silu).then_inc(s_silu, 1)
                    if n >= 1 and TILES[n - 1] == ("d", NS - 1, 1):
                        y_copy(i, 0)
                    if n == place["d", 2 * NS - 1, 0]:
                        act.wait_ge(s_hT, 8 * i + 2 * NS)
                        act.copy(gTh[:], ps[:, 6, 0:FC * CAP].rearrange("p (f c) -> p f c", f=FC))\
                            .then_inc(s_gth, 1)
                    if not (last and n + AHEAD >= NTI):
                        split(i, n + AHEAD) if n + AHEAD < NTI else split(i + 1, n + AHEAD - NTI)
                y_copy(i, 1)

            xt_copy(0, 0, 0)
            xt_copy(0, 1, 0)
            for n in range(AHEAD):
                split(0, n)
            with act.Fori(0, NPAIR - 1) as i:
                pair(i, False)
            pair(NPAIR - 1, True)

        @block.vector
        def _(dve):
            ch = Chain(dve, s_dve)

            def low_parts(n):
                for k in range(KD):
                    dve.wait_ge(s_wih, KD * n + k + 1)
                    dve.tensor_tensor(slice_low(n, k), slice_raw(n, k), wih[:, k, :].bitcast(F32),
                                      ALU.subtract).then_inc(s_wil, 1)

            low_parts(0)
            dve.wait_ge(s_lrh, 1)
            dve.tensor_tensor(wlrl[:], wlr[:], wlrh[:].bitcast(F32), ALU.subtract).then_inc(s_lrl, 1)
            dve.wait_ge(s_const, 16 * NCONST)
            for s in range(2):
                for ab in range(2):
                    m = 2 * s + ab
                    dve.tensor_tensor(tabs[:, m, :, :], tabs[:, m, :, :],
                                      gains[:, m, :].unsqueeze(1).broadcast_to([P, 4, DK]),
                                      ALU.mult).then_inc(s_tab, 1)
            ch.mark(dve.tensor_tensor_reduce(lamv[:, 0, :], lamv[:, 0, :], lamv[:, 1, :], 1.0, 0.0,
                                             ALU.mult, ALU.add, nlam[:, 0:1]))
            dve.tensor_tensor_reduce(lamv[:, 2, :], lamv[:, 2, :], lamv[:, 3, :], 1.0, 0.0,
                                     ALU.mult, ALU.add, nlam[:, 1:2]).then_inc(s_lamd, 1)
            ch.mark(dve.tensor_scalar(og_gain[:, 1, :], og_gain[:, 1, :], 1.0 - LAM_INIT, None, ALU.mult))
            dve.wait_ge(s_lame, 1)
            ch.link(dve.tensor_tensor(nlam[:, 0:1], nlam[:, 3:4], nlam[:, 2:3], ALU.subtract))
            ch.mark(dve.tensor_scalar(nlam[:, 0:1], nlam[:, 0:1], -LAM_INIT, None, ALU.add))

            for t in range(NT + 1):
                if t < NT:
                    dve.wait_ge(s_ss1, t + 1)
                    dve.tensor_scalar(st[:, 8 + t:9 + t], st[:, t:t + 1], 1.0 / D, EPS, ALU.mult, ALU.add)\
                        .then_inc(s_var1, 1)
                    dve.wait_ge(s_rt1, t + 1)
                    ch.link(dve.reciprocal(st[:, 16 + t:17 + t], st[:, 16 + t:17 + t]))
                    if t >= 2:
                        dve.wait_ge(s_tr1, 2 * (t - 1))
                    dve.scalar_tensor_tensor(hn[:, t % 2, :], X[:, t, :], st[:, 16 + t:17 + t], gnorm[:],
                                             ALU.mult, ALU.mult).then_inc(s_hn1, 1)
                if t >= 1:
                    v = t - 1
                    for f in range(2):
                        dve.wait_ge(s_ht_a, 2 * v + f + 1)
                        dve.tensor_tensor(HTl[:, v, 4 * f:4 * f + 4, :],
                                          ps[:, 2 * (v % 2) + f, :].rearrange("p (k c) -> p k c", k=4),
                                          HTh[:, 4 * f:4 * f + 4, v * P:(v + 1) * P].bitcast(F32),
                                          ALU.subtract).then_inc(s_ht_d, 1)

            by_chunk = lambda x: x.rearrange("p (n c) -> p n c", n=NCH)

            def logits(h):
                if h >= 1:
                    dve.wait_ge(s_e1, h)
                for g, (t0, n) in enumerate(GROUPS):
                    if h >= 1:
                        dve.wait_ge(s_z, 2 * (h - 1) + g + 1)
                        b = g
                    else:
                        u = UNITS.index(("gate", 0, g))
                        dve.wait_ge(s_unit, u + 1)
                        b = u % 8
                    dve.tensor_scalar(zT1[:, t0 * P:(t0 + n) * P], ps[:, b, 0:n * P], bg[:, h:h + 1], None,
                                      ALU.add).then_inc(s_zb, 1)
                dve.wait_ge(s_zb, 2 * h + 2)
                if h >= 1:
                    dve.wait_ge(s_e4, h)
                dve.scalar_tensor_tensor(zT2, zT1, -1.0, zT1, ALU.mult, ALU.max).then_inc(s_absz, 1)

            def sums(h):
                dve.wait_ge(s_sp, h + 1)
                ch.link(dve.scalar_tensor_tensor(zT2, zT1, 0.0, zT2, ALU.min, ALU.subtract))
                if h >= 1:
                    dve.wait_ge(s_e3, h)
                    dve.wait_ge(s_dlast, h)
                dve.tensor_tensor_scan(cum[0:DK], scanm[0:DK], zT2[0:DK], 0.0, ALU.mult, ALU.add)
                dve.tensor_tensor_scan(cum[DK:P, ::-1], scanm[DK:P, ::-1], zT2[DK:P, ::-1], 0.0,
                                       ALU.mult, ALU.add).then_inc(s_cum, 1)
                dve.wait_ge(s_cum, h + 1)
                if h >= 1:
                    dve.wait_ge(s_dec, h)
                dve.tensor_copy(bmid[0:DK], by_chunk(cum)[0:DK, :, CHUNK // 2 - 1])
                dve.tensor_copy(bmid[DK:P], by_chunk(cum)[DK:P, :, CHUNK // 2])
                dve.tensor_copy(blast[0:DK], by_chunk(cum)[0:DK, :, CHUNK - 1])
                dve.tensor_copy(blast[DK:P], by_chunk(cum)[DK:P, :, 0]).then_inc(s_mid, 1)
                dve.wait_ge(s_mid, h + 1)
                dve.tensor_tensor(by_chunk(zT1), by_chunk(cum), bmid.unsqueeze(2).broadcast_to([P, NCH, CHUNK]),
                                  ALU.subtract).then_inc(s_dmid, 1)

            def score_factors(h):
                dve.wait_ge(s_e1, h + 1)
                dve.tensor_tensor(qtil[h % 2], qtil[h % 2], Q[:, h, :], ALU.mult).then_inc(s_qt, 1)
                dve.tensor_tensor(ktil[h % 2], ktil[h % 2], K[:, h, :], ALU.mult).then_inc(s_qt, 1)

            def rope_add(v):
                dve.wait_ge(s_swap, 2 * (v + 1))
                dve.tensor_tensor(t1[v % 2], t1[v % 2], t2[v % 2], ALU.add).then_inc(s_rope, 1)

            dve.wait_ge(s_tab, 4)
            for u, (kind, s, t) in enumerate(UNITS):
                if u + 1 in NEXT_SLICE:
                    if NEXT_SLICE[u + 1] == 4:
                        rope_add(2 * NT - 1)
                    low_parts(NEXT_SLICE[u + 1])
                if kind == "gate" and t == 1:
                    logits(0)
                    sums(0)
                    score_factors(0)
                if kind != "dqk":
                    continue
                v = s * NT + t
                pos = t if t < 2 else t - 2
                b8 = 8 * (v % 2)
                dve.wait_ge(s_sq, v + 1)
                dve.tensor_reduce(st[:, 24 + b8:32 + b8], sq[v % 2].rearrange("p (m c) -> p m c", m=8),
                                  AX_X, ALU.add).then_inc(s_sumq, 1)
                dve.wait_ge(s_sumq, v + 1)
                dve.tensor_scalar(st[:, 24 + b8:32 + b8], st[:, 24 + b8:32 + b8], 1.0 / DK, EPS,
                                  ALU.mult, ALU.add).then_inc(s_varq, 1)
                if v >= 1:
                    rope_add(v - 1)
                dve.wait_ge(s_rtq, v + 1)
                ch.link(dve.reciprocal(st[:, 40 + b8:48 + b8], st[:, 40 + b8:48 + b8]))
                if v >= 2:
                    dve.wait_ge(s_swap, 2 * (v - 1))
                dve.tensor_tensor(yr[v % 2].rearrange("p (m c) -> p m c", m=8),
                                  ps[:, u % 8, :].rearrange("p (m c) -> p m c", m=8),
                                  st[:, 40 + b8:48 + b8].unsqueeze(2).broadcast_to([P, 8, DK]),
                                  ALU.mult).then_inc(s_free_d, 1)
                dve.wait_ge(s_free_d, v + 1)
                if v >= 2:
                    dve.wait_ge(s_unit, UNITS.index(("rope", (v - 2) // NT, (v - 2) % NT)) + 1)
                ch.link(dve.tensor_tensor(t1[v % 2].rearrange("p (m c) -> p m c", m=8),
                                          yr[v % 2].rearrange("p (m c) -> p m c", m=8),
                                          tabs[:, 2 * s, pos, :].unsqueeze(1).broadcast_to([P, 8, DK]),
                                          ALU.mult))

            dve.wait_ge(s_unit, len(UNITS))
            for b in range(2):
                ch.mark(dve.memset(Ssb[b], 0.0))
                ch.link(dve.memset(states[b], 0.0))
            def mask(h, g):
                t0, n = GROUPS[g]
                dve.wait_ge(s_sc, 2 * h + g + 1)
                if h >= 2:
                    dve.wait_ge(s_o, 2 * (h - 2) + g + 1)
                for d in range(2):
                    last = dve.copy_predicated(Ssb[h % 2][:, t0:t0 + n, :],
                                               pmask[:, d, :].unsqueeze(1).broadcast_to([P, n, P]),
                                               ps[:, 2 + d, 0:n * P].rearrange("p (t c) -> p t c", t=n))
                    if d == 0:
                        ch.link(last)
                last.then_inc(s_pred, 1)

            def carry(h, g):
                t0, n = GROUPS[g]
                b = h % 2
                dve.wait_ge(s_u, 2 * h + g + 1)
                dve.wait_ge(s_dec, h + 1)
                if h >= 2:
                    dve.wait_ge(s_o, 2 * (h - 2) + g + 1)
                c0, nc_ = 2 * t0, 2 * n
                for m in range(nc_ - 1):
                    for d, c, nxt in ((0, c0 + m, c0 + m + 1), (1, c0 + nc_ - 1 - m, c0 + nc_ - 2 - m)):
                        r = slice(d * DK, (d + 1) * DK)
                        t = c // 2 - t0
                        last = dve.scalar_tensor_tensor(states[b][r, nxt, :], states[b][r, c, :],
                                                        decay[b][r, c:c + 1],
                                                        ps[r, 6 + c % 2, t * P:(t + 1) * P], ALU.mult, ALU.add)
                    if m < nc_ - 2:
                        ch.link(last)
                last.then_inc(s_st, 1)

            for h in range(HEADS):
                more = h + 1 < HEADS
                if more:
                    logits(h + 1)
                mask(h, 0)
                if more:
                    sums(h + 1)
                carry(h, 0)
                mask(h, 1)
                if more:
                    score_factors(h + 1)
                carry(h, 1)

            hsums = st[:, 64:112].rearrange("p (t m) -> p t m", t=NT)
            roots = st[:, 112:160].rearrange("p (t m) -> p t m", t=NT)
            heads = lambda x: x.rearrange("p (h c) -> p h c", h=HEADS)

            def head_squares(o_, m, t):
                ch.link(dve.tensor_tensor(square[m], o_[:, t, :], o_[:, t, :], ALU.mult))

            def head_sums(o_, m, t):
                ch.mark(dve.tensor_reduce(hsums[:, t, 4 * m:4 * m + 4], heads(square[m]), AX_X, ALU.add))

            def head_gain(o_, m, t):
                ch.mark(dve.tensor_tensor(heads(o_[:, t, :]), heads(o_[:, t, :]),
                                          og_gain[:, m, :].unsqueeze(1).broadcast_to([P, HEADS, DV]), ALU.mult))

            def head_gate(t):
                ch.own()
                ch.mark(dve.tensor_tensor(OA[:, t, :], OA[:, t, :], OG[:, t, :], ALU.mult))

            def beside(i):
                if i == 0:
                    dve.wait_ge(s_oc, 2 * HEADS)
                    dve.wait_ge(s_ego, 1)
                if i < 4 * NT:
                    t = i // 4
                    ch.own()
                    (head_squares, head_sums, head_gain, lambda o_, m, t: head_gate(t))[i % 4](OA, 0, t)
                if i >= 8 and (i - 8) % 4 == 0:
                    t = (i - 8) // 4
                    dve.wait_ge(s_pvc, 4 * (t + 1))
                    head_squares(OD, 1, t)
                    head_sums(OD, 1, t)
                    head_gain(OD, 1, t)

            def wout_low_part(f, k):
                dve.wait_ge(s_woh, KD * f + k + 1)
                dve.tensor_tensor(wout_low[f][:, k, :], W[f][:, k, :], wout_high(f, k).bitcast(F32),
                                  ALU.subtract).then_inc(s_wol, 1)

            for i in range(len(ATT) + 2):
                if i < len(ATT):
                    n = GROUPS[ATT[i][0]][1] * P
                    b, b3 = 2 * (i % 2), 2 * (i % 3)
                    dve.wait_ge(s_s, i + 1)
                    if i >= 2:
                        dve.wait_ge(s_p, 2 * (i - 1))
                    dve.tensor_reduce(st[:, 56 + b:58 + b], ps[:, b3:b3 + 2, 0:n], AX_X, ALU.max, negate=True)\
                        .then_inc(s_mx, 1)
                if 1 <= i <= len(ATT):
                    v = i - 1
                    b = 2 * (v % 2)
                    dve.wait_ge(s_p, 2 * v + 2)
                    if v >= 2:
                        dve.wait_ge(s_w, v - 1)
                    ch.link(dve.reciprocal(st[:, 160 + b:162 + b], st[:, 60 + b:62 + b]))
                    dve.tensor_tensor(st[:, 164 + b:165 + b], st[:, 161 + b:162 + b], nlam[:, 0:1],
                                      ALU.mult).then_inc(s_c, 1)
                if i >= 2:
                    v = i - 2
                    n = GROUPS[ATT[v][0]][1] * P
                    b = 2 * (v % 2)
                    dve.wait_ge(s_cm, v + 1)
                    dve.scalar_tensor_tensor(wmix[v % 2][:, 0:n], prob[v % 3][:, 0, 0:n],
                                             st[:, 160 + b:161 + b], wmix[v % 2][:, 0:n],
                                             ALU.mult, ALU.add).then_inc(s_w, 1)
                if 1 <= i <= len(ATT):
                    beside(i - 1)
                if 8 <= i < 8 + 2 * KD and i % 2 == 0:
                    wout_low_part(0, (i - 8) // 2)
            for t in (NT - 2, NT - 1):
                ch.own()
                beside(4 * t + 8)
            ch.own()
            dve.tensor_scalar(st[:, 64:112], st[:, 64:112], 1.0 / DV, EPS, ALU.mult, ALU.add).then_inc(s_vare, 1)
            dve.wait_ge(s_rte, 1)
            ch.link(dve.reciprocal(st[:, 112:160], st[:, 112:160]))

            def scale_heads(t):
                for m, o_ in enumerate((OA, OD)):
                    dve.tensor_tensor(heads(o_[:, t, :]), heads(o_[:, t, :]),
                                      roots[:, t, 4 * m:4 * m + 4].unsqueeze(2).broadcast_to([P, HEADS, DV]),
                                      ALU.mult).then_inc(s_mix, 1)

            scale_heads(0)
            for t in range(NT + 2):
                if t + 1 < NT:
                    scale_heads(t + 1)
                if t < NT:
                    for f in range(2):
                        dve.wait_ge(s_mta, 2 * t + f + 1)
                        dve.tensor_tensor(MTl[:, t, 4 * f:4 * f + 4, :],
                                          ps[:, f, :].rearrange("p (k c) -> p k c", k=4),
                                          HTh[:, 4 * f:4 * f + 4, t * P:(t + 1) * P].bitcast(F32),
                                          ALU.subtract).then_inc(s_mtd, 1)
                if t == 0:
                    for k in range(KD):
                        wout_low_part(1, k)
                if 1 <= t <= NT:
                    v = t - 1
                    for f in range(2):
                        u = 2 * v + f
                        dve.wait_ge(s_op, u + 1)
                        if f == 0:
                            dve.wait_ge(s_x[v], 32)
                        x = X[:, v, f * 512:(f + 1) * 512]
                        dve.tensor_tensor(x, x, ps[:, 4 + u % 3, :], ALU.add).then_inc(s_x1, 1)
                    dve.wait_ge(s_ss2, v + 1)
                    dve.tensor_scalar(st[:, 8 + v:9 + v], st[:, v:v + 1], 1.0 / D, EPS, ALU.mult, ALU.add)\
                        .then_inc(s_var2, 1)
                    dve.wait_ge(s_rt2, v + 1)
                    ch.link(dve.reciprocal(st[:, 16 + v:17 + v], st[:, 16 + v:17 + v]))
                    if v == 0:
                        dve.wait_ge(s_late, 32)
                    if v >= 2:
                        dve.wait_ge(s_h2w[v % 2], 16 * (v // 2))
                        dve.wait_ge(s_tr2, 2 * (v - 1))
                    dve.scalar_tensor_tensor(hn[:, v % 2, :], X[:, v, :], st[:, 16 + v:17 + v], gnorm[:],
                                             ALU.mult, ALU.mult).then_inc(s_hn2, 1)
                if t >= 2:
                    v = t - 2
                    dve.wait_ge(s_tr2, 2 * v + 2)
                    if v >= 2:
                        dve.wait_ge(s_lg, v - 1)
                    dve.tensor_copy(h2T[v % 2][:, 4:8, :],
                                    ps[:, 3, :].rearrange("p (k c) -> p k c", k=4)).then_inc(s_h2d, 1)

            aff_tok = st[:, 64:160].rearrange("p (t e) -> p t e", t=NT)
            logit = ps[:, 7, 0:NT * NE].rearrange("p (t e) -> p t e", t=NT)
            stat = st[:, 24:24 + NT]
            dve.wait_ge(s_lg, NT)
            ch.link(dve.tensor_reduce(stat, logit, AX_X, ALU.max))
            dve.tensor_tensor(aff_tok, logit, stat.unsqueeze(2).broadcast_to([P, NT, NE]), ALU.subtract)\
                .then_inc(s_lmx, 1)
            dve.wait_ge(s_lex, 1)
            ch.link(dve.tensor_reduce(stat, aff_tok, AX_X, ALU.add))
            ch.link(dve.reciprocal(stat, stat))
            dve.tensor_tensor(aff_tok, aff_tok, stat.unsqueeze(2).broadcast_to([P, NT, NE]), ALU.mult)\
                .then_inc(s_aff, 1)
            dve.wait_ge(s_afT, 1)
            dve.tensor_copy(aff[:, 0:4 * P], ps[0:NE, 4, :]).then_inc(s_afc, 1)
            dve.tensor_copy(aff[:, 4 * P:TOK], ps[0:NE, 5, 0:2 * P]).then_inc(s_afc, 1)

            dve.wait_ge(s_afc, 2)
            for lo, n, c0, cap in ((0, T_PROMPT, 0, CAP_P), (T_PROMPT, T_SAMPLE, CAP_P, CAP_S)):
                row = aff[:, lo:lo + n]
                for c in range(c0, c0 + cap, 8):
                    ch.link(dve.max(topv[:, c:c + 8], row))
                    ch.link(dve.max_index(topi[:, c:c + 8], topv[:, c:c + 8], row))
                    ch.link(dve.match_replace(row, topv[:, c:c + 8], row, -1.0))
            ch.link(dve.tensor_copy(topf, topi))
            dve.tensor_scalar(topf[:, CAP_P:CAP], topf[:, CAP_P:CAP], float(T_PROMPT), None, ALU.add)\
                .then_inc(s_top, 1)
            dve.wait_ge(s_topT, 1)
            ch.mark(dve.tensor_copy(gidx[0:CAP, 0:NE], ps[0:CAP, 0, 0:NE]))
            ch.mark(dve.tensor_copy(grow[0:CAP, :], ps[0:CAP, 0, 0:NE]))
            dve.tensor_copy(gate[0:CAP, :], ps[0:CAP, 0, 32:32 + NE]).then_inc(s_route, 1)
            dve.wait_ge(s_route, 1)
            dve.tensor_copy(idx_col[0:CAP, 0:1], gidx[0:CAP, 0:1]).then_inc(s_icol, 1)

            def split(i, n):
                dve.wait_ge(s_wh, i * NTI + (n + 1))
                dve.tensor_tensor(wl[:, n % CONV, :], raw[:, n % RAW, :], wh[:, n % CONV, :].bitcast(F32),
                                  ALU.subtract).then_inc(s_wl, 1)

            def xt_copy(e, half, j):
                dve.wait_ge(s_xth, 2 * e + (half + 1))
                dve.tensor_tensor(XTl[j][:, 4 * half:4 * half + 4, :],
                                  ps[:, 7, 0:4 * CAP].rearrange("p (k c) -> p k c", k=4),
                                  XTh[j][:, 4 * half:4 * half + 4, :].bitcast(F32), ALU.subtract).then_inc(s_xtl, 1)

            def y_copy(i, j):
                for half in range(2):
                    c = slice(half * 512, (half + 1) * 512)
                    dve.wait_ge(s_yh, 4 * i + (2 * j + half + 1))
                    dve.scalar_tensor_tensor(Yl[j][0:CAP, c], ps[0:CAP, 4 + half, :], cur[0:CAP, 1:2],
                                             Yh[j][0:CAP, c].bitcast(F32), ALU.mult, ALU.subtract).then_inc(s_yl, 1)

            def next_rows(i, j):
                dve.wait_ge(s_gat, 32 * i + 16 * (j + 1))
                dve.tensor_copy(idx_col[0:CAP, 0:1], gidx[0:CAP, bass.ds(2 * i + (j + 1), 1)])\
                    .then_inc(s_icol, 1)

            def selection(i, j):
                ch.mark(dve.tensor_copy(cur[0:CAP, 0:1], grow[0:CAP, bass.ds(2 * i + j, 1)]))
                ch.link(dve.tensor_copy(cur[0:CAP, 1:2], gate[0:CAP, bass.ds(2 * i + j, 1)]))
                dve.tensor_scalar(sel[j][0:CAP], iota[0:CAP], cur[0:CAP, 0:1], None, ALU.is_equal)\
                    .then_inc(s_sel, 1)

            def pair(i, last):
                for n in range(NTI):
                    kind, q, part_ = TILES[n]
                    if n == 0:
                        next_rows(i, 0)
                        selection(i, 0)
                    if part_ == 0 and kind == "u" and q >= 1:
                        dve.wait_ge(s_gth, 8 * i + q)
                        dve.tensor_tensor(gTl[:], ps[:, 6, 0:FC * CAP].rearrange("p (f c) -> p f c", f=FC),
                                          gTh[:].bitcast(F32), ALU.subtract).then_inc(s_gtl, 1)
                    turns = kind in "ud" and q % NS == (1 if kind == "u" else 0) and part_ == 0 \
                        and (kind == "u" or q % NS == 0) and not (last and q >= NS)
                    if turns:
                        e = 2 * i + (q // NS + 1)
                        xt_copy(e, 0 if kind == "u" else 1, (q // NS + 1) % 2)
                        if kind == "d" and q == 0 and not last:
                            next_rows(i, 1)
                    if n >= 1 and TILES[n - 1][0] == "u" and TILES[n - 1][2] == 1:
                        qq = TILES[n - 1][1]
                        dve.wait_ge(s_silu, 8 * i + (qq + 1))
                        dve.tensor_tensor(hid[0:CAP], hid[0:CAP], ps[0:CAP, 2 + qq % 2, :], ALU.mult)\
                            .then_inc(s_hid, 1)
                    if n >= 1 and TILES[n - 1] == ("d", NS - 1, 1):
                        y_copy(i, 0)
                        dve.wait_ge(s_yl, 4 * i + 2)
                        selection(i, 1)
                    if n == place["d", 2 * NS - 1, 0]:
                        dve.wait_ge(s_gth, 8 * i + 2 * NS)
                        dve.tensor_tensor(gTl[:], ps[:, 6, 0:FC * CAP].rearrange("p (f c) -> p f c", f=FC),
                                          gTh[:].bitcast(F32), ALU.subtract).then_inc(s_gtl, 1)
                    if not (last and n + AHEAD >= NTI):
                        split(i, n + AHEAD) if n + AHEAD < NTI else split(i + 1, n + AHEAD - NTI)
                y_copy(i, 1)
                banks = (0, 1, 2, 3, 6, 7)
                for u in range(2 * NT):
                    dve.wait_ge(s_scat, 2 * NT * i + (u + 1))
                    x = X[:, u // 2, (u % 2) * 512:(u % 2 + 1) * 512]
                    dve.tensor_tensor(x, x, ps[:, banks[u % len(banks)], :], ALU.add).then_inc(s_acc, 1)

            xt_copy(0, 0, 0)
            xt_copy(0, 1, 0)
            for n in range(AHEAD):
                split(0, n)
            steps = 4
            n0 = ch.n
            with dve.Fori(0, NPAIR - 1) as i:
                ch.base = i * steps
                pair(i, False)
            assert ch.n - n0 == steps
            ch.n, ch.base = n0 + (NPAIR - 1) * steps, 0
            pair(NPAIR - 1, True)


_INPUTS = ("x_prompt", "x_sample", "norm1_g", "w_in", "gla_wg_f", "gla_bg_f", "gla_wg_b", "gla_bg_b",
           "gla_norm_g", "qk_norm_q", "qk_norm_k", "lambda_q1", "lambda_k1", "lambda_q2", "lambda_k2",
           "diff_norm_g", "w_out", "norm2_g", "w_router", "w_gate", "w_up", "w_down")


def shape_constants():
    f = np.float32
    inv = np.power(f(10000.0), -np.arange(0, DK, 2, dtype=f) / f(DK)).astype(f)
    ang = np.arange(T_SAMPLE, dtype=f)[:, None] * inv[None, :]
    cos, sin = np.cos(ang).astype(f), np.sin(ang).astype(f)
    A = np.concatenate([cos, cos], 1).reshape(4, P, DK).transpose(1, 0, 2)
    B = np.concatenate([-sin, sin], 1).reshape(4, P, DK).transpose(1, 0, 2)
    sc = f(DK ** -0.5)
    rot = np.stack([A * sc, B * sc, A, B], 1).reshape(P, -1)
    scan = np.ones((P, TOK), f)
    scan[:DK, ::CHUNK] = 0
    scan[DK:, CHUNK - 1::CHUNK] = 0
    key, qry = np.arange(P)[:, None], np.arange(P)[None, :]
    same = (key // CHUNK) == (qry // CHUNK)
    mask = np.concatenate([same & (qry >= key), same & (qry < key)], 1).astype(np.uint32)
    return {"ident": np.eye(P, dtype=f), "rot": np.ascontiguousarray(rot), "scan_mask": scan,
            "pair_mask": mask, "iota": np.broadcast_to(np.arange(TOK, dtype=f), (P, TOK)).copy()}


def kernel(**inputs):
    import concourse.bacc as bacc
    from concourse.bass_utils import run_bass_kernel_spmd

    nc = bacc.Bacc("TRN2", target_bir_lowering=False, num_devices=1)
    arrays, aps = {}, {}
    data = {n: np.ascontiguousarray(inputs[n]) for n in _INPUTS}
    data.update(shape_constants())
    for name, x in data.items():
        arrays[f"in_{name}"] = x
        aps[name] = nc.dram_tensor(f"in_{name}", x.shape, mybir.dt.from_np(x.dtype), kind="ExternalInput").ap()
    y_prompt = nc.dram_tensor("y_prompt", (1, T_PROMPT, D), F32, kind="ExternalOutput").ap()
    y_sample = nc.dram_tensor("y_sample", (1, T_SAMPLE, D), F32, kind="ExternalOutput").ap()
    h2 = nc.dram_tensor("h2_rows", (TOK, D), F32, kind="Internal").ap()
    build(nc, aps, y_prompt, y_sample, h2)
    r = run_bass_kernel_spmd(nc, [arrays], core_ids=[0])
    return r.results[0]["y_prompt"], r.results[0]["y_sample"]
```
